# Optimizing a Trainium2 kernel written in Bass

```python
import jax, jax.numpy as jnp
from jax import lax
import numpy as np

D_MODEL = 1024
BATCH = 1
SEQ = 1024
DEPTH = 2

N_META = 16
CHUNK = 64
META_PAD = CHUNK - N_META
D_MIX = D_MODEL
LRU_WIDTH = D_MIX // 2
LRU_HEADS = 8
LRU_HEAD_DIM = LRU_WIDTH // LRU_HEADS
LRU_C = 8.0
CONV_WIDTH = 4
CONV_LEFT = 2
CONV_RIGHT = CONV_WIDTH - 1 - CONV_LEFT
GLA_WIDTH = D_MIX - LRU_WIDTH
GLA_HEADS = 4
GLA_DV = GLA_WIDTH // GLA_HEADS
GLA_DK = GLA_DV // 2
GLA_RANK = 16
GLA_GATE_NORM = 16.0
D_FF = 4 * D_MODEL
EPS = 1e-6

IN_WIDTHS = [LRU_WIDTH, LRU_WIDTH,
             GLA_HEADS * GLA_DK, GLA_HEADS * GLA_DK,
             GLA_WIDTH, GLA_WIDTH,
             GLA_RANK, GLA_RANK]
D_IN = int(sum(IN_WIDTHS))
IN_SPLITS = [int(s) for s in np.cumsum(IN_WIDTHS)[:-1]]

kernel_name = "bidir_hymba_rglru_gla_block"

def rmsnorm(x, g):
    xf = x.astype(jnp.float32)
    y = xf * lax.rsqrt(jnp.mean(xf * xf, axis=-1, keepdims=True) + EPS)
    return y.astype(x.dtype) * g

def centred_dwconv(x, w, b):
    y = lax.conv_general_dilated(x, w[:, None, :], window_strides=(1,),
                                 padding=[(CONV_LEFT, CONV_RIGHT)],
                                 dimension_numbers=('NWC', 'WIO', 'NWC'),
                                 feature_group_count=x.shape[-1])
    return y + b

def _lin_combine(c1, c2):
    a1, b1 = c1
    a2, b2 = c2
    return a1 * a2, a2 * b1 + b2

def rglru_direction(xc, wa, ba, wx, bx, lam, reverse):
    B, T, _ = xc.shape
    xh = xc.reshape(B, T, LRU_HEADS, LRU_HEAD_DIM)
    r = jax.nn.sigmoid(jnp.einsum('bthi,hij->bthj', xh, wa).reshape(B, T, LRU_WIDTH) + ba)
    i = jax.nn.sigmoid(jnp.einsum('bthi,hij->bthj', xh, wx).reshape(B, T, LRU_WIDTH) + bx)
    log_a = -LRU_C * r * jax.nn.softplus(-lam)
    a = jnp.exp(log_a)
    u = jnp.sqrt(-jnp.expm1(2.0 * log_a)) * (i * xc)
    _, h = lax.associative_scan(_lin_combine, (a, u), axis=1, reverse=reverse)
    return h

def rglru_group(x_br, gate_br, conv_w, conv_b,
                wa_f, ba_f, wx_f, bx_f, lam_f, wa_b, ba_b, wx_b, bx_b, lam_b):
    xc = centred_dwconv(x_br, conv_w, conv_b).astype(jnp.float32)
    h = (rglru_direction(xc, wa_f, ba_f, wx_f, bx_f, lam_f, reverse=False)
         + rglru_direction(xc, wa_b, ba_b, wx_b, bx_b, lam_b, reverse=True))
    return h.astype(x_br.dtype) * jax.nn.gelu(gate_br)

def insert_pad(t):
    z = jnp.zeros((t.shape[0], META_PAD, t.shape[2]), t.dtype)
    return jnp.concatenate([t[:, :N_META], z, t[:, N_META:]], axis=1)

def remove_pad(t):
    return jnp.concatenate([t[:, :N_META], t[:, CHUNK:]], axis=1)

def to_chunks(t, d):
    B, Tp = t.shape[0], t.shape[1]
    return t.reshape(B, Tp // CHUNK, CHUNK, GLA_HEADS, d).transpose(1, 0, 3, 2, 4)

def from_chunks(o):
    N, B = o.shape[0], o.shape[1]
    return o.transpose(1, 0, 3, 2, 4).reshape(B, N * CHUNK, GLA_HEADS * GLA_DV)

def gla_chunk_scan(q, k, v, g, strict):
    B, H = q.shape[1], q.shape[2]
    b = jnp.cumsum(g, axis=3)
    mask = jnp.tril(jnp.ones((CHUNK, CHUNK), dtype=bool), k=-1 if strict else 0)

    def step(S, inp):
        qc, kc, vc, bc = inp
        diff = bc[:, :, :, None, :] - bc[:, :, None, :, :]
        decay = jnp.where(mask[:, :, None], jnp.exp(jnp.minimum(diff, 0.0)), 0.0)
        scores = jnp.einsum('bhtc,bhtsc,bhsc->bhts', qc, decay, kc)
        intra = jnp.einsum('bhts,bhsv->bhtv', scores, vc)
        inter = jnp.einsum('bhtc,bhcv->bhtv', qc * jnp.exp(bc), S)
        b_last = bc[:, :, -1:, :]
        S_new = (jnp.exp(b_last)[:, :, 0, :, None] * S
                 + jnp.einsum('bhsc,bhsv->bhcv', kc * jnp.exp(b_last - bc), vc))
        return S_new, intra + inter

    S0 = jnp.zeros((B, H, GLA_DK, GLA_DV), jnp.float32)
    _, o = lax.scan(step, S0, (q, k, v, b))
    return o

def gla_bidirectional(q, k, v, g_f, g_b):
    qp, kp, vp, gfp, gbp = (insert_pad(t) for t in (q, k, v, g_f, g_b))
    o_f = gla_chunk_scan(to_chunks(qp, GLA_DK), to_chunks(kp, GLA_DK),
                         to_chunks(vp, GLA_DV), to_chunks(gfp, GLA_DK), strict=False)
    flip = lambda t: t[:, ::-1]
    o_b = gla_chunk_scan(to_chunks(flip(qp), GLA_DK), to_chunks(flip(kp), GLA_DK),
                         to_chunks(flip(vp), GLA_DV), to_chunks(flip(gbp), GLA_DK), strict=True)
    o = from_chunks(o_f) + flip(from_chunks(o_b))
    return remove_pad(o)

def gla_group(q, k, v, g_out, zg_f, zg_b, wg_f, bg_f, wg_b, bg_b, head_norm):
    B, T = q.shape[0], q.shape[1]
    in_dtype = q.dtype
    q = q.astype(jnp.float32) * (GLA_DK ** -0.5)
    g_f = jax.nn.log_sigmoid((zg_f @ wg_f + bg_f).astype(jnp.float32)) / GLA_GATE_NORM
    g_b = jax.nn.log_sigmoid((zg_b @ wg_b + bg_b).astype(jnp.float32)) / GLA_GATE_NORM
    o = gla_bidirectional(q, k.astype(jnp.float32), v.astype(jnp.float32), g_f, g_b)
    o = o.reshape(B, T, GLA_HEADS, GLA_DV)
    o = o * lax.rsqrt(jnp.mean(o * o, axis=-1, keepdims=True) + EPS)
    o = o.reshape(B, T, GLA_WIDTH).astype(in_dtype) * head_norm
    return o * jax.nn.silu(g_out)

def hybrid_mixer(h, w_in, conv_w, conv_b,
                 lru_wa_f, lru_ba_f, lru_wx_f, lru_bx_f, lru_lambda_f,
                 lru_wa_b, lru_ba_b, lru_wx_b, lru_bx_b, lru_lambda_b,
                 gla_wg_f, gla_bg_f, gla_wg_b, gla_bg_b, gla_head_norm, w_out):
    z = h @ w_in
    x_br, gate_br, q, k, v, g_out, zg_f, zg_b = jnp.split(z, IN_SPLITS, axis=-1)
    y_lru = rglru_group(x_br, gate_br, conv_w, conv_b,
                        lru_wa_f, lru_ba_f, lru_wx_f, lru_bx_f, lru_lambda_f,
                        lru_wa_b, lru_ba_b, lru_wx_b, lru_bx_b, lru_lambda_b)
    y_gla = gla_group(q, k, v, g_out, zg_f, zg_b,
                      gla_wg_f, gla_bg_f, gla_wg_b, gla_bg_b, gla_head_norm)
    return jnp.concatenate([y_lru, y_gla], axis=-1) @ w_out

def squared_relu_mlp(h, w_up, w_down):
    return jnp.square(jax.nn.relu(h @ w_up)) @ w_down

def setup_inputs(seed: int = 0) -> dict:
    key = jax.random.key(seed)
    ks = iter(jax.random.split(key, 40))
    nrm = lambda shape, scale: jax.random.normal(next(ks), shape, jnp.float32) * scale
    gain = lambda shape: 1.0 + nrm(shape, 0.05)

    def lam(shape):
        u = jax.random.uniform(next(ks), shape, jnp.float32, 0.9, 0.999)
        s = u ** (1.0 / LRU_C)
        return jnp.log(s) - jnp.log1p(-s)

    L = DEPTH
    return {
        "x": nrm((BATCH, SEQ, D_MODEL), 1.0),
        "meta_tokens": nrm((N_META, D_MODEL), 1.0),
        "norm_mix_pre": gain((L, D_MODEL)),
        "norm_mix_post": gain((L, D_MODEL)),
        "norm_mlp_pre": gain((L, D_MODEL)),
        "norm_mlp_post": gain((L, D_MODEL)),
        "w_in": nrm((L, D_MODEL, D_IN), D_MODEL ** -0.5),
        "conv_w": nrm((L, CONV_WIDTH, LRU_WIDTH), CONV_WIDTH ** -0.5),
        "conv_b": nrm((L, LRU_WIDTH), 0.01),
        "lru_wa_f": nrm((L, LRU_HEADS, LRU_HEAD_DIM, LRU_HEAD_DIM), LRU_HEAD_DIM ** -0.5),
        "lru_ba_f": nrm((L, LRU_WIDTH), 0.01),
        "lru_wx_f": nrm((L, LRU_HEADS, LRU_HEAD_DIM, LRU_HEAD_DIM), LRU_HEAD_DIM ** -0.5),
        "lru_bx_f": nrm((L, LRU_WIDTH), 0.01),
        "lru_lambda_f": lam((L, LRU_WIDTH)),
        "lru_wa_b": nrm((L, LRU_HEADS, LRU_HEAD_DIM, LRU_HEAD_DIM), LRU_HEAD_DIM ** -0.5),
        "lru_ba_b": nrm((L, LRU_WIDTH), 0.01),
        "lru_wx_b": nrm((L, LRU_HEADS, LRU_HEAD_DIM, LRU_HEAD_DIM), LRU_HEAD_DIM ** -0.5),
        "lru_bx_b": nrm((L, LRU_WIDTH), 0.01),
        "lru_lambda_b": lam((L, LRU_WIDTH)),
        "gla_wg_f": nrm((L, GLA_RANK, GLA_HEADS * GLA_DK), GLA_RANK ** -0.5),
        "gla_bg_f": nrm((L, GLA_HEADS * GLA_DK), 0.1),
        "gla_wg_b": nrm((L, GLA_RANK, GLA_HEADS * GLA_DK), GLA_RANK ** -0.5),
        "gla_bg_b": nrm((L, GLA_HEADS * GLA_DK), 0.1),
        "gla_head_norm": gain((L, GLA_WIDTH)),
        "w_out": nrm((L, D_MIX, D_MODEL), D_MIX ** -0.5),
        "w_mlp_up": nrm((L, D_MODEL, D_FF), D_MODEL ** -0.5),
        "w_mlp_down": nrm((L, D_FF, D_MODEL), D_FF ** -0.5),
    }

def reference(x, meta_tokens, norm_mix_pre, norm_mix_post, norm_mlp_pre, norm_mlp_post,
              w_in, conv_w, conv_b,
              lru_wa_f, lru_ba_f, lru_wx_f, lru_bx_f, lru_lambda_f,
              lru_wa_b, lru_ba_b, lru_wx_b, lru_bx_b, lru_lambda_b,
              gla_wg_f, gla_bg_f, gla_wg_b, gla_bg_b, gla_head_norm,
              w_out, w_mlp_up, w_mlp_down):
    B = x.shape[0]
    meta = jnp.broadcast_to(meta_tokens.astype(x.dtype)[None], (B, N_META, D_MODEL))
    h = jnp.concatenate([meta, x], axis=1)
    for l in range(DEPTH):
        mix = hybrid_mixer(rmsnorm(h, norm_mix_pre[l]), w_in[l], conv_w[l], conv_b[l],
                           lru_wa_f[l], lru_ba_f[l], lru_wx_f[l], lru_bx_f[l], lru_lambda_f[l],
                           lru_wa_b[l], lru_ba_b[l], lru_wx_b[l], lru_bx_b[l], lru_lambda_b[l],
                           gla_wg_f[l], gla_bg_f[l], gla_wg_b[l], gla_bg_b[l], gla_head_norm[l],
                           w_out[l])
        h = h + rmsnorm(mix, norm_mix_post[l])
        ff = squared_relu_mlp(rmsnorm(h, norm_mlp_pre[l]), w_mlp_up[l], w_mlp_down[l])
        h = h + rmsnorm(ff, norm_mlp_post[l])
    return h[:, N_META:]


_drawn_inputs = setup_inputs


def setup_inputs(seed=0):
    import zlib

    import numpy as np

    out = dict(_drawn_inputs(seed))
    spreads = {}
    factors = {'lru_ba_f': 51.006,
     'lru_bx_f': 34.426,
     'lru_ba_b': 47.313,
     'lru_bx_b': 31.446,
     'gla_bg_f': 3.101,
     'gla_bg_b': 3.131}
    for name, (base, spread) in spreads.items():
        noise = np.random.default_rng([zlib.crc32(name.encode()), seed]).standard_normal(out[name].shape)
        drawn = base * np.exp(spread * noise) if base else spread * noise
        out[name] = __import__('jax').numpy.asarray(drawn.astype(out[name].dtype))
    for name, factor in factors.items():
        out[name] = (out[name] * factor).astype(out[name].dtype)
    return out
```

```python
import concourse.bass as bass
from concourse import mybir
from contextlib import ExitStack

L = 2
D = 1024
N_META, SEQ = 16, 1024
NT = N_META + SEQ
NB, BN = 3, 348
NP = NB * BN
KT = D // 128
LW, LT = 512, 4
DK, DV, HEADS, RANK = 64, 128, 4, 16
C, NC = 104, NT // 104
MID = C // 2 - 1
F_TILES, GROUPS, GT = 32, 8, 4
EPS = 1e-6
GATE_NORM = 16.0
LRU_C = 8.0

U_OUT, U_MLP = 20, 28
UNITS = U_MLP + 8 * GROUPS
PAIRS = UNITS // 2

(P_CONVW, P_CONVB, P_BAF, P_BXF, P_BAB, P_BXB, P_LAM, P_BG, P_GMIX, P_GMIXPOST, P_GMLP, P_GMLPPOST,
 P_GOUT, P_ONE, P_SP, P_NSP, NPAR) = (0, 16, 20, 24, 28, 32, 36, 44, 48, 56, 64, 72, 80, 88, 96, 104, 112)
N_LOADED = P_SP

J_STAT = 0


def j_x(t): return 6 * t + 1
def j_gate(t): return 6 * t + 2
def j_lru(t, n): return 6 * t + 3 + n


J_ZG, J_Q0, J_W, J_Q1, J_K, J_SG, J_V, J_O, J_POST, J_STAT2, J_MLP = 25, 26, 27, 31, 32, 34, 38, 42, 50, 51, 52
J_POST2 = J_MLP + 12 * GROUPS
NJ = J_POST2 + 1
SET_JOBS = ((NJ + 1) // 2, NJ // 2)


def j_up(g, i): return J_MLP + 12 * g + i
def j_down(g, m): return J_MLP + 12 * g + GT + m


FIRST = 1

X_PER = 4 + NC + 8 + 8


def trunk_kernel(nc, x_in, w_units, w_zg, w_gates, w_decay, params, h_out):
    f32, f32r, bf16, u8 = mybir.dt.float32, mybir.dt.float32r, mybir.dt.bfloat16, mybir.dt.uint8
    ALU, ACT = mybir.AluOpType, mybir.ActivationFunctionType
    h_mid = nc.dram_tensor("h_mid", (L, KT, 128, NP), f32, kind="Internal").ap()

    ctx = ExitStack()
    with ctx:
        def sb(name, shape, dt=f32):
            return ctx.enter_context(nc.sbuf_tensor(name, shape, dt))

        def sem(name):
            return ctx.enter_context(nc.semaphore(name))

        X = sb("X", [128, KT, 2, NP], f32r)
        w_raw = sb("w_raw", [128, 2, 8, 128])
        w_hl = sb("w_hl", [128, 2, 2, 8, 128], f32r)
        par = sb("par", [128, L, NPAR])
        ones = sb("ones", [128, 128])
        ident = sb("ident", [128, 128])
        gates_w = sb("gates_w", [128, 4, 128])
        decay_w = sb("decay_w", [2 * RANK, 512])
        zg_raw = sb("zg_raw", [128, 8, 2 * RANK])
        zg_hl = sb("zg_hl", [128, 2, 8, 2 * RANK], f32r)
        reset = sb("reset", [128, NT + 1], bf16)
        later = sb("later", [C, HEADS, C], u8)
        eps = sb("eps", [128, 1])
        b_mid = sb("b_mid", [128, 4, NC])
        b_tot = sb("b_tot", [128, 4, NC])
        fac = sb("fac", [128, 4, NC])
        TB = NP * 4
        base = (nc.sbuf_base + 31) // 32 * 32

        def at(name, shape, tile, dt=f32, extra=0):
            return nc.alloc_sbuf_tensor_at(name, shape, dt, offset=base + tile * TB + extra, align_bytes=16)

        A_RS, A_ACC, A_T, A_YL, A_T3, A_SG, A_D, A_QK = 0, 1, 2, 5, 9, 10, 14, 18
        rs = at("rs", [128, NP], A_RS)
        acc = at("acc", [128, NP], A_ACC)
        T = [at("T0", [128, NP], A_T), at("T1", [128, NP], A_T + 1), at("T2", [128, NP], A_T + 2), at("T3", [128, NP], A_T3)]
        y_lru = at("y_lru", [128, LT, NP], A_YL)
        lr = at("lr", [128, 2, NP], A_SG)
        li = at("li", [128, 2, NP], A_SG + 2)
        la = at("la", [128, 2, NP], A_D)
        lt_ = at("lt", [128, 2, NP], A_D + 2)
        xc = at("xc", [128, NP], A_QK)
        gg = at("gg", [128, LT, NP], A_QK + 1)
        xb = at("xb", [128, NP + 4], A_QK + 5)
        hh = [T[0], at("hh1", [128, NP], A_QK + 7)]
        dd = at("dd", [128, 4, NP], A_D)
        vT = at("vT", [128, HEADS, NP], A_D)
        qi = at("qi", [128, 4, NP], A_QK)
        ki = at("ki", [128, 4, NP], A_QK + 4)
        sg = at("sg", [128, HEADS, NP], A_SG)
        ee = at("ee", [128, 2, NP], A_SG)
        v_tok = at("v_tok", [128, NC, HEADS * DV], A_YL)
        st_b = at("st_b", [128, NC, 2, DV], A_T)
        kt_b = at("kt_b", [128, 2, 2, 128], A_RS)
        kv_b = at("kv_b", [128, 2, DV], A_RS, extra=2048)
        p_t = at("p_t", [128, 2, 2, 2 * C], A_ACC)
        kt_f = at("kt_f", [128, 2, 2, 128], A_D)
        st_f = at("st_f", [128, 2, 2, DV], A_D, extra=2048)
        kv_f = at("kv_f", [128, 2, DV], A_D, extra=4096)
        o_sq = at("o_sq", [128, 2, HEADS * C], A_D, extra=5120)
        o_rs = at("o_rs", [128, 2, HEADS * C], A_D, extra=5120 + 3328)
        o_y = at("o_y", [128, 2, HEADS * C], A_D, extra=5120 + 6656)
        h_old = at("h_old", [128, 4, NP], A_D)
        Y = at("Y", [128, KT, NP], A_QK)
        act_hi = at("act_hi", [128, GT, NP], A_YL, f32r)
        act_lo = at("act_lo", [128, GT, NP], A_SG, f32r)
        assert 5120 + 3 * 3328 <= 4 * TB and 4 * NC * HEADS * DV <= 5 * TB and 4 * NC * 2 * DV <= 3 * TB

        banks = ctx.enter_context(nc.psum_tensor("banks", [128, 8, 512], f32))

        def ps(j, rows=128):
            s = (j % 2) * NB
            return banks[0:rows, s:s + NB, 0:BN]

        def blk(ap):
            return ap.rearrange("p (b n) -> p b n", b=NB)

        w_loaded = [sem(f"w_loaded{i}") for i in range(2)]
        w_scaled = sem("w_scaled")
        w_ready = sem("w_ready")
        zgw_loaded, zgw_step, zgw_ready = sem("zgw_loaded"), sem("zgw_step"), sem("zgw_ready")
        gatew_loaded = sem("gatew_loaded")
        decayw_loaded = sem("decayw_loaded")
        par_loaded, par_step, par_ready = sem("par_loaded"), sem("par_step"), sem("par_ready")
        const_step, const_ready = sem("const_step"), sem("const_ready")
        x_loaded = [sem(f"x_loaded{m}") for m in range(KT)]
        mm_done = sem("mm_done")
        ps_free = [sem("ps_free_a"), sem("ps_free_b")]
        x_hi, x_lo = sem("x_hi"), sem("x_lo")
        sq_h, sq_read = sem("sq_h"), sem("sq_read")
        rs_log, rs_ready = sem("rs_log"), sem("rs_ready")
        pad_zeroed, conv_step, xc_ready = sem("pad_zeroed"), sem("conv_step"), sem("xc_ready")
        lru_tanh, lru_a, lru_a2 = sem("lru_tanh"), sem("lru_a"), sem("lru_a2")
        lru_ix, lru_v, lru_root, lru_u, lru_h = (sem(n) for n in ("lru_ix", "lru_v", "lru_root", "lru_u", "lru_h"))
        gelu_done, lru_sum, ylru_done = sem("gelu_done"), sem("lru_sum"), sem("ylru_done")
        softplus_step = sem("softplus_step")
        decay_step, d_ready = sem("decay_step"), sem("d_ready")
        fac_step, fac_in, fac_ready = sem("fac_step"), sem("fac_in"), sem("fac_ready")
        e_ready, qk_made = sem("e_ready"), sem("qk_made")
        silu_done = sem("silu_done")
        g_vt, g_ktb, g_kvb = sem("g_vt"), sem("g_ktb"), sem("g_kvb")
        vtok_ready, ktb_ready, stb_sum, stb_ready = sem("vtok_ready"), sem("ktb_ready"), sem("stb_sum"), sem("stb_ready")
        g_ktf, g_kvf, g_s, g_o, g_ss = (sem(n) for n in ("g_ktf", "g_kvf", "g_s", "g_o", "g_ss"))
        ktf_ready, p_fwd, p_ready = sem("ktf_ready"), sem("p_fwd"), sem("p_ready")
        stf_sum, stf_ready = sem("stf_sum"), sem("stf_ready")
        osq_ready, o_gated, ss_log, ors_ready, oy_ready = (sem(n) for n in ("osq_ready", "o_gated", "ss_log", "ors_ready", "oy_ready"))
        sq_y, acc_done = sem("sq_y"), sem("acc_done")
        hold_loaded = [sem(f"hold_loaded{i}") for i in range(4)]
        y_scaled, y_new = sem("y_scaled"), sem("y_new")
        h_stored = sem("h_stored")
        act_sq, a_hi, a_lo = sem("act_sq"), sem("a_hi"), sem("a_lo")

        waited_pool, waited_dve = sem("waited_pool"), sem("waited_dve")

        def heads(ap):
            return ap.rearrange("p (r j c) -> p r j c", r=2, j=2)

        def by_parity(ap):
            return ap.rearrange("p (j r) c -> p r j c", r=2)

        def done(l, j):
            return l * NJ + j + 1

        def freed(l, j):
            return l * SET_JOBS[j % 2] + j // 2 + 1

        block = ctx.enter_context(nc.Block())

        @block.sync
        def _(sp):
            sp.sem_inc(w_ready, 2)
            for s in (mm_done, *ps_free, ylru_done, lru_h, a_lo):
                sp.sem_inc(s, FIRST)
            sp.dma_start(par[:, :, 0:N_LOADED], params).then_inc(par_loaded, 16)
            for m in range(KT):
                sp.dma_start(Y[:, m, :], x_in[m]).then_inc(x_loaded[m], 16)

            def pair(l, i):
                for s in range(2):
                    sp.wait_ge(w_ready, (l * PAIRS + i) * 2 + s + 1)
                    sp.dma_start(w_raw[:, s], w_units[l, i * 2 + s]).then_inc(w_loaded[s], 16)

            with sp.Fori(0, L) as l:
                sp.wait_ge(mm_done, FIRST + l * NJ)
                sp.dma_start(zg_raw[:, :, :], w_zg[l]).then_inc(zgw_loaded, 16)
                sp.dma_start(decay_w[:, :], w_decay[l]).then_inc(decayw_loaded, 16)
                with sp.Fori(0, LT) as t:
                    pair(l, t)
                    sp.wait_ge(mm_done, FIRST + l * NJ + j_lru(t, 3) + 1 - 6)
                    sp.dma_start(gates_w[:, :, :], w_gates[l, t]).then_inc(gatew_loaded, 16)
                with sp.Fori(LT, PAIRS) as i:
                    pair(l, i)

        @block.gpsimd
        def _(pool):
            nc.gpsimd.memset(ones[:, :], 1.0).then_inc(const_step, 1)
            nc.gpsimd.memset(ident[:, :], 0.0).then_inc(const_step, 1)
            nc.gpsimd.memset(reset[:, :], 1.0).then_inc(const_step, 1)
            nc.gpsimd.memset(eps[:, :], EPS).then_inc(const_step, 1)
            pool.wait_ge(const_step, 4)
            nc.gpsimd.memset(reset[:, 0:NT + 1:C], 0.0).then_inc(const_step, 1)
            nc.gpsimd.affine_select(out=ident[:, :], in_=ident[:, :], compare_op=ALU.not_equal, fill=1.0,
                                    base=0, pattern=[[-1, 128]], channel_multiplier=1).then_inc(const_step, 1)
            nc.gpsimd.memset(T[0][0:C, 0:C], 1.0).then_inc(const_step, 1)
            pool.wait_ge(const_step, 7)
            nc.gpsimd.affine_select(out=T[0][0:C, 0:C], in_=T[0][0:C, 0:C], compare_op=ALU.is_gt, fill=0.0,
                                    base=0, pattern=[[-1, C]], channel_multiplier=1).then_inc(const_step, 1)
            pool.wait_ge(const_step, 8)
            nc.gpsimd.tensor_copy(later[:, :, :], T[0][0:C, 0:C].unsqueeze(1).to_broadcast([C, HEADS, C]))\
                .then_inc(const_ready, 1)

            pool.wait_ge(par_loaded, 16)

            def split_pair(l, i, gain, before0, before1):
                for s, before in ((0, before0), (1, before1)):
                    gains = par[:, l, gain:gain + 8].unsqueeze(2).to_broadcast([128, 8, 128])
                    unit = (l * PAIRS + i) * 2 + s
                    pool.wait_ge(w_loaded[s], 16 * (l * PAIRS + i + 1))
                    pool.wait_ge(mm_done, FIRST + before)
                    pool.sem_inc(waited_pool, 1)
                    nc.gpsimd.tensor_tensor(w_hl[:, s, 0], w_raw[:, s], gains, ALU.mult).then_inc(w_scaled, 1)
                    pool.wait_ge(w_scaled, 2 * unit + 1)
                    pool.sem_inc(waited_pool, 1)
                    nc.gpsimd.tensor_tensor(w_raw[:, s], w_raw[:, s], gains, ALU.mult).then_inc(w_scaled, 1)
                    pool.wait_ge(w_scaled, 2 * unit + 2)
                    nc.gpsimd.tensor_tensor(w_hl[:, s, 1], w_raw[:, s], w_hl[:, s, 0].bitcast(f32), ALU.subtract)\
                        .then_inc(w_ready, 1)

            def group(l, g, before0, before1):
                i0 = U_MLP // 2 + 4 * g
                split_pair(l, i0, P_GMLP, before0, before1)
                split_pair(l, i0 + 1, P_GMLP, done(l, j_up(g, 0)), done(l, j_up(g, 1)))
                split_pair(l, i0 + 2, P_ONE, done(l, j_up(g, 2)), done(l, j_up(g, 3)))
                split_pair(l, i0 + 3, P_ONE, done(l, j_down(g, 1)), done(l, j_down(g, 3)))

            with pool.Fori(0, L) as l:
                split_pair(l, 0, P_GMIX, l * NJ, l * NJ)
                gains = par[:, l, P_GMIX:P_GMIX + 8].unsqueeze(2).to_broadcast([128, 8, 2 * RANK])
                pool.wait_ge(zgw_loaded, 16 * (l + 1))
                pool.sem_inc(waited_pool, 1)
                nc.gpsimd.tensor_tensor(zg_hl[:, 0], zg_raw[:, :, :], gains, ALU.mult).then_inc(zgw_step, 1)
                pool.wait_ge(zgw_step, 2 * l + 1)
                pool.sem_inc(waited_pool, 1)
                nc.gpsimd.tensor_tensor(zg_raw[:, :, :], zg_raw[:, :, :], gains, ALU.mult).then_inc(zgw_step, 1)
                pool.wait_ge(zgw_step, 2 * l + 2)
                nc.gpsimd.tensor_tensor(zg_hl[:, 1], zg_raw[:, :, :], zg_hl[:, 0].bitcast(f32), ALU.subtract)\
                    .then_inc(zgw_ready, 1)
                with pool.Fori(1, LT) as t:
                    split_pair(l, t, P_GMIX, done(l, j_x(t - 1)), done(l, j_gate(t - 1)))
                split_pair(l, 4, P_GMIX, done(l, j_x(3)), done(l, j_gate(3)))
                split_pair(l, 5, P_GMIX, done(l, J_Q0), done(l, J_Q1))
                with pool.Fori(0, 4) as i:
                    split_pair(l, 6 + i, P_GMIX, done(l, J_K + 2 * i), done(l, J_K + 2 * i + 1))
                with pool.Fori(0, 4) as i:
                    split_pair(l, U_OUT // 2 + i, P_GOUT, done(l, J_O - 2 + 2 * i), done(l, J_O - 1 + 2 * i))
                group(l, 0, done(l, J_O + 6), done(l, J_O + 7))
                with pool.Fori(1, GROUPS) as g:
                    group(l, g, done(l, j_down(g - 1, 5)), done(l, j_down(g - 1, 7)))

        @block.tensor
        def _(pe):
            def product(out, w, xs, first, last):
                for n, (wp, xp) in enumerate(((w[0], xs[0]), (w[0], xs[1]), (w[1], xs[0]))):
                    for b in range(NB):
                        ins = nc.tensor.matmul(out[:, b, :], wp, blk(xp)[:, b, :],
                                               start=first and n == 0, stop=last and n == 2)
                return ins

            def wslot(s, k):
                return w_hl[:, s, 0, k, :], w_hl[:, s, 1, k, :]

            def xtile(k):
                return X[:, k, 0, :], X[:, k, 1, :]

            def take_set(l, j):
                pe.wait_ge(ps_free[j % 2], FIRST + l * SET_JOBS[j % 2] + j // 2)

            def unit_job(l, unit, s, jp, jx):
                pe.wait_ge(w_ready, l * UNITS + unit + 3)
                pe.wait_ge(ps_free[jp % 2], FIRST + l * SET_JOBS[jp % 2] + jx)
                for k in range(KT):
                    ins = product(ps(jp), wslot(s, k), xtile(k), k == 0, k == KT - 1)
                ins.then_inc(mm_done, 1)

            def stat_and_first(l, j, unit, xbase, sbase, rbase):
                take_set(l, j)
                for k in range(KT):
                    pe.wait_ge(sq_h, sbase + k + 1)
                    for b in range(NB):
                        ins = nc.tensor.matmul(ps(j)[:, b, :], ones[:, :], blk(T[2 + k % 2][:, :])[:, b, :],
                                               start=k == 0, stop=k == KT - 1)
                    ins.then_inc(sq_read if k < KT - 1 else mm_done, 1)
                    if k == 0:
                        pe.wait_ge(w_ready, l * UNITS + unit + 3)
                        take_set(l, j + 1)
                    pe.wait_ge(x_hi, xbase + k + 1)
                    pe.wait_ge(x_lo, xbase + k + 1)
                    ins = product(ps(j + 1), wslot(0, k), xtile(k), k == 0, k == KT - 1)
                ins.then_inc(mm_done, 1)

            def lru_gates(l, t):
                pe.wait_ge(gatew_loaded, 16 * (l * LT + t + 1))
                pe.wait_ge(xc_ready, l * LT + t + 1)
                for n in range(4):
                    jp = 3 + n
                    pe.wait_ge(ps_free[jp % 2], FIRST + l * SET_JOBS[jp % 2] + 3 * t + jp // 2)
                    for b in range(NB):
                        ins = nc.tensor.matmul(ps(jp)[:, b, :], gates_w[:, n, :], blk(xc[:, :])[:, b, :],
                                               start=True, stop=True)
                    ins.then_inc(mm_done, 1)

            def row_sum(l, j, values_ready, n):
                take_set(l, j)
                pe.wait_ge(values_ready, n)
                for b in range(NB):
                    ins = nc.tensor.matmul(ps(j)[:, b, :], ones[:, :], blk(acc[:, :])[:, b, :], start=True, stop=True)
                ins.then_inc(mm_done, 1)

            def down_unit(l, g, i, j0, jx):
                s = i % 2
                pe.wait_ge(w_ready, l * UNITS + U_MLP + 8 * g + 4 + i + 3)
                for m, ks in ((0, (0, 1, 2)), (1, (0, 1, 2)), (0, (3,)), (1, (3,))):
                    jp = j0 + 2 * i + m
                    if ks[0] == 0:
                        pe.wait_ge(ps_free[jp % 2], FIRST + l * SET_JOBS[jp % 2] + jx + i)
                    for k in ks:
                        if i == 0 and m == 0:
                            pe.wait_ge(a_hi, l * F_TILES + GT * g + k + 1)
                            pe.wait_ge(a_lo, FIRST + l * F_TILES + GT * g + k + 1)
                        ins = product(ps(jp), wslot(s, m * 4 + k), (act_hi[:, k, :], act_lo[:, k, :]),
                                      k == 0, k == GT - 1)
                    if ks[0] == 3:
                        ins.then_inc(mm_done, 1)

            def gla(l, xbase):
                def chunk(c):
                    return slice(c * C, (c + 1) * C)

                def key_transposes(c, d, bank, signal):
                    for j in range(2):
                        ins = nc.tensor.transpose(banks[0:C, bank, j * 128:(j + 1) * 128],
                                                  ki[:, 2 * d + j, chunk(c)], ident[:, :])
                    ins.then_inc(signal, 1)

                def key_values(c, kt, bank, signal):
                    for h in range(HEADS):
                        j, r = h // 2, 64 * (h % 2)
                        ins = nc.tensor.matmul(banks[r:r + DK, bank, j * DV:(j + 1) * DV], kt[0:C, j, r:r + DK],
                                               v_tok[0:C, c, h * DV:(h + 1) * DV], start=True, stop=True)
                    ins.then_inc(signal, 1)

                pe.wait_ge(ps_free[0], FIRST + freed(l, J_V + 2))
                pe.wait_ge(ps_free[1], FIRST + freed(l, J_V + 3))

                def to_rows(n):
                    c = NC - 1 - n
                    if n >= 2:
                        pe.wait_ge(vtok_ready, l * NC + n - 1)
                    for h in range(HEADS):
                        ins = nc.tensor.transpose(banks[0:C, n % 2, h * DV:(h + 1) * DV], vT[:, h, chunk(c)], ident[:, :])
                    ins.then_inc(g_vt, 1)
                    if n < NC - 1:
                        if n >= 2:
                            pe.wait_ge(ktb_ready, l * (NC - 1) + n - 1)
                        key_transposes(c, 1, 2 + n % 2, g_ktb)

                to_rows(0)
                for n in range(NC):
                    if n + 1 < NC:
                        to_rows(n + 1)
                    if n < NC - 1:
                        pe.wait_ge(vtok_ready, l * NC + n + 1)
                        pe.wait_ge(ktb_ready, l * (NC - 1) + n + 1)
                        if n >= 2:
                            pe.wait_ge(stb_sum, l * (NC - 1) + n - 1)
                        key_values(NC - 1 - n, kt_b[:, n % 2], 4 + n % 2, g_kvb)
                pe.wait_ge(vtok_ready, (l + 1) * NC)
                pe.wait_ge(ktb_ready, (l + 1) * (NC - 1))
                pe.wait_ge(stb_ready, (l + 1) * (NC - 1))

                def keys_in_rows(c):
                    if c >= 1:
                        pe.wait_ge(ktf_ready, l * (NC - 1) + c)
                    key_transposes(c, 0, 0, g_ktf)

                def scores(c):
                    if c >= 1:
                        pe.wait_ge(p_ready, l * NC + c)
                    for d in range(2):
                        for j in range(2):
                            for r in range(2):
                                rows = slice(64 * r, 64 * r + DK)
                                ins = nc.tensor.matmul(banks[0:C, 2 + r, (2 * d + j) * C:(2 * d + j + 1) * C],
                                                       ki[rows, 2 * d + j, chunk(c)], qi[rows, 2 * d + j, chunk(c)],
                                                       start=True, stop=True)
                    ins.then_inc(g_s, 1)

                def squares(c):
                    pe.wait_ge(osq_ready, l * NC + c + 1)
                    if c >= 1:
                        pe.wait_ge(ss_log, l * NC + c)
                    nc.tensor.matmul(banks[:, 6, 0:HEADS * C], ones[:, :], o_sq[:, c % 2, :], start=True, stop=True)\
                        .then_inc(g_ss, 1)

                keys_in_rows(0)
                scores(0)
                for c in range(NC):
                    if c + 1 < NC - 1:
                        keys_in_rows(c + 1)
                    if c < NC - 1:
                        pe.wait_ge(ktf_ready, l * (NC - 1) + c + 1)
                        if c >= 1:
                            pe.wait_ge(stf_sum, l * (NC - 1) + c)
                        key_values(c, kt_f[:, c % 2], 1, g_kvf)
                    if c + 1 < NC:
                        scores(c + 1)
                    pe.wait_ge(p_ready, l * NC + c + 1)
                    if c >= 1:
                        pe.wait_ge(stf_ready, l * (NC - 1) + c)
                        pe.wait_ge(o_gated, l * NC + c)
                    for j in range(2):
                        for r in range(2):
                            h, rows = 2 * j + r, slice(64 * r, 64 * r + DK)
                            terms = [(v_tok[0:C, c, h * DV:(h + 1) * DV], p_t[0:C, c % 2, r, j * C:(j + 1) * C])]
                            if c > 0:
                                terms.append((st_f[rows, c % 2, j, :], qi[rows, j, chunk(c)]))
                            if c < NC - 1:
                                terms.append((st_b[rows, c, j, :], qi[rows, 2 + j, chunk(c)]))
                            for n, (a, b) in enumerate(terms):
                                ins = nc.tensor.matmul(banks[:, 4 + r, j * C:(j + 1) * C], a, b,
                                                       start=n == 0, stop=n == len(terms) - 1)
                    ins.then_inc(g_o, 1)
                    if c >= 1:
                        squares(c - 1)

                def half(s, ks):
                    for k in ks:
                        ins = product(ps(J_O + s), wslot(s, k), xtile(k), k == 0, k == KT - 1)
                    return ins

                for s in range(2):
                    pe.wait_ge(w_ready, l * UNITS + U_OUT + s + 3)
                    take_set(l, J_O + s)
                    if s == 0:
                        pe.wait_ge(x_lo, xbase + KT + LT)
                    else:
                        squares(NC - 1)
                        pe.wait_ge(o_gated, (l + 1) * NC)
                    half(s, range(LT))
                pe.wait_ge(x_hi, xbase + KT + LT + NC)
                pe.wait_ge(x_lo, xbase + KT + LT + NC)
                for s in range(2):
                    half(s, range(LT, KT)).then_inc(mm_done, 1)

            pe.wait_ge(const_ready, 1)
            with pe.Fori(0, L) as l:
                xbase = l * X_PER
                stat_and_first(l, J_STAT, 0, xbase, l * 16, l * 14)
                unit_job(l, 1, 1, 2, 1)
                lru_gates(l, 0)
                with pe.Fori(1, LT) as t:
                    unit_job(l, 2 * t, 0, 1, 3 * t)
                    unit_job(l, 2 * t + 1, 1, 2, 3 * t + 1)
                    lru_gates(l, t)
                pe.wait_ge(zgw_ready, l + 1)
                take_set(l, J_ZG)
                for k in range(KT):
                    ins = product(ps(J_ZG, 2 * RANK), (zg_hl[:, 0, k, :], zg_hl[:, 1, k, :]), xtile(k), k == 0, k == KT - 1)
                ins.then_inc(mm_done, 1)
                unit_job(l, 8, 0, J_Q0, J_Q0 // 2)
                pe.wait_ge(decayw_loaded, 16 * (l + 1))
                pe.wait_ge(ps_free[J_ZG % 2], FIRST + freed(l, J_ZG))
                for n in range(4):
                    take_set(l, J_W + n)
                    for b in range(NB):
                        ins = nc.tensor.matmul(ps(J_W + n)[:, b, :], decay_w[:, n * 128:(n + 1) * 128],
                                               blk(acc[0:2 * RANK, :])[:, b, :], start=True, stop=True)
                    ins.then_inc(mm_done, 1)
                unit_job(l, 9, 1, J_Q1, J_Q1 // 2)
                with pe.Fori(0, 5) as i:
                    unit_job(l, 10 + 2 * i, 0, J_K, J_K // 2 + i)
                    unit_job(l, 11 + 2 * i, 1, J_K + 1, J_K // 2 + i)
                gla(l, xbase)
                with pe.Fori(1, 4) as i:
                    unit_job(l, U_OUT + 2 * i, 0, J_O, J_O // 2 + i)
                    unit_job(l, U_OUT + 2 * i + 1, 1, J_O + 1, J_O // 2 + i)
                row_sum(l, J_POST, acc_done, l * 14 + 7)
                stat_and_first(l, J_STAT2, U_MLP, xbase + KT + LT + NC, l * 16 + 8, l * 14 + 7)
                for i in range(1, GT):
                    unit_job(l, U_MLP + i, i % 2, J_MLP + i, (J_MLP + i) // 2)
                for i in range(4):
                    down_unit(l, 0, i, J_MLP + GT, (J_MLP + GT) // 2)
                with pe.Fori(1, GROUPS) as g:
                    for i in range(GT):
                        unit_job(l, U_MLP + 8 * g + i, i % 2, J_MLP + i, (J_MLP + i) // 2 + 6 * g)
                    for i in range(4):
                        down_unit(l, g, i, J_MLP + GT, (J_MLP + GT) // 2 + 6 * g)
                row_sum(l, J_POST2, acc_done, l * 14 + 14)
            for k in range(KT - 1):
                pe.wait_ge(sq_h, L * 16 + k + 1)
                pe.sem_inc(sq_read, 1)

        @block.scalar
        def _(act):
            def inv_rms(l, j, n):
                act.wait_ge(mm_done, FIRST + done(l, j))
                nc.scalar.activation(blk(rs[:, :]), ps(j), ACT.Ln, scale=1.0 / D, bias=eps[:, 0:1]).then_inc(ps_free[j % 2], 1)
                act.wait_ge(ps_free[j % 2], FIRST + freed(l, j))
                nc.scalar.activation(rs[:, :], rs[:, :], ACT.Exp, scale=-0.5).then_inc(rs_ready, 1)

            def split_hi_and_square(m, squares):
                nc.scalar.activation(X[:, m, 0, :], Y[:, m, :], ACT.Copy).then_inc(x_hi, 1)
                if m >= 2:
                    act.wait_ge(sq_read, squares + m - 1)
                nc.scalar.activation(T[2 + m % 2][:, :], Y[:, m, :], ACT.Square).then_inc(sq_h, 1)

            def load_old(m, source):
                act.dma_start(h_old[:, m % 4, :], source[m]).then_inc(hold_loaded[m % 4], 16)

            def square_out(l, m, j, jx, phase):
                act.wait_ge(ps_free[j % 2], FIRST + l * SET_JOBS[j % 2] + jx + 1)
                if m >= 3:
                    act.wait_ge(acc_done, l * 14 + phase * 7 + m - 2)
                out = acc if m == 0 else T[2 + m % 2]
                nc.scalar.activation(out[:, :], Y[:, m, :], ACT.Square).then_inc(sq_y, 1)

            def update(l, phase, source, target):
                for m in range(KT):
                    act.wait_ge(y_new, l * 16 + phase * 8 + m + 1)
                    if m + 4 < KT:
                        load_old(m + 4, source)
                    split_hi_and_square(m, l * 14 + phase * 7 + 7)
                    act.dma_start(target[m], Y[:, m, :]).then_inc(h_stored, 16)

            act.wait_ge(const_ready, 1)
            act.wait_ge(par_loaded, 16)
            nc.scalar.activation(par[:, :, P_SP:P_SP + 8], par[:, :, P_LAM:P_LAM + 8], ACT.Abs).then_inc(par_step, 1)
            act.wait_ge(par_step, 1)
            nc.scalar.activation(par[:, :, P_SP:P_SP + 8], par[:, :, P_SP:P_SP + 8], ACT.Exp, scale=-1.0).then_inc(par_step, 1)
            for m in range(KT):
                act.wait_ge(x_loaded[m], 16)
                act.dma_start(h_out[0, m], Y[:, m, :]).then_inc(h_stored, 16)
                split_hi_and_square(m, 0)
            act.wait_ge(par_ready, 1)
            with act.Fori(0, L) as l:
                xbase = l * X_PER + KT
                inv_rms(l, J_STAT, 0)
                with act.Fori(0, LT) as t:
                    for n, (out, bias) in enumerate(((lr[:, 0], P_BAF), (li[:, 0], P_BXF), (lr[:, 1], P_BAB), (li[:, 1], P_BXB))):
                        jp = 3 + n
                        act.wait_ge(mm_done, FIRST + l * NJ + 6 * t + jp + 1)
                        if n == 1:
                            act.wait_ge(lru_h, FIRST + (l * LT + t) * 2)
                        nc.scalar.activation(blk(out), ps(jp), ACT.Sigmoid, bias=par[:, l, bass.ds(bias + t, 1)])\
                            .then_inc(ps_free[jp % 2], 1)
                    for d in range(2):
                        act.wait_ge(ps_free[1], FIRST + l * SET_JOBS[1] + 3 * t + d + 2)
                        nc.scalar.activation(lt_[:, d, 0:NT], lr[:, d, 0:NT], ACT.Tanh,
                                             scale=par[:, l, bass.ds(P_SP + 4 * d + t, 1)]).then_inc(lru_tanh, 1)
                    for d in range(2):
                        nc.scalar.activation(la[:, d, 0:NT], lr[:, d, 0:NT], ACT.Exp,
                                             scale=par[:, l, bass.ds(P_NSP + 4 * d + t, 1)]).then_inc(lru_a, 1)
                    for d in range(2):
                        act.wait_ge(lru_a, (l * LT + t) * 2 + d + 1)
                        nc.scalar.activation(lr[:, d, 0:NT], la[:, d, 0:NT], ACT.Square).then_inc(lru_a2, 1)
                    act.wait_ge(ps_free[0], FIRST + l * SET_JOBS[0] + 3 * t + 2)
                    nc.scalar.activation(gg[:, t, 0:NT], gg[:, t, 0:NT], ACT.Gelu_apprx_tanh).then_inc(gelu_done, 1)
                    for d in range(2):
                        act.wait_ge(lru_v, (l * LT + t) * 2 + d + 1)
                        nc.scalar.activation(lt_[:, d, 0:NT], lt_[:, d, 0:NT], ACT.Sqrt).then_inc(lru_root, 1)
                for n in range(4):
                    ab = T[2 + n % 2]
                    act.wait_ge(mm_done, FIRST + done(l, J_W + n))
                    if n >= 2:
                        act.wait_ge(d_ready, l * 4 + n - 1)
                    nc.scalar.activation(blk(ab[:, :]), ps(J_W + n), ACT.Abs, bias=par[:, l, P_BG + n:P_BG + n + 1])\
                        .then_inc(softplus_step, 1)
                    act.wait_ge(softplus_step, l * 12 + 3 * n + 1)
                    nc.scalar.activation(ab[:, 0:NT], ab[:, 0:NT], ACT.Exp, scale=-1.0).then_inc(softplus_step, 1)
                    act.wait_ge(softplus_step, l * 12 + 3 * n + 2)
                    nc.scalar.activation(ab[:, 0:NT], ab[:, 0:NT], ACT.Ln, bias=1.0).then_inc(softplus_step, 1)
                for e in range(4):
                    j = e % 2
                    for d in range(2):
                        if e == 0:
                            act.wait_ge(d_ready, l * 4 + 2 * d + 2)
                        else:
                            act.wait_ge(qk_made, l * 8 + 2 * (e - 1) + d + 1)
                        nc.scalar.activation(ee[:, d, 0:NT], dd[:, 2 * d + j, 0:NT], ACT.Exp,
                                             scale=(1.0 if e < 2 else -1.0) / GATE_NORM).then_inc(e_ready, 1)
                act.wait_ge(fac_in, 2 * l + 2)
                nc.scalar.activation(fac[:, :, :], fac[:, :, :], ACT.Exp, scale=1.0 / GATE_NORM).then_inc(fac_ready, 1)
                for h in range(HEADS):
                    act.wait_ge(ps_free[(J_SG + h) % 2], FIRST + freed(l, J_SG + h))
                    nc.scalar.activation(sg[:, h, 0:NT], sg[:, h, 0:NT], ACT.Silu).then_inc(silu_done, 1)
                act.wait_ge(mm_done, FIRST + done(l, J_V + 3))
                for t in range(LT):
                    nc.scalar.activation(X[:, t, 0, 0:NT], y_lru[:, t, 0:NT], ACT.Copy).then_inc(x_hi, 1)
                act.wait_ge(x_lo, xbase + LT)
                for n in range(NC):
                    act.wait_ge(g_vt, l * NC + n + 1)
                    nc.scalar.activation(v_tok[0:C, NC - 1 - n, :], banks[0:C, n % 2, :], ACT.Copy).then_inc(vtok_ready, 1)
                act.wait_ge(stb_ready, (l + 1) * (NC - 1))

                def before_scores(c):
                    if c < NC - 1:
                        act.wait_ge(g_ktf, l * (NC - 1) + c + 1)
                        if c >= 2:
                            act.wait_ge(g_kvf, l * (NC - 1) + c - 1)
                        nc.scalar.activation(kt_f[0:C, c % 2].rearrange("p j n -> p (j n)"), banks[0:C, 0, 0:256], ACT.Copy)\
                            .then_inc(ktf_ready, 1)
                    act.wait_ge(g_s, l * NC + c + 1)
                    if c >= 2:
                        act.wait_ge(g_o, l * NC + c - 1)
                    nc.scalar.activation(p_t[0:C, c % 2], banks[0:C, 2:4, 0:2 * C], ACT.Copy)\
                        .then_inc(p_fwd, 1)

                def head_norm(c):
                    act.wait_ge(g_ss, l * NC + c + 1)
                    flat = o_rs[:, c % 2, :]
                    if c >= 2:
                        act.wait_ge(oy_ready, l * NC + c - 1)
                    nc.scalar.activation(flat, banks[:, 6, 0:HEADS * C], ACT.Ln, scale=1.0 / DV, bias=eps[:, 0:1])\
                        .then_inc(ss_log, 1)
                    act.wait_ge(ss_log, l * NC + c + 1)
                    nc.scalar.activation(flat, flat, ACT.Exp, scale=-0.5).then_inc(ors_ready, 1)
                    act.wait_ge(oy_ready, l * NC + c + 1)
                    nc.scalar.activation(by_parity(X[:, 4:8, 0, c * C:(c + 1) * C]), heads(o_y[:, c % 2, :]), ACT.Copy).then_inc(x_hi, 1)

                before_scores(0)
                for c in range(NC):
                    if c + 1 < NC:
                        before_scores(c + 1)
                    act.wait_ge(g_o, l * NC + c + 1)
                    if c >= 2:
                        act.wait_ge(g_ss, l * NC + c - 1)
                    nc.scalar.activation(o_sq[:, c % 2, :].rearrange("p (r n) -> p r n", r=2), banks[:, 4:6, 0:2 * C], ACT.Square)\
                        .then_inc(osq_ready, 1)
                    if c >= 1:
                        head_norm(c - 1)
                head_norm(NC - 1)
                act.wait_ge(x_lo, xbase + LT + NC)
                act.wait_ge(h_stored, 16 * (16 * l + 8))
                for m in range(4):
                    load_old(m, h_out[l])
                for m in range(KT):
                    square_out(l, m, J_O + m, (J_O + m) // 2, 0)
                inv_rms(l, J_POST, 1)
                update(l, 0, h_out[l], h_mid[l])
                inv_rms(l, J_STAT2, 2)

                def hidden(g, i, jx):
                    jp = J_MLP + i
                    act.wait_ge(ps_free[jp % 2], FIRST + l * SET_JOBS[jp % 2] + jx + i // 2 + 1)
                    if i >= 2:
                        act.wait_ge(a_lo, FIRST + l * F_TILES + g * GT + i - 1)
                    else:
                        act.wait_ge(a_lo, FIRST + l * F_TILES + g * GT)
                    nc.scalar.activation(T[2 + i % 2][:, :], T[i % 2][:, :], ACT.Square).then_inc(act_sq, 1)
                    act.wait_ge(act_sq, l * F_TILES + g * GT + i + 1)
                    nc.scalar.activation(act_hi[:, i, :], T[2 + i % 2][:, :], ACT.Copy).then_inc(a_hi, 1)

                with act.Fori(0, GROUPS - 1) as g:
                    for i in range(GT):
                        hidden(g, i, J_MLP // 2 + 6 * g)
                act.wait_ge(h_stored, 16 * (16 * l + 16))
                for m in range(4):
                    load_old(m, h_mid[l])
                for i in range(GT):
                    hidden(GROUPS - 1, i, J_MLP // 2 + 6 * (GROUPS - 1))
                for m in range(KT):
                    if m < 2:
                        act.wait_ge(a_lo, FIRST + (l + 1) * F_TILES)
                    square_out(l, m, j_down(GROUPS - 1, m), j_down(GROUPS - 1, m) // 2, 1)
                inv_rms(l, J_POST2, 3)
                update(l, 1, h_mid[l], h_out[l + 1])
            act.wait_ge(h_stored, 16 * (16 * L + 8))

        @block.vector
        def _(dve):
            V = nc.vector

            def split_lo(m):
                V.tensor_tensor(X[:, m, 1, :], Y[:, m, :], X[:, m, 0, :].bitcast(f32), ALU.subtract).then_inc(x_lo, 1)

            def scaled_out(l, jp, jx, jd, out, rows=128, factor=None):
                dve.wait_ge(mm_done, FIRST + jd)
                if factor is None:
                    ins = V.tensor_tensor(out, ps(jp, rows), blk(rs[0:rows, :]), ALU.mult)
                else:
                    ins = V.scalar_tensor_tensor(out=out, in0=ps(jp, rows), scalar=factor, in1=blk(rs[0:rows, :]),
                                                 op0=ALU.mult, op1=ALU.mult)
                ins.then_inc(ps_free[jp % 2], 1)

            def add_square(l, phase, m):
                dve.wait_ge(sq_y, l * 16 + phase * 8 + m + 1)
                if m == 1:
                    pass
                else:
                    dve.wait_ge(acc_done, l * 14 + phase * 7 + m - 1)
                V.tensor_tensor(acc[:, :], acc[:, :], T[2 + m % 2][:, :], ALU.add).then_inc(acc_done, 1)

            def update(l, phase, gain, xbase):
                for m in range(KT):
                    V.tensor_tensor(Y[:, m, :], Y[:, m, :], rs[:, :], ALU.mult).then_inc(y_scaled, 1)
                    dve.wait_ge(y_scaled, l * 16 + phase * 8 + m + 1)
                    dve.wait_ge(hold_loaded[m % 4], 16 * (4 * l + 2 * phase + m // 4 + 1))
                    V.scalar_tensor_tensor(out=Y[:, m, :], in0=Y[:, m, :], scalar=par[:, l, gain + m:gain + m + 1],
                                           in1=h_old[:, m % 4, :], op0=ALU.mult, op1=ALU.add).then_inc(y_new, 1)
                    if m >= 1:
                        dve.wait_ge(x_hi, xbase + m)
                        split_lo(m - 1)
                dve.wait_ge(x_hi, xbase + KT)
                split_lo(KT - 1)

            lam, sp, nsp = (par[:, :, c:c + 8] for c in (P_LAM, P_SP, P_NSP))
            z2 = acc[:, 0:8 * L].rearrange("p (l n) -> p l n", l=L)
            series = acc[:, 64:64 + 8 * L].rearrange("p (l n) -> p l n", l=L)
            steps = [2]

            def step(ins):
                steps[0] += 1
                ins.then_inc(par_step, 1)
                dve.wait_ge(par_step, steps[0])

            dve.wait_ge(par_step, 2)
            step(V.tensor_scalar(nsp, sp, 2.0, None, ALU.add))
            step(V.reciprocal(nsp, nsp))
            step(V.tensor_tensor(sp, sp, nsp, ALU.mult))
            step(V.tensor_tensor(z2, sp, sp, ALU.mult))
            step(V.tensor_scalar(series, z2, 1.0 / 19, 1.0 / 17, ALU.mult, ALU.add))
            for n in (15, 13, 11, 9, 7, 5, 3, 1):
                step(V.tensor_tensor(series, series, z2, ALU.mult))
                step(V.tensor_scalar(series, series, 1.0 / n, None, ALU.add))
            step(V.scalar_tensor_tensor(out=sp, in0=sp, scalar=2 * LRU_C, in1=series, op0=ALU.mult, op1=ALU.mult))
            step(V.tensor_scalar(nsp, lam, -LRU_C, 0.0, ALU.mult, ALU.max))
            step(V.tensor_tensor(sp, sp, nsp, ALU.add))
            V.tensor_scalar(nsp, sp, -1.0, None, ALU.mult).then_inc(par_ready, 1)
            for m in range(KT):
                dve.wait_ge(x_loaded[m], 16)
                dve.wait_ge(x_hi, m + 1)
                split_lo(m)

            with dve.Fori(0, L) as l:
                xbase = l * X_PER + KT

                def root_to_state(t):
                    for d in range(2):
                        n = (l * LT + t) * 2 + d
                        dve.wait_ge(lru_root, n + 1)
                        V.tensor_tensor(li[:, d, 0:NT], li[:, d, 0:NT], lt_[:, d, 0:NT], ALU.mult).then_inc(lru_u, 1)
                    dve.wait_ge(ylru_done, FIRST + l * LT + t)
                    for d in range(2):
                        n = (l * LT + t) * 2 + d
                        dve.wait_ge(lru_u, n + 1)
                        a, u, h = la[:, d, 0:NT], li[:, d, 0:NT], hh[d][:, 0:NT]
                        if d == 1:
                            a, u, h = a[:, ::-1], u[:, ::-1], h[:, ::-1]
                        V.tensor_tensor_scan(h, a, u, 0.0, ALU.mult, ALU.add).then_inc(lru_h, 1)

                def lru_result(t):
                    dve.wait_ge(lru_h, FIRST + (l * LT + t) * 2 + 2)
                    V.tensor_tensor(hh[0][:, 0:NT], hh[0][:, 0:NT], hh[1][:, 0:NT], ALU.add).then_inc(lru_sum, 1)
                    dve.wait_ge(lru_sum, l * LT + t + 1)
                    dve.wait_ge(gelu_done, l * LT + t + 1)
                    V.tensor_tensor(y_lru[:, t, 0:NT], hh[0][:, 0:NT], gg[:, t, 0:NT], ALU.mult).then_inc(ylru_done, 1)

                def branch_in(t):
                    scaled_out(l, 1, 0, l * NJ + 6 * t + 2, blk(xb[:, 2:2 + NP]))

                def conv(t):
                    base = (l * LT + t) * 3

                    def tap(n):
                        return par[:, l, bass.ds(P_CONVW + 4 * t + n, 1)]
                    dve.wait_ge(ps_free[1], FIRST + l * SET_JOBS[1] + 3 * t + 1)
                    V.tensor_scalar(xc[:, :], xb[:, 0:NP], tap(0), par[:, l, bass.ds(P_CONVB + t, 1)], ALU.mult, ALU.add)\
                        .then_inc(conv_step, 1)
                    for n in range(1, 4):
                        dve.wait_ge(conv_step, base + n)
                        V.scalar_tensor_tensor(out=xc[:, :], in0=xb[:, n:n + NP], scalar=tap(n), in1=xc[:, :],
                                               op0=ALU.mult, op1=ALU.add).then_inc(conv_step if n < 3 else xc_ready, 1)

                def gate_in(t):
                    scaled_out(l, 2, 0, l * NJ + 6 * t + 3, blk(gg[:, t, :]))

                def input_and_decay(t):
                    dve.wait_ge(xc_ready, l * LT + t + 1)
                    for d in range(2):
                        dve.wait_ge(ps_free[0], FIRST + l * SET_JOBS[0] + 3 * t + 3 + d)
                        V.tensor_tensor(li[:, d, 0:NT], li[:, d, 0:NT], xc[:, 0:NT], ALU.mult).then_inc(lru_ix, 1)
                    for d in range(2):
                        n = (l * LT + t) * 2 + d
                        dve.wait_ge(lru_a2, n + 1)
                        dve.wait_ge(lru_tanh, n + 1)
                        V.scalar_tensor_tensor(out=lt_[:, d, 0:NT], in0=lr[:, d, 0:NT], scalar=1.0, in1=lt_[:, d, 0:NT],
                                               op0=ALU.add, op1=ALU.mult).then_inc(lru_v, 1)

                dve.wait_ge(h_stored, 16 * (16 * l + 8))
                dve.wait_ge(rs_ready, 4 * l + 1)
                V.memset(xb[:, 0:2], 0.0).then_inc(pad_zeroed, 1)
                V.memset(xb[:, 2 + NP:4 + NP], 0.0).then_inc(pad_zeroed, 1)
                dve.wait_ge(pad_zeroed, 2 * l + 2)
                branch_in(0)
                conv(0)
                gate_in(0)
                input_and_decay(0)
                with dve.Fori(1, LT) as t:
                    branch_in(t)
                    dve.wait_ge(mm_done, FIRST + l * NJ + 6 * t + 1)
                    dve.wait_ge(lru_ix, (l * LT + t) * 2)
                    conv(t)
                    root_to_state(t - 1)
                    gate_in(t)
                    lru_result(t - 1)
                    input_and_decay(t)
                scaled_out(l, J_ZG, 0, done(l, J_ZG), blk(acc[0:2 * RANK, :]), rows=2 * RANK)
                root_to_state(LT - 1)
                scaled_out(l, J_Q0, 0, done(l, J_Q0), blk(T[1][:, :]), factor=DK ** -0.5)
                lru_result(LT - 1)

                for n in range(4):
                    log_term, d_n = T[2 + n % 2][:, 0:NT], dd[:, n, 0:NT]
                    dve.wait_ge(softplus_step, l * 12 + 3 * n + 1)
                    V.tensor_scalar(blk(dd[:, n, :]), ps(J_W + n), par[:, l, P_BG + n:P_BG + n + 1], 0.0, ALU.add, ALU.min)\
                        .then_inc(ps_free[(J_W + n) % 2], 1)
                    dve.wait_ge(softplus_step, l * 12 + 3 * n + 3)
                    dve.wait_ge(ps_free[(J_W + n) % 2], FIRST + freed(l, J_W + n))
                    V.tensor_tensor(d_n, d_n, log_term, ALU.subtract).then_inc(decay_step, 1)
                    dve.wait_ge(decay_step, l * 8 + 2 * n + 1)
                    if n < 2:
                        V.tensor_tensor_scan(log_term, reset[:, 0:NT], d_n, 0.0, ALU.mult, ALU.add).then_inc(decay_step, 1)
                    else:
                        V.tensor_tensor_scan(log_term[:, ::-1], reset[:, 1:NT + 1][:, ::-1], d_n[:, ::-1], 0.0, ALU.mult, ALU.add)\
                            .then_inc(decay_step, 1)
                    dve.wait_ge(decay_step, l * 8 + 2 * n + 2)
                    by_chunk = log_term.rearrange("p (c t) -> p c t", t=C)
                    end = C - 1 if n < 2 else 0
                    V.tensor_copy(b_mid[:, n, :], by_chunk[:, :, MID]).then_inc(fac_step, 1)
                    V.tensor_copy(b_tot[:, n, :], by_chunk[:, :, end]).then_inc(fac_step, 1)
                    dve.wait_ge(fac_step, l * 9 + 2 * n + 2)
                    V.tensor_tensor(d_n.rearrange("p (c t) -> p c t", t=C), by_chunk,
                                    b_mid[:, n, :].unsqueeze(2).to_broadcast([128, NC, C]), ALU.subtract).then_inc(d_ready, 1)
                V.tensor_tensor(fac[:, :, :], b_tot[:, :, :], b_mid[:, :, :], ALU.subtract).then_inc(fac_step, 1)
                dve.wait_ge(fac_step, l * 9 + 9)
                V.tensor_tensor(fac[:, 0:2, 0:NC - 1], fac[:, 0:2, 0:NC - 1], b_mid[:, 0:2, 1:NC], ALU.add).then_inc(fac_in, 1)
                V.tensor_tensor(fac[:, 2:4, 1:NC], fac[:, 2:4, 1:NC], b_mid[:, 2:4, 0:NC - 1], ALU.add).then_inc(fac_in, 1)
                for e, j in enumerate((J_Q0, J_Q1, J_K, J_K + 1)):
                    if e > 0:
                        dve.wait_ge(qk_made, l * 8 + 2 * e)
                        scaled_out(l, j, 0, done(l, j), blk(T[1][:, :]), factor=DK ** -0.5 if e == 1 else None)
                    dve.wait_ge(ps_free[j % 2], FIRST + freed(l, j))
                    for d in range(2):
                        dve.wait_ge(e_ready, l * 8 + 2 * e + d + 1)
                        out = (qi if e < 2 else ki)[:, 2 * d + e % 2, 0:NT]
                        V.tensor_tensor(out, T[1][:, 0:NT], ee[:, d, 0:NT], ALU.mult).then_inc(qk_made, 1)
                dve.wait_ge(qk_made, l * 8 + 8)
                for h in range(HEADS):
                    scaled_out(l, J_SG + h, 0, done(l, J_SG + h), blk(sg[:, h, :]))
                for h in range(HEADS):
                    scaled_out(l, J_V + h, 0, done(l, J_V + h), blk(vT[:, h, :]))
                for t in range(LT):
                    dve.wait_ge(x_hi, xbase + t + 1)
                    V.tensor_tensor(X[:, t, 1, 0:NT], y_lru[:, t, 0:NT], X[:, t, 0, 0:NT].bitcast(f32), ALU.subtract)\
                        .then_inc(x_lo, 1)
                dve.wait_ge(fac_ready, l + 1)
                for n in range(NC - 1):
                    c = NC - 1 - n
                    dve.wait_ge(g_ktb, l * (NC - 1) + n + 1)
                    if n >= 2:
                        dve.wait_ge(g_kvb, l * (NC - 1) + n - 1)
                    V.tensor_copy(kt_b[0:C, n % 2].rearrange("p j n -> p (j n)"), banks[0:C, 2 + n % 2, 0:256])\
                        .then_inc(ktb_ready, 1)
                    dve.wait_ge(g_kvb, l * (NC - 1) + n + 1)
                    kv = banks[:, 4 + n % 2, 0:2 * DV].rearrange("p (j v) -> p j v", j=2)
                    if n == 0:
                        V.tensor_copy(kv_b[:, :, :], kv).then_inc(stb_sum, 1)
                    else:
                        dve.wait_ge(stb_ready, l * (NC - 1) + n)
                        V.tensor_tensor(kv_b[:, :, :], kv, st_b[:, c, :, :], ALU.add).then_inc(stb_sum, 1)
                    dve.wait_ge(stb_sum, l * (NC - 1) + n + 1)
                    V.tensor_tensor(st_b[:, c - 1, :, :], kv_b[:, :, :],
                                    fac[:, 2:4, c:c + 1].to_broadcast([128, 2, DV]), ALU.mult).then_inc(stb_ready, 1)
                dve.wait_ge(silu_done, (l + 1) * HEADS)

                def select(c):
                    dve.wait_ge(g_s, l * NC + c + 1)
                    dve.wait_ge(p_fwd, l * NC + c + 1)
                    dve.sem_inc(waited_dve, 1)
                    V.copy_predicated(p_t[0:C, c % 2], later[:, :, :].rearrange("p (r j) c -> p r (j c)", r=2),
                                      banks[0:C, 2:4, 2 * C:4 * C]).then_inc(p_ready, 1)

                def finish(c):
                    dve.wait_ge(ors_ready, l * NC + c + 1)
                    dve.wait_ge(o_gated, l * NC + c + 1)
                    V.tensor_tensor(o_y[:, c % 2, :], o_y[:, c % 2, :], o_rs[:, c % 2, :], ALU.mult).then_inc(oy_ready, 1)
                    dve.wait_ge(x_hi, xbase + LT + c + 1)
                    dve.wait_ge(oy_ready, l * NC + c + 1)
                    cols = slice(c * C, (c + 1) * C)
                    V.tensor_tensor(by_parity(X[:, 4:8, 1, cols]), heads(o_y[:, c % 2, :]),
                                    by_parity(X[:, 4:8, 0, cols].bitcast(f32)), ALU.subtract)\
                        .then_inc(x_lo, 1)

                select(0)
                for c in range(NC):
                    if c + 1 < NC:
                        select(c + 1)
                    if c < NC - 1:
                        dve.wait_ge(g_kvf, l * (NC - 1) + c + 1)
                        kv = banks[:, 1, 0:2 * DV].rearrange("p (j v) -> p j v", j=2)
                        if c == 0:
                            V.tensor_copy(kv_f[:, :, :], kv).then_inc(stf_sum, 1)
                        else:
                            dve.wait_ge(stf_ready, l * (NC - 1) + c)
                            V.tensor_tensor(kv_f[:, :, :], kv, st_f[:, c % 2], ALU.add).then_inc(stf_sum, 1)
                            dve.wait_ge(g_o, l * NC + c)
                        dve.wait_ge(stf_sum, l * (NC - 1) + c + 1)
                        V.tensor_tensor(st_f[:, (c + 1) % 2], kv_f[:, :, :],
                                        fac[:, 0:2, c:c + 1].to_broadcast([128, 2, DV]), ALU.mult).then_inc(stf_ready, 1)
                    dve.wait_ge(osq_ready, l * NC + c + 1)
                    if c >= 2:
                        dve.wait_ge(x_lo, xbase + LT + c - 1)
                    V.tensor_tensor(heads(o_y[:, c % 2, :]),
                                    banks[:, 4:6, 0:2 * C].rearrange("p r (j c) -> p r j c", j=2),
                                    by_parity(sg[:, :, c * C:(c + 1) * C]), ALU.mult).then_inc(o_gated, 1)
                    if c >= 1:
                        finish(c - 1)
                finish(NC - 1)

                for m in range(KT):
                    j = J_O + m
                    dve.wait_ge(mm_done, FIRST + done(l, j))
                    V.tensor_copy(blk(Y[:, m, :]), ps(j)).then_inc(ps_free[j % 2], 1)
                    if m >= 2:
                        add_square(l, 0, m - 1)
                add_square(l, 0, KT - 1)
                dve.wait_ge(rs_ready, 4 * l + 2)
                update(l, 0, P_GMIXPOST, xbase + LT + NC)

                def group(g, jx, jd, first):
                    def relu(i):
                        jp = J_MLP + i
                        dve.wait_ge(mm_done, FIRST + jd + i + 1)
                        if i >= 2:
                            dve.wait_ge(act_sq, l * F_TILES + g * GT + i - 1)
                        V.scalar_tensor_tensor(out=blk(T[i % 2][:, :]), in0=ps(jp), scalar=0.0, in1=blk(rs[:, :]),
                                               op0=ALU.max, op1=ALU.mult).then_inc(ps_free[jp % 2], 1)

                    def hidden_lo(i):
                        dve.wait_ge(a_hi, l * F_TILES + g * GT + i + 1)
                        V.tensor_tensor(act_lo[:, i, :], T[2 + i % 2][:, :], act_hi[:, i, :].bitcast(f32), ALU.subtract)\
                            .then_inc(a_lo, 1)

                    for i in range(GT):
                        relu(i)
                        if i >= 1:
                            hidden_lo(i - 1)
                    hidden_lo(GT - 1)

                def down_sum(m, jd, first):
                    jp = J_MLP + GT + m
                    dve.wait_ge(mm_done, FIRST + jd + GT + m + 1)
                    if first:
                        ins = V.tensor_copy(blk(Y[:, m, :]), ps(jp))
                    else:
                        ins = V.tensor_tensor(blk(Y[:, m, :]), ps(jp), blk(Y[:, m, :]), ALU.add)
                    ins.then_inc(ps_free[jp % 2], 1)

                dve.wait_ge(rs_ready, 4 * l + 3)
                group(0, J_MLP // 2, l * NJ + J_MLP, True)
                dve.wait_ge(h_stored, 16 * (16 * l + 16))
                for m in range(KT):
                    down_sum(m, l * NJ + J_MLP, True)
                with dve.Fori(1, GROUPS - 1) as g:
                    group(g, 0, l * NJ + J_MLP + 12 * g, False)
                    for m in range(KT):
                        down_sum(m, l * NJ + J_MLP + 12 * g, False)
                g = GROUPS - 1
                group(g, 0, l * NJ + J_MLP + 12 * g, False)
                for m in range(KT):
                    down_sum(m, l * NJ + J_MLP + 12 * g, False)
                    if m >= 2:
                        add_square(l, 1, m - 1)
                add_square(l, 1, KT - 1)
                dve.wait_ge(rs_ready, 4 * l + 4)
                update(l, 1, P_GMLPPOST, xbase + LT + NC + KT)



def kernel(**inputs):
    import numpy as np
    import concourse.bacc as bacc
    from concourse.bass_utils import run_bass_kernel_spmd

    a = {k: np.asarray(v) for k, v in inputs.items()}

    tokens = np.concatenate([a["meta_tokens"], a["x"][0]], axis=0)
    x_in = np.zeros((KT, 128, NP), np.float32)
    x_in[:, :, :NT] = tokens.T.reshape(KT, 128, NT)

    def out_tile(w, c):
        return w[:, c:c + 128].reshape(KT, 128, 128).transpose(1, 0, 2)

    q0, k0, v0, g0, z0 = 2 * LW, 2 * LW + 256, 2 * LW + 512, 2 * LW + 1024, 2 * LW + 1536
    w_units = np.empty((L, UNITS, 128, 8, 128), np.float32)
    w_gates = np.zeros((L, LT, 128, 4, 128), np.float32)
    w_decay = np.zeros((L, 2 * RANK, 512), np.float32)
    w_zg = np.empty((L, 128, KT, 2 * RANK), np.float32)
    params = np.empty((128, L, N_LOADED), np.float32)
    for l in range(L):
        win, wout, up, down = a["w_in"][l], a["w_out"][l], a["w_mlp_up"][l], a["w_mlp_down"][l]
        columns = [c for t in range(LT) for c in (128 * t, LW + 128 * t)]
        columns += [q0, q0 + 128, k0, k0 + 128] + [g0 + 128 * h for h in range(4)] + [v0 + 128 * h for h in range(4)]
        for u, c in enumerate(columns):
            w_units[l, u] = out_tile(win, c)
        for m in range(KT):
            w_units[l, U_OUT + m] = out_tile(wout, 128 * m)
        for g in range(GROUPS):
            for i in range(GT):
                w_units[l, U_MLP + 8 * g + i] = out_tile(up, 128 * (GT * g + i))
                w_units[l, U_MLP + 8 * g + GT + i] = down[512 * g:512 * (g + 1), 256 * i:256 * (i + 1)]\
                    .reshape(4, 128, 2, 128).transpose(1, 2, 0, 3).reshape(128, 8, 128)
        w_zg[l] = win[:, z0:z0 + 2 * RANK].reshape(KT, 128, 2 * RANK).transpose(1, 0, 2)
        for n, name in enumerate(("lru_wa_f", "lru_wx_f", "lru_wa_b", "lru_wx_b")):
            for head in range(8):
                r = 64 * (head % 2)
                w_gates[l, head // 2, r:r + 64, n, r:r + 64] = a[name][l, head]
        w_decay[l, :RANK, 0:256] = a["gla_wg_f"][l]
        w_decay[l, RANK:, 256:512] = a["gla_wg_b"][l]

        def put(at, v):
            v = v.reshape(-1, 128).T
            params[:, l, at:at + v.shape[1]] = v
        for t in range(LT):
            params[:, l, P_CONVW + 4 * t:P_CONVW + 4 * t + 4] = a["conv_w"][l][:, 128 * t:128 * t + 128].T
        for at, name in ((P_CONVB, "conv_b"), (P_BAF, "lru_ba_f"), (P_BXF, "lru_bx_f"), (P_BAB, "lru_ba_b"),
                         (P_BXB, "lru_bx_b"), (P_LAM, "lru_lambda_f"), (P_LAM + 4, "lru_lambda_b"),
                         (P_BG, "gla_bg_f"), (P_BG + 2, "gla_bg_b"), (P_GMIX, "norm_mix_pre"),
                         (P_GMIXPOST, "norm_mix_post"), (P_GMLP, "norm_mlp_pre"), (P_GMLPPOST, "norm_mlp_post"),
                         (P_GOUT + 4, "gla_head_norm")):
            put(at, a[name][l])
        params[:, l, P_GOUT:P_GOUT + 4] = 1.0
        params[:, l, P_ONE:P_ONE + 8] = 1.0

    nc = bacc.Bacc("TRN2", target_bir_lowering=False, num_devices=1)
    arrays = {"x_in": x_in, "w_units": w_units, "w_zg": w_zg, "w_gates": w_gates, "w_decay": w_decay, "params": params}
    args = [nc.dram_tensor(n, v.shape, mybir.dt.float32, kind="ExternalInput").ap() for n, v in arrays.items()]
    h_out = nc.dram_tensor("h_out", (L + 1, KT, 128, NP), mybir.dt.float32, kind="ExternalOutput").ap()
    trunk_kernel(nc, *args, h_out)
    r = run_bass_kernel_spmd(nc, [arrays], core_ids=[0])
    h = np.asarray(r.results[0]["h_out"])[L]
    return np.ascontiguousarray(h.reshape(D, NP)[:, N_META:NT].T)[None]
```

```python
import concourse.bass as bass
from concourse import mybir
from contextlib import ExitStack

L = 2
D = 1024
N_META, SEQ = 16, 1024
NT = N_META + SEQ
NB, BN = 3, 348
NP = NB * BN
KT = D // 128
LW, LT = 512, 4
DK, DV, HEADS, RANK = 64, 128, 4, 16
C, NC = 104, NT // 104
MID = C // 2 - 1
F_TILES, GROUPS, GT = 32, 8, 4
EPS = 1e-6
GATE_NORM = 16.0
LRU_C = 8.0

U_OUT, U_MLP = 20, 28
UNITS = U_MLP + 8 * GROUPS
PAIRS = UNITS // 2

(P_CONVW, P_CONVB, P_BAF, P_BXF, P_BAB, P_BXB, P_LAM, P_BG, P_GMIX, P_GMIXPOST, P_GMLP, P_GMLPPOST,
 P_GOUT, P_ONE, P_SP, P_NSP, NPAR) = (0, 16, 20, 24, 28, 32, 36, 44, 48, 56, 64, 72, 80, 88, 96, 104, 112)
N_LOADED = P_SP



def j_x(t): return 6 * t + (t > 0)
def j_gate(t): return 6 * t + 1 + (t > 0)
def j_lru(t, n): return 6 * t + 3 + n


J_ZG, J_Q0, J_Q1, J_W, J_K, J_SG, J_V, J_O, J_MLP = 2, 25, 26, 27, 31, 33, 37, 41, 49
NJ = J_MLP + 12 * GROUPS
SET_JOBS = ((NJ + 1) // 2, NJ // 2)


def j_up(g, i): return J_MLP + 12 * g + i
def j_down(g, m): return J_MLP + 12 * g + GT + m


PRE_MIX, POST_MIX, PRE_MLP, POST_MLP, NEXT_PRE_MIX = range(5)
SUMS = 4 * NB
NX, QT = NB * KT // 2, KT // 2
SQ_RING = 3
H_FIRST = 2 * NB

FIRST = 3

X_PER = 4 + NC + 2 * NX


def squares_read(n):
    n -= SQ_RING
    n += n % QT == QT - 1
    return n + 1 - n // QT


def piece(n):
    return n % QT * 2, n // QT


def trunk_kernel(nc, x_in, w_units, w_zg, w_gates, w_decay, params, h_out):
    f32, f32r, bf16, u8 = mybir.dt.float32, mybir.dt.float32r, mybir.dt.bfloat16, mybir.dt.uint8
    ALU, ACT = mybir.AluOpType, mybir.ActivationFunctionType
    h_mid = nc.dram_tensor("h_mid", (L, KT, 128, NP), f32, kind="Internal").ap()

    ctx = ExitStack()
    with ctx:
        def sb(name, shape, dt=f32):
            return ctx.enter_context(nc.sbuf_tensor(name, shape, dt))

        def sem(name):
            return ctx.enter_context(nc.semaphore(name))

        X = sb("X", [128, KT, 2, NP], f32r)
        w_raw = sb("w_raw", [128, 2, 8, 128])
        w_hl = sb("w_hl", [128, 2, 2, 8, 128], f32r)
        par = sb("par", [128, L, NPAR])
        ones = sb("ones", [128, 128])
        ident = sb("ident", [128, 128])
        gates_w = sb("gates_w", [128, 4, 128])
        decay_w = sb("decay_w", [2 * RANK, 512])
        zg_raw = sb("zg_raw", [128, 8, 2 * RANK])
        zg_hl = sb("zg_hl", [128, 2, 8, 2 * RANK], f32r)
        reset = sb("reset", [128, NT + 1], bf16)
        later = sb("later", [C, HEADS, C], u8)
        eps = sb("eps", [128, 1])
        b_mid = sb("b_mid", [128, 4, NC])
        b_tot = sb("b_tot", [128, 4, NC])
        fac = sb("fac", [128, 4, NC])
        TB = NP * 4
        base = (nc.sbuf_base + 31) // 32 * 32

        def at(name, shape, tile, dt=f32, extra=0):
            return nc.alloc_sbuf_tensor_at(name, shape, dt, offset=base + tile * TB + extra, align_bytes=16)

        A_RS, A_ACC, A_T, A_YL, A_T3, A_SG, A_D, A_QK = 0, 1, 2, 5, 9, 10, 14, 18
        rs = at("rs", [128, NP], A_RS)
        acc = at("acc", [128, NP], A_ACC)
        T = [at("T0", [128, NP], A_T), at("T1", [128, NP], A_T + 1), at("T2", [128, NP], A_T + 2), at("T3", [128, NP], A_T3)]
        y_lru = at("y_lru", [128, LT, NP], A_YL)
        lr = at("lr", [128, 2, NP], A_SG)
        li = at("li", [128, 2, NP], A_SG + 2)
        la = at("la", [128, 2, NP], A_D)
        lt_ = at("lt", [128, 2, NP], A_D + 2)
        xc = at("xc", [128, NP], A_QK)
        gg = at("gg", [128, LT, NP], A_QK + 1)
        xb = at("xb", [128, NP + 4], A_QK + 5)
        hh = [T[0], at("hh1", [128, NP], A_QK + 7)]
        dd = at("dd", [128, 4, NP], A_D)
        vT = at("vT", [128, HEADS, NP], A_D)
        qi = at("qi", [128, 4, NP], A_QK)
        ki = at("ki", [128, 4, NP], A_QK + 4)
        sg = at("sg", [128, HEADS, NP], A_SG)
        q1 = at("q1", [128, NP], A_SG)
        ee = at("ee", [128, 2, NP], A_SG + 2)
        v_tok = at("v_tok", [128, NC, HEADS * DV], A_YL)
        st_b = at("st_b", [128, NC, 2, DV], A_T)
        kt_b = at("kt_b", [128, 2, 2, 128], A_RS)
        kv_b = at("kv_b", [128, 2, DV], A_RS, extra=2048)
        p_t = at("p_t", [128, 2, 2, 2 * C], A_ACC)
        kt_f = at("kt_f", [128, 2, 2, 128], A_D)
        st_f = at("st_f", [128, 2, 2, DV], A_D, extra=2048)
        kv_f = at("kv_f", [128, 2, DV], A_D, extra=4096)
        o_sq = at("o_sq", [128, 2, HEADS * C], A_D, extra=5120)
        o_rs = at("o_rs", [128, 2, HEADS * C], A_D, extra=5120 + 3328)
        o_y = at("o_y", [128, 2, HEADS * C], A_D, extra=5120 + 6656)
        h_old = at("h_old", [128, 3, 2, BN], A_D)
        w_third = at("w_third", [128, 2, 8, 128], A_D + 2, f32r)
        sq = at("sq", [128, SQ_RING, 2, BN], A_T + 1)
        Y = at("Y", [128, KT, NP], A_QK)
        act_hi = at("act_hi", [128, GT, NP], A_YL, f32r)
        act_lo = at("act_lo", [128, GT, NP], A_SG, f32r)
        assert 5120 + 3 * 3328 <= 4 * TB and 4 * NC * HEADS * DV <= 5 * TB and 4 * NC * 2 * DV <= 3 * TB

        wslots = (w_hl[:, 0], w_hl[:, 1], w_third)

        banks = ctx.enter_context(nc.psum_tensor("banks", [128, 8, 512], f32))

        def ps(j, rows=128):
            s = (j % 2) * NB
            return banks[0:rows, s:s + NB, 0:BN]

        def blk(ap):
            return ap.rearrange("p (b n) -> p b n", b=NB)

        def cols(b):
            return slice(b * BN, (b + 1) * BN)

        def sum_bank(norm, b):
            return banks[:, 6 + (norm * NB + b) % 2, 0:BN]

        w_loaded = [sem(f"w_loaded{i}") for i in range(2)]
        w_scaled = sem("w_scaled")
        w_ready = sem("w_ready")
        zgw_loaded, zgw_step, zgw_ready = sem("zgw_loaded"), sem("zgw_step"), sem("zgw_ready")
        gatew_loaded = sem("gatew_loaded")
        decayw_loaded = sem("decayw_loaded")
        par_loaded, par_step, par_ready = sem("par_loaded"), sem("par_step"), sem("par_ready")
        const_step, const_ready = sem("const_step"), sem("const_ready")
        x_loaded = [sem(f"x_loaded{n}") for n in range(2 * NB)]
        mm_done = sem("mm_done")
        ps_free = [sem("ps_free_a"), sem("ps_free_b")]
        x_hi, x_lo = sem("x_hi"), sem("x_lo")
        sq_pair = sem("sq_pair")
        sq_h, sq_read = sem("sq_h"), sem("sq_read")
        sum_done, sum_read = sem("sum_done"), sem("sum_read")
        rs_ready = sem("rs_ready")
        pad_zeroed, conv_step, xc_ready = sem("pad_zeroed"), sem("conv_step"), sem("xc_ready")
        lru_tanh, lru_a, lru_a2 = sem("lru_tanh"), sem("lru_a"), sem("lru_a2")
        lru_ix, lru_v, lru_root, lru_u, lru_h = (sem(n) for n in ("lru_ix", "lru_v", "lru_root", "lru_u", "lru_h"))
        gelu_done, lru_sum, ylru_done = sem("gelu_done"), sem("lru_sum"), sem("ylru_done")
        softplus_step = sem("softplus_step")
        decay_step, d_ready = sem("decay_step"), sem("d_ready")
        fac_step, fac_in, fac_ready = sem("fac_step"), sem("fac_in"), sem("fac_ready")
        e_ready, qk_made = sem("e_ready"), sem("qk_made")
        silu_done = sem("silu_done")
        g_vt, g_ktb, g_kvb = sem("g_vt"), sem("g_ktb"), sem("g_kvb")
        vtok_ready, ktb_ready, stb_sum, stb_ready = sem("vtok_ready"), sem("ktb_ready"), sem("stb_sum"), sem("stb_ready")
        g_ktf, g_kvf, g_s, g_o, g_ss = (sem(n) for n in ("g_ktf", "g_kvf", "g_s", "g_o", "g_ss"))
        ktf_ready, p_fwd, p_ready = sem("ktf_ready"), sem("p_fwd"), sem("p_ready")
        stf_sum, stf_ready = sem("stf_sum"), sem("stf_ready")
        osq_ready, o_gated, ss_log, ors_ready, oy_ready = (sem(n) for n in ("osq_ready", "o_gated", "ss_log", "ors_ready", "oy_ready"))
        sq_y, acc_done = sem("sq_y"), sem("acc_done")
        hold_loaded = [sem(f"hold_loaded{i}") for i in range(3)]
        last_block, y_last = sem("last_block"), sem("y_last")
        y_scaled, y_new = sem("y_scaled"), sem("y_new")
        h_stored = sem("h_stored")
        act_sq, a_hi, a_lo = sem("act_sq"), sem("a_hi"), sem("a_lo")

        waited_pool, waited_dve = sem("waited_pool"), sem("waited_dve")

        def heads(ap):
            return ap.rearrange("p (r j c) -> p r j c", r=2, j=2)

        def by_parity(ap):
            return ap.rearrange("p (j r) c -> p r j c", r=2)

        def done(l, j):
            return l * NJ + j + 1

        def freed(l, j):
            return l * SET_JOBS[j % 2] + j // 2 + 1

        block = ctx.enter_context(nc.Block())

        @block.sync
        def _(sp):
            sp.sem_inc(w_ready, 2)
            for s in (mm_done, *ps_free, ylru_done, lru_h, a_lo):
                sp.sem_inc(s, FIRST)
            sp.dma_start(par[:, :, 0:N_LOADED], params).then_inc(par_loaded, 16)
            sp.sem_inc(sum_read, 2)

            def pair(l, i):
                for s in range(2):
                    sp.wait_ge(w_ready, (l * PAIRS + i) * 2 + s + 1)
                    sp.dma_start(w_raw[:, s], w_units[l, i * 2 + s]).then_inc(w_loaded[s], 16)

            with sp.Fori(0, L) as l:
                pair(l, 0)
                sp.wait_ge(mm_done, FIRST + l * NJ - 2)
                sp.dma_start(zg_raw[:, :, :], w_zg[l]).then_inc(zgw_loaded, 16)
                sp.dma_start(gates_w[:, :, :], w_gates[l, 0]).then_inc(gatew_loaded, 16)
                sp.dma_start(decay_w[:, :], w_decay[l]).then_inc(decayw_loaded, 16)
                with sp.Fori(1, LT) as t:
                    pair(l, t)
                    sp.wait_ge(mm_done, FIRST + l * NJ + 6 * t + 1)
                    sp.dma_start(gates_w[:, :, :], w_gates[l, t]).then_inc(gatew_loaded, 16)
                with sp.Fori(LT, PAIRS) as i:
                    pair(l, i)

        @block.gpsimd
        def _(pool):
            nc.gpsimd.memset(ones[:, :], 1.0).then_inc(const_step, 1)
            nc.gpsimd.memset(ident[:, :], 0.0).then_inc(const_step, 1)
            nc.gpsimd.memset(reset[:, :], 1.0).then_inc(const_step, 1)
            nc.gpsimd.memset(eps[:, :], EPS).then_inc(const_step, 1)
            pool.wait_ge(const_step, 4)
            nc.gpsimd.memset(reset[:, 0:NT + 1:C], 0.0).then_inc(const_step, 1)
            nc.gpsimd.affine_select(out=ident[:, :], in_=ident[:, :], compare_op=ALU.not_equal, fill=1.0,
                                    base=0, pattern=[[-1, 128]], channel_multiplier=1).then_inc(const_step, 1)
            nc.gpsimd.memset(T[0][0:C, 0:C], 1.0).then_inc(const_step, 1)
            pool.wait_ge(const_step, 7)
            nc.gpsimd.affine_select(out=T[0][0:C, 0:C], in_=T[0][0:C, 0:C], compare_op=ALU.is_gt, fill=0.0,
                                    base=0, pattern=[[-1, C]], channel_multiplier=1).then_inc(const_step, 1)
            pool.wait_ge(const_step, 8)
            nc.gpsimd.tensor_copy(later[:, :, :], T[0][0:C, 0:C].unsqueeze(1).to_broadcast([C, HEADS, C]))\
                .then_inc(const_ready, 1)

            pool.wait_ge(par_loaded, 16)

            def gains(l, column, n=128):
                return par[:, l, column:column + 8].unsqueeze(2).to_broadcast([128, 8, n])

            def split(l, i, s, gain, before, slot):
                unit = (l * PAIRS + i) * 2 + s
                pool.wait_ge(w_loaded[s], 16 * (l * PAIRS + i + 1))
                pool.sem_inc(waited_pool, 1)
                if gain is None:
                    pool.sem_inc(w_scaled, 1)
                else:
                    nc.gpsimd.tensor_tensor(w_raw[:, s], w_raw[:, s], gains(l, gain), ALU.mult).then_inc(w_scaled, 1)
                pool.wait_ge(w_scaled, 2 * unit + 1)
                pool.wait_ge(mm_done, FIRST + before)
                pool.sem_inc(waited_pool, 1)
                nc.gpsimd.tensor_tensor(slot[:, 0], w_raw[:, s], gains(l, P_ONE), ALU.mult).then_inc(w_scaled, 1)
                pool.wait_ge(w_scaled, 2 * unit + 2)
                nc.gpsimd.tensor_tensor(slot[:, 1], w_raw[:, s], slot[:, 0].bitcast(f32), ALU.subtract).then_inc(w_ready, 1)

            def split_pair(l, i, gain, before0, before1, slots=(0, 1)):
                for s, before in ((0, before0), (1, before1)):
                    split(l, i, s, gain, before, wslots[slots[s]])

            def split_lo(xbase):
                for n in range(NX):
                    m, b = piece(n)
                    pool.wait_ge(x_hi, xbase + n + 1)
                    nc.gpsimd.tensor_tensor(X[:, m:m + 2, 1, cols(b)], Y[:, m:m + 2, cols(b)],
                                            X[:, m:m + 2, 0, cols(b)].bitcast(f32), ALU.subtract).then_inc(x_lo, 1)

            def downs(l, g, before0, before1):
                i0 = U_MLP // 2 + 4 * g
                split_pair(l, i0 + 2, None, before0, before1)
                split_pair(l, i0 + 3, None, done(l, j_down(g, 1)), done(l, j_down(g, 3)))

            with pool.Fori(0, L) as l:
                split_pair(l, 0, P_GMIX, l * NJ - 2, l * NJ - 2, (0, 2))
                pool.wait_ge(zgw_loaded, 16 * (l + 1))
                pool.sem_inc(waited_pool, 1)
                nc.gpsimd.tensor_tensor(zg_hl[:, 0], zg_raw[:, :, :], gains(l, P_GMIX, 2 * RANK), ALU.mult).then_inc(zgw_step, 1)
                pool.wait_ge(zgw_step, 2 * l + 1)
                pool.sem_inc(waited_pool, 1)
                nc.gpsimd.tensor_tensor(zg_raw[:, :, :], zg_raw[:, :, :], gains(l, P_GMIX, 2 * RANK), ALU.mult).then_inc(zgw_step, 1)
                pool.wait_ge(zgw_step, 2 * l + 2)
                nc.gpsimd.tensor_tensor(zg_hl[:, 1], zg_raw[:, :, :], zg_hl[:, 0].bitcast(f32), ALU.subtract)\
                    .then_inc(zgw_ready, 1)
                split_lo(l * X_PER)
                split_pair(l, 1, P_GMIX, l * NJ, done(l, j_x(0)), (1, 0))
                for t in range(1, LT):
                    split_pair(l, t + 1, P_GMIX, done(l, j_x(t)), done(l, j_gate(t)), (1, 0))
                split_pair(l, 5, P_GMIX, done(l, J_Q0), done(l, J_Q1), (1, 0))
                with pool.Fori(0, 4) as i:
                    split_pair(l, 6 + i, P_GMIX, done(l, J_K + 2 * i), done(l, J_K + 2 * i + 1), (1, 0))
                with pool.Fori(0, 4) as i:
                    split_pair(l, U_OUT // 2 + i, P_GOUT, done(l, J_O - 2 + 2 * i), done(l, J_O - 1 + 2 * i), (1, 0))
                split_pair(l, U_MLP // 2, P_GMLP, done(l, J_O + 6), done(l, J_O + 5), (1, 2))
                split(l, U_MLP // 2 + 1, 0, P_GMLP, done(l, J_O + 7), wslots[0])
                split_lo(l * X_PER + NX + LT + NC)
                split(l, U_MLP // 2 + 1, 1, P_GMLP, done(l, j_up(0, 0)), wslots[1])
                downs(l, 0, done(l, j_up(0, 2)), done(l, j_up(0, 3)))
                with pool.Fori(1, GROUPS) as g:
                    i0 = U_MLP // 2 + 4 * g
                    split_pair(l, i0, P_GMLP, done(l, j_down(g - 1, 5)), done(l, j_down(g - 1, 7)))
                    split_pair(l, i0 + 1, P_GMLP, done(l, j_up(g, 0)), done(l, j_up(g, 1)))
                    downs(l, g, done(l, j_up(g, 2)), done(l, j_up(g, 3)))

        @block.tensor
        def _(pe):
            def product(out, w, xs, first, last):
                for n, (wp, xp) in enumerate(((w[0], xs[0]), (w[0], xs[1]), (w[1], xs[0]))):
                    for b in range(NB):
                        ins = nc.tensor.matmul(out[:, b, :], wp, blk(xp)[:, b, :],
                                               start=first and n == 0, stop=last and n == 2)
                return ins

            def wslot(s, k):
                return wslots[s][:, 0, k, :], wslots[s][:, 1, k, :]

            def xtile(k):
                return X[:, k, 0, :], X[:, k, 1, :]

            def take_set(l, j):
                pe.wait_ge(ps_free[j % 2], FIRST + l * SET_JOBS[j % 2] + j // 2)

            def unit_job(l, unit, s, jp, jx):
                pe.wait_ge(w_ready, l * UNITS + unit + 3)
                pe.wait_ge(ps_free[jp % 2], FIRST + l * SET_JOBS[jp % 2] + jx)
                for k in range(KT):
                    ins = product(ps(jp), wslot(s, k), xtile(k), k == 0, k == KT - 1)
                ins.then_inc(mm_done, 1)

            def product_block(j, b, w, xs, first, last):
                for n, (wp, xp) in enumerate(((w[0], xs[0]), (w[0], xs[1]), (w[1], xs[0]))):
                    ins = nc.tensor.matmul(ps(j)[:, b, :], wp, xp[:, cols(b)], start=first and n == 0, stop=last and n == 2)
                return ins

            def take_sum_bank(l, norm, b):
                pe.wait_ge(sum_read, l * SUMS + norm * NB + b + 1)

            def add_piece(l, norm, n, sbase):
                b, first, last = n // QT, n % QT == 0, n % QT == QT - 1
                if first:
                    take_sum_bank(l, norm, b)
                pe.wait_ge(sq_pair, sbase + n + 1)
                nc.tensor.matmul(sum_bank(norm, b), ones[:, :], sq[:, n % SQ_RING, 0, :], start=first, stop=last)\
                    .then_inc(sum_done if last else sq_read, 1)

            def first_pair(l, norm, unit, j, s, xbase, sbase):
                def second(b, k):
                    return product_block(j + 1, b, wslot(2, k), xtile(k), k == 0, k == KT - 1)

                for n in range(NX):
                    m, b = piece(n)
                    add_piece(l, norm, n, sbase)
                    if n == 0:
                        for u in range(2):
                            pe.wait_ge(w_ready, l * UNITS + unit + u + 3)
                            take_set(l, j + u)
                    pe.wait_ge(x_hi, xbase + n + 1)
                    pe.wait_ge(x_lo, xbase + n + 1)
                    for k in (m, m + 1):
                        first = product_block(j, b, wslot(s, k), xtile(k), k == 0, k == KT - 1)
                    if n == NX - 1:
                        first.then_inc(mm_done, 1)
                    late = b == NB - 1
                    for k in (m, m + 1):
                        if not late:
                            second(b, k)
                        elif k >= QT:
                            second(b, k - QT)
                for k in range(QT, KT):
                    ins = second(NB - 1, k)
                ins.then_inc(mm_done, 1)

            def by_blocks(l, j, s, blocks, xs):
                for b in range(NB):
                    for n, (k, x) in enumerate(zip(blocks, xs)):
                        ins = product_block(j, b, wslot(s, k), x, n == 0, n == len(blocks) - 1)
                    ins.then_inc(last_block if b < NB - 1 else mm_done, 1)

            def row_sums(l, norm, n):
                for b in range(NB):
                    take_sum_bank(l, norm, b)
                    pe.wait_ge(acc_done, n + b + 1)
                    nc.tensor.matmul(sum_bank(norm, b), ones[:, :], acc[:, cols(b)], start=True, stop=True)\
                        .then_inc(sum_done, 1)

            def lru_gates(l, t):
                pe.wait_ge(gatew_loaded, 16 * (l * LT + t + 1))
                pe.wait_ge(xc_ready, l * LT + t + 1)
                for n in range(4):
                    jp = 3 + n
                    pe.wait_ge(ps_free[jp % 2], FIRST + l * SET_JOBS[jp % 2] + 3 * t + jp // 2)
                    for b in range(NB):
                        ins = nc.tensor.matmul(ps(jp)[:, b, :], gates_w[:, n, :], blk(xc[:, :])[:, b, :],
                                               start=True, stop=True)
                    ins.then_inc(mm_done, 1)

            def down_unit(l, g, i):
                s = i % 2
                pe.wait_ge(w_ready, l * UNITS + U_MLP + 8 * g + 4 + i + 3)
                for m, ks in ((0, (0, 1, 2)), (1, (0, 1, 2)), (0, (3,)), (1, (3,))):
                    jp = j_down(0, 2 * i + m)
                    if ks[0] == 0:
                        pe.wait_ge(ps_free[jp % 2], FIRST + l * SET_JOBS[jp % 2] + 6 * g + jp // 2)
                    for k in ks:
                        if i == 0 and m == 0:
                            pe.wait_ge(a_hi, l * F_TILES + GT * g + k + 1)
                            pe.wait_ge(a_lo, FIRST + l * F_TILES + GT * g + k + 1)
                        ins = product(ps(jp), wslot(s, m * 4 + k), (act_hi[:, k, :], act_lo[:, k, :]),
                                      k == 0, k == GT - 1)
                    if ks[0] == 3:
                        ins.then_inc(mm_done, 1)

            def last_down_unit(l, g):
                pe.wait_ge(w_ready, (l + 1) * UNITS + 2)
                j = j_down(g, KT - 2)
                for m in range(2):
                    take_set(l, j + m)
                    if m == 0:
                        for k in range(GT):
                            ins = product(ps(j), wslot(1, k), (act_hi[:, k, :], act_lo[:, k, :]), k == 0, k == GT - 1)
                        ins.then_inc(mm_done, 1)
                    else:
                        by_blocks(l, j + 1, 1, range(GT, 2 * GT), [(act_hi[:, k, :], act_lo[:, k, :]) for k in range(GT)])

            def gla(l, xbase):
                def chunk(c):
                    return slice(c * C, (c + 1) * C)

                def key_transposes(c, d, bank, signal):
                    for j in range(2):
                        ins = nc.tensor.transpose(banks[0:C, bank, j * 128:(j + 1) * 128],
                                                  ki[:, 2 * d + j, chunk(c)], ident[:, :])
                    ins.then_inc(signal, 1)

                def key_values(c, kt, bank, signal):
                    for h in range(HEADS):
                        j, r = h // 2, 64 * (h % 2)
                        ins = nc.tensor.matmul(banks[r:r + DK, bank, j * DV:(j + 1) * DV], kt[0:C, j, r:r + DK],
                                               v_tok[0:C, c, h * DV:(h + 1) * DV], start=True, stop=True)
                    ins.then_inc(signal, 1)

                for j in (J_V + 2, J_V + 3):
                    pe.wait_ge(ps_free[j % 2], FIRST + freed(l, j))

                def to_rows(n):
                    c = NC - 1 - n
                    if n >= 2:
                        pe.wait_ge(vtok_ready, l * NC + n - 1)
                    for h in range(HEADS):
                        ins = nc.tensor.transpose(banks[0:C, n % 2, h * DV:(h + 1) * DV], vT[:, h, chunk(c)], ident[:, :])
                    ins.then_inc(g_vt, 1)
                    if n < NC - 1:
                        if n >= 2:
                            pe.wait_ge(ktb_ready, l * (NC - 1) + n - 1)
                        key_transposes(c, 1, 2 + n % 2, g_ktb)

                to_rows(0)
                for n in range(NC):
                    if n + 1 < NC:
                        to_rows(n + 1)
                    if n < NC - 1:
                        pe.wait_ge(vtok_ready, l * NC + n + 1)
                        pe.wait_ge(ktb_ready, l * (NC - 1) + n + 1)
                        if n >= 2:
                            pe.wait_ge(stb_sum, l * (NC - 1) + n - 1)
                        key_values(NC - 1 - n, kt_b[:, n % 2], 4 + n % 2, g_kvb)
                pe.wait_ge(vtok_ready, (l + 1) * NC)
                pe.wait_ge(ktb_ready, (l + 1) * (NC - 1))
                pe.wait_ge(stb_ready, (l + 1) * (NC - 1))

                def keys_in_rows(c):
                    if c >= 1:
                        pe.wait_ge(ktf_ready, l * (NC - 1) + c)
                    key_transposes(c, 0, 0, g_ktf)

                def scores(c):
                    if c >= 1:
                        pe.wait_ge(p_ready, l * NC + c)
                    for d in range(2):
                        for j in range(2):
                            for r in range(2):
                                rows = slice(64 * r, 64 * r + DK)
                                ins = nc.tensor.matmul(banks[0:C, 2 + r, (2 * d + j) * C:(2 * d + j + 1) * C],
                                                       ki[rows, 2 * d + j, chunk(c)], qi[rows, 2 * d + j, chunk(c)],
                                                       start=True, stop=True)
                    ins.then_inc(g_s, 1)

                def squares(c):
                    pe.wait_ge(osq_ready, l * NC + c + 1)
                    if c >= 1:
                        pe.wait_ge(ss_log, l * NC + c)
                    nc.tensor.matmul(banks[:, 6, 0:HEADS * C], ones[:, :], o_sq[:, c % 2, :], start=True, stop=True)\
                        .then_inc(g_ss, 1)

                keys_in_rows(0)
                scores(0)
                for c in range(NC):
                    if c + 1 < NC - 1:
                        keys_in_rows(c + 1)
                    if c < NC - 1:
                        pe.wait_ge(ktf_ready, l * (NC - 1) + c + 1)
                        if c >= 1:
                            pe.wait_ge(stf_sum, l * (NC - 1) + c)
                        key_values(c, kt_f[:, c % 2], 1, g_kvf)
                    if c + 1 < NC:
                        scores(c + 1)
                    pe.wait_ge(p_ready, l * NC + c + 1)
                    if c >= 1:
                        pe.wait_ge(stf_ready, l * (NC - 1) + c)
                        pe.wait_ge(o_gated, l * NC + c)
                    for j in range(2):
                        for r in range(2):
                            h, rows = 2 * j + r, slice(64 * r, 64 * r + DK)
                            terms = [(v_tok[0:C, c, h * DV:(h + 1) * DV], p_t[0:C, c % 2, r, j * C:(j + 1) * C])]
                            if c > 0:
                                terms.append((st_f[rows, c % 2, j, :], qi[rows, j, chunk(c)]))
                            if c < NC - 1:
                                terms.append((st_b[rows, c, j, :], qi[rows, 2 + j, chunk(c)]))
                            for n, (a, b) in enumerate(terms):
                                ins = nc.tensor.matmul(banks[:, 4 + r, j * C:(j + 1) * C], a, b,
                                                       start=n == 0, stop=n == len(terms) - 1)
                    ins.then_inc(g_o, 1)
                    if c >= 1:
                        squares(c - 1)

                def half(s, ks):
                    for k in ks:
                        ins = product(ps(J_O + s), wslot(1 - s, k), xtile(k), k == 0, k == KT - 1)
                    return ins

                pe.wait_ge(w_ready, l * UNITS + U_OUT + 1 + 3)
                for s in (1, 0):
                    take_set(l, J_O + s)
                    if s == 1:
                        pe.wait_ge(x_lo, xbase + NX + LT)
                    else:
                        squares(NC - 1)
                        pe.wait_ge(o_gated, (l + 1) * NC)
                    half(s, range(LT))
                pe.wait_ge(x_hi, xbase + NX + LT + NC)
                pe.wait_ge(x_lo, xbase + NX + LT + NC)
                for s in range(2):
                    half(s, range(LT, KT)).then_inc(mm_done, 1)

            pe.wait_ge(const_ready, 1)
            with pe.Fori(0, L) as l:
                xbase = l * X_PER
                first_pair(l, PRE_MIX, 0, j_x(0), 0, xbase, l * 2 * NX)
                pe.wait_ge(zgw_ready, l + 1)
                take_set(l, J_ZG)
                for k in range(KT):
                    ins = product(ps(J_ZG, 2 * RANK), (zg_hl[:, 0, k, :], zg_hl[:, 1, k, :]), xtile(k), k == 0, k == KT - 1)
                ins.then_inc(mm_done, 1)
                lru_gates(l, 0)
                unit_job(l, 2, 1, j_x(1), 3)
                unit_job(l, 3, 0, j_gate(1), 4)
                lru_gates(l, 1)
                with pe.Fori(2, LT) as t:
                    unit_job(l, 2 * t, 1, 1, 3 * t)
                    unit_job(l, 2 * t + 1, 0, 2, 3 * t + 1)
                    lru_gates(l, t)
                unit_job(l, 8, 1, J_Q0, J_Q0 // 2)
                unit_job(l, 9, 0, J_Q1, J_Q1 // 2)
                pe.wait_ge(decayw_loaded, 16 * (l + 1))
                pe.wait_ge(ps_free[J_ZG % 2], FIRST + freed(l, J_ZG))
                for n in range(4):
                    take_set(l, J_W + n)
                    for b in range(NB):
                        ins = nc.tensor.matmul(ps(J_W + n)[:, b, :], decay_w[:, n * 128:(n + 1) * 128],
                                               blk(acc[0:2 * RANK, :])[:, b, :], start=True, stop=True)
                    ins.then_inc(mm_done, 1)
                with pe.Fori(0, 5) as i:
                    unit_job(l, 10 + 2 * i, 1, J_K, J_K // 2 + i)
                    unit_job(l, 11 + 2 * i, 0, J_K + 1, (J_K + 1) // 2 + i)
                gla(l, xbase)
                with pe.Fori(1, 3) as i:
                    unit_job(l, U_OUT + 2 * i, 1, J_O, J_O // 2 + i)
                    unit_job(l, U_OUT + 2 * i + 1, 0, J_O + 1, (J_O + 1) // 2 + i)
                unit_job(l, U_OUT + 6, 1, J_O + 6, (J_O + 6) // 2)
                pe.wait_ge(w_ready, l * UNITS + U_OUT + 7 + 3)
                take_set(l, J_O + 7)
                by_blocks(l, J_O + 7, 0, range(KT), [xtile(k) for k in range(KT)])
                row_sums(l, POST_MIX, l * 18 + 6)
                first_pair(l, PRE_MLP, U_MLP, J_MLP, 1, xbase + NX + LT + NC, l * 2 * NX + NX)
                unit_job(l, U_MLP + 2, 0, J_MLP + 2, (J_MLP + 2) // 2)
                unit_job(l, U_MLP + 3, 1, J_MLP + 3, (J_MLP + 3) // 2)
                for i in range(4):
                    down_unit(l, 0, i)
                with pe.Fori(1, GROUPS - 1) as g:
                    for i in range(GT):
                        unit_job(l, U_MLP + 8 * g + i, i % 2, J_MLP + i, (J_MLP + i) // 2 + 6 * g)
                    for i in range(4):
                        down_unit(l, g, i)
                g = GROUPS - 1
                for i in range(GT):
                    unit_job(l, U_MLP + 8 * g + i, i % 2, j_up(g, i), j_up(g, i) // 2)
                for i in range(3):
                    down_unit(l, g, i)
                last_down_unit(l, g)
                row_sums(l, POST_MLP, l * 18 + 15)
            for n in range(NX):
                add_piece(L, PRE_MIX, n, L * 2 * NX)

        @block.scalar
        def _(act):
            def log_mean(l, norm, b):
                act.wait_ge(sum_done, l * SUMS + norm * NB + b + 1)
                nc.scalar.activation(rs[:, cols(b)], sum_bank(norm, b), ACT.Ln, scale=1.0 / D, bias=eps[:, 0:1])\
                    .then_inc(sum_read, 1)

            def inv_root(l, norm, b):
                act.wait_ge(sum_read, l * SUMS + norm * NB + b + 3)
                nc.scalar.activation(rs[:, cols(b)], rs[:, cols(b)], ACT.Exp, scale=-0.5).then_inc(rs_ready, 1)

            def split_hi_and_square(n, read):
                m, b = piece(n)
                nc.scalar.activation(X[:, m:m + 2, 0, cols(b)], Y[:, m:m + 2, cols(b)], ACT.Copy).then_inc(x_hi, 1)
                if n >= SQ_RING:
                    act.wait_ge(sq_read, read + squares_read(n))
                nc.scalar.activation(sq[:, n % SQ_RING], Y[:, m:m + 2, cols(b)], ACT.Square).then_inc(sq_h, 1)

            def sums_between(l, norm, n):
                if n == QT:
                    log_mean(l, norm, 0)
                if n == 2 * QT:
                    log_mean(l, norm, 1)
                    inv_root(l, norm, 0)
                    inv_root(l, norm, 1)

            def last_sum(l, norm):
                log_mean(l, norm, NB - 1)
                inv_root(l, norm, NB - 1)

            def stream(dram, n):
                m, b = piece(n)
                return dram[m:m + 2, :, cols(b)].rearrange("k p n -> p k n")

            def load_old(n, source):
                act.dma_start(h_old[:, n % 3], stream(source, n)).then_inc(hold_loaded[n % 3], 16)

            def square_out(l, m, j, phase):
                if m < KT - 1:
                    act.wait_ge(ps_free[j % 2], FIRST + l * SET_JOBS[j % 2] + j // 2 + 1)
                    if m >= 3:
                        act.wait_ge(acc_done, l * 18 + phase * 9 + m - 2)
                    out = acc if m == 0 else T[2 + m % 2]
                    nc.scalar.activation(out[:, :], Y[:, m, :], ACT.Square).then_inc(sq_y, 1)
                else:
                    for b in range(NB):
                        if b < NB - 1:
                            act.wait_ge(y_last, l * 4 + phase * 2 + b + 1)
                        else:
                            act.wait_ge(ps_free[j % 2], FIRST + l * SET_JOBS[j % 2] + j // 2 + 1)
                        nc.scalar.activation(T[0][:, cols(b)], Y[:, m, cols(b)], ACT.Square).then_inc(sq_y, 1)

            def update(l, phase, source, target):
                norm = POST_MIX + 2 * phase
                for b in range(NB):
                    log_mean(l, norm, b)
                for b in range(NB):
                    inv_root(l, norm, b)
                for n in range(NX):
                    m, b = piece(n)
                    act.wait_ge(y_new, (l * 2 + phase) * NX + n + 1)
                    if n + 3 < NX:
                        load_old(n + 3, source)
                    act.dma_start(stream(target, n), Y[:, m:m + 2, cols(b)]).then_inc(h_stored, 16)
                    split_hi_and_square(n, (l * 2 + phase + 1) * NB * (QT - 1))
                    sums_between(l, norm + 1, n)

            for n in range(2 * NB):
                tiles, c = slice(n % 2 * 4, n % 2 * 4 + 4), cols(n // 2)
                act.dma_start(Y[:, tiles, c], x_in[tiles, :, c].rearrange("k p n -> p k n")).then_inc(x_loaded[n], 16)
            act.wait_ge(const_ready, 1)
            act.wait_ge(par_loaded, 16)
            nc.scalar.activation(par[:, :, P_SP:P_SP + 8], par[:, :, P_LAM:P_LAM + 8], ACT.Abs).then_inc(par_step, 1)
            act.wait_ge(par_step, 1)
            nc.scalar.activation(par[:, :, P_SP:P_SP + 8], par[:, :, P_SP:P_SP + 8], ACT.Exp, scale=-1.0).then_inc(par_step, 1)
            for n in range(NX):
                if n % 2 == 0:
                    act.wait_ge(x_loaded[n // 2], 16)
                    tiles, c = slice(n % QT * 2, n % QT * 2 + 4), cols(n // QT)
                    act.dma_start(h_out[0, tiles, :, c].rearrange("k p n -> p k n"), Y[:, tiles, c]).then_inc(h_stored, 16)
                split_hi_and_square(n, 0)
                sums_between(0, PRE_MIX, n)
            act.wait_ge(par_ready, 1)
            with act.Fori(0, L) as l:
                xbase = l * X_PER + NX
                last_sum(l, PRE_MIX)
                with act.Fori(0, LT) as t:
                    for n, (out, bias) in enumerate(((lr[:, 0], P_BAF), (li[:, 0], P_BXF), (lr[:, 1], P_BAB), (li[:, 1], P_BXB))):
                        jp = 3 + n
                        act.wait_ge(mm_done, FIRST + l * NJ + 6 * t + jp + 1)
                        if n == 1:
                            act.wait_ge(lru_h, FIRST + (l * LT + t) * 2)
                        nc.scalar.activation(blk(out), ps(jp), ACT.Sigmoid, bias=par[:, l, bass.ds(bias + t, 1)])\
                            .then_inc(ps_free[jp % 2], 1)
                    for d in range(2):
                        act.wait_ge(ps_free[1], FIRST + l * SET_JOBS[1] + 3 * t + d + 2)
                        nc.scalar.activation(lt_[:, d, 0:NT], lr[:, d, 0:NT], ACT.Tanh,
                                             scale=par[:, l, bass.ds(P_SP + 4 * d + t, 1)]).then_inc(lru_tanh, 1)
                    for d in range(2):
                        nc.scalar.activation(la[:, d, 0:NT], lr[:, d, 0:NT], ACT.Exp,
                                             scale=par[:, l, bass.ds(P_NSP + 4 * d + t, 1)]).then_inc(lru_a, 1)
                    for d in range(2):
                        act.wait_ge(lru_a, (l * LT + t) * 2 + d + 1)
                        nc.scalar.activation(lr[:, d, 0:NT], la[:, d, 0:NT], ACT.Square).then_inc(lru_a2, 1)
                    act.wait_ge(ps_free[0], FIRST + l * SET_JOBS[0] + 3 * t + 2)
                    nc.scalar.activation(gg[:, t, 0:NT], gg[:, t, 0:NT], ACT.Gelu_apprx_tanh).then_inc(gelu_done, 1)
                    for d in range(2):
                        act.wait_ge(lru_v, (l * LT + t) * 2 + d + 1)
                        nc.scalar.activation(lt_[:, d, 0:NT], lt_[:, d, 0:NT], ACT.Sqrt).then_inc(lru_root, 1)
                for n in range(4):
                    ab = T[2 + n % 2]
                    act.wait_ge(mm_done, FIRST + done(l, J_W + n))
                    if n >= 2:
                        act.wait_ge(d_ready, l * 4 + n - 1)
                    nc.scalar.activation(blk(ab[:, :]), ps(J_W + n), ACT.Abs, bias=par[:, l, P_BG + n:P_BG + n + 1])\
                        .then_inc(softplus_step, 1)
                    act.wait_ge(softplus_step, l * 12 + 3 * n + 1)
                    nc.scalar.activation(ab[:, 0:NT], ab[:, 0:NT], ACT.Exp, scale=-1.0).then_inc(softplus_step, 1)
                    act.wait_ge(softplus_step, l * 12 + 3 * n + 2)
                    nc.scalar.activation(ab[:, 0:NT], ab[:, 0:NT], ACT.Ln, bias=1.0).then_inc(softplus_step, 1)
                for e in range(4):
                    j = e % 2
                    for d in range(2):
                        if e == 0:
                            act.wait_ge(d_ready, l * 4 + 2 * d + 2)
                        else:
                            act.wait_ge(qk_made, l * 8 + 2 * (e - 1) + d + 1)
                        nc.scalar.activation(ee[:, d, 0:NT], dd[:, 2 * d + j, 0:NT], ACT.Exp,
                                             scale=(1.0 if e < 2 else -1.0) / GATE_NORM).then_inc(e_ready, 1)
                act.wait_ge(fac_in, 2 * l + 2)
                nc.scalar.activation(fac[:, :, :], fac[:, :, :], ACT.Exp, scale=1.0 / GATE_NORM).then_inc(fac_ready, 1)
                for h in range(HEADS):
                    act.wait_ge(ps_free[(J_SG + h) % 2], FIRST + freed(l, J_SG + h))
                    nc.scalar.activation(sg[:, h, 0:NT], sg[:, h, 0:NT], ACT.Silu).then_inc(silu_done, 1)
                act.wait_ge(mm_done, FIRST + done(l, J_V + 3))
                for t in range(LT):
                    nc.scalar.activation(X[:, t, 0, 0:NT], y_lru[:, t, 0:NT], ACT.Copy).then_inc(x_hi, 1)
                act.wait_ge(x_lo, xbase + LT)
                for n in range(NC):
                    act.wait_ge(g_vt, l * NC + n + 1)
                    nc.scalar.activation(v_tok[0:C, NC - 1 - n, :], banks[0:C, n % 2, :], ACT.Copy).then_inc(vtok_ready, 1)
                act.wait_ge(stb_ready, (l + 1) * (NC - 1))

                def before_scores(c):
                    if c < NC - 1:
                        act.wait_ge(g_ktf, l * (NC - 1) + c + 1)
                        if c >= 2:
                            act.wait_ge(g_kvf, l * (NC - 1) + c - 1)
                        nc.scalar.activation(kt_f[0:C, c % 2].rearrange("p j n -> p (j n)"), banks[0:C, 0, 0:256], ACT.Copy)\
                            .then_inc(ktf_ready, 1)
                    act.wait_ge(g_s, l * NC + c + 1)
                    if c >= 2:
                        act.wait_ge(g_o, l * NC + c - 1)
                    nc.scalar.activation(p_t[0:C, c % 2], banks[0:C, 2:4, 0:2 * C], ACT.Copy)\
                        .then_inc(p_fwd, 1)

                def head_norm(c):
                    act.wait_ge(g_ss, l * NC + c + 1)
                    flat = o_rs[:, c % 2, :]
                    if c >= 2:
                        act.wait_ge(oy_ready, l * NC + c - 1)
                    nc.scalar.activation(flat, banks[:, 6, 0:HEADS * C], ACT.Ln, scale=1.0 / DV, bias=eps[:, 0:1])\
                        .then_inc(ss_log, 1)
                    act.wait_ge(ss_log, l * NC + c + 1)
                    nc.scalar.activation(flat, flat, ACT.Exp, scale=-0.5).then_inc(ors_ready, 1)
                    act.wait_ge(oy_ready, l * NC + c + 1)
                    nc.scalar.activation(by_parity(X[:, 4:8, 0, c * C:(c + 1) * C]), heads(o_y[:, c % 2, :]), ACT.Copy).then_inc(x_hi, 1)

                before_scores(0)
                for c in range(NC):
                    if c + 1 < NC:
                        before_scores(c + 1)
                    act.wait_ge(g_o, l * NC + c + 1)
                    if c >= 2:
                        act.wait_ge(g_ss, l * NC + c - 1)
                    nc.scalar.activation(o_sq[:, c % 2, :].rearrange("p (r n) -> p r n", r=2), banks[:, 4:6, 0:2 * C], ACT.Square)\
                        .then_inc(osq_ready, 1)
                    if c >= 1:
                        head_norm(c - 1)
                head_norm(NC - 1)
                act.wait_ge(x_lo, xbase + LT + NC)
                act.wait_ge(h_stored, 16 * (2 * NX * l + H_FIRST))
                for n in range(3):
                    load_old(n, h_out[l])
                for m in range(KT):
                    square_out(l, m, J_O + m, 0)
                update(l, 0, h_out[l], h_mid[l])
                last_sum(l, PRE_MLP)

                def hidden(g, i):
                    jp = J_MLP + i
                    act.wait_ge(ps_free[jp % 2], FIRST + l * SET_JOBS[jp % 2] + 6 * g + jp // 2 + 1)
                    if i >= 2:
                        act.wait_ge(a_lo, FIRST + l * F_TILES + g * GT + i - 1)
                    else:
                        act.wait_ge(a_lo, FIRST + l * F_TILES + g * GT)
                    nc.scalar.activation(T[2 + i % 2][:, :], T[i % 2][:, :], ACT.Square).then_inc(act_sq, 1)
                    act.wait_ge(act_sq, l * F_TILES + g * GT + i + 1)
                    nc.scalar.activation(act_hi[:, i, :], T[2 + i % 2][:, :], ACT.Copy).then_inc(a_hi, 1)

                with act.Fori(0, GROUPS - 1) as g:
                    for i in range(GT):
                        hidden(g, i)
                act.wait_ge(h_stored, 16 * (2 * NX * l + H_FIRST + NX))
                for n in range(3):
                    load_old(n, h_mid[l])
                for i in range(GT):
                    hidden(GROUPS - 1, i)
                for m in range(KT):
                    if m < 2:
                        act.wait_ge(a_lo, FIRST + (l + 1) * F_TILES)
                    square_out(l, m, j_down(GROUPS - 1, m), 1)
                update(l, 1, h_mid[l], h_out[l + 1])
            act.wait_ge(h_stored, 16 * (2 * NX * L + H_FIRST))

        @block.vector
        def _(dve):
            V = nc.vector

            def add_pair(total, n):
                dve.wait_ge(sq_h, total + n + 1)
                V.tensor_tensor(sq[:, n % SQ_RING, 0, :], sq[:, n % SQ_RING, 0, :], sq[:, n % SQ_RING, 1, :], ALU.add)\
                    .then_inc(sq_pair, 1)

            def scaled_out(l, jp, jx, jd, out, rows=128, factor=None):
                dve.wait_ge(mm_done, FIRST + jd)
                if factor is None:
                    ins = V.tensor_tensor(out, ps(jp, rows), blk(rs[0:rows, :]), ALU.mult)
                else:
                    ins = V.scalar_tensor_tensor(out=out, in0=ps(jp, rows), scalar=factor, in1=blk(rs[0:rows, :]),
                                                 op0=ALU.mult, op1=ALU.mult)
                ins.then_inc(ps_free[jp % 2], 1)

            def add_square(l, phase, m, b=None):
                last = m == KT - 1
                c = cols(b) if last else slice(0, NP)
                dve.wait_ge(sq_y, l * 20 + phase * 10 + m + 1 + (b if last else 0))
                if m >= 2:
                    dve.wait_ge(acc_done, l * 18 + phase * 9 + m - 1)
                V.tensor_tensor(acc[:, c], acc[:, c], T[0][:, c] if last else T[2 + m % 2][:, :], ALU.add).then_inc(acc_done, 1)

            def projected(l, phase, j0, add):
                for m in range(KT):
                    j = j0 + m
                    for b in range(NB) if m == KT - 1 else (None,):
                        if b is None or b == NB - 1:
                            dve.wait_ge(mm_done, FIRST + done(l, j))
                        else:
                            dve.wait_ge(last_block, l * 4 + phase * 2 + b + 1)
                        if b is None:
                            y, out = blk(Y[:, m, :]), ps(j)
                        else:
                            y, out = Y[:, m, cols(b)], ps(j)[:, b, :]
                        ins = V.tensor_tensor(y, out, y, ALU.add) if add else V.tensor_copy(y, out)
                        ins.then_inc(y_last if b is not None and b < NB - 1 else ps_free[j % 2], 1)
                        if b is None and m >= 2:
                            add_square(l, phase, m - 1)
                        elif b == 0:
                            add_square(l, phase, KT - 2)
                        elif b is not None:
                            add_square(l, phase, KT - 1, b - 1)
                add_square(l, phase, KT - 1, NB - 1)

            def update(l, phase, gain):
                total = (l * 2 + phase) * NX
                for n in range(NX):
                    m, b = piece(n)
                    y = Y[:, m:m + 2, cols(b)]
                    if m == 0:
                        dve.wait_ge(rs_ready, l * SUMS + (POST_MIX + 2 * phase) * NB + b + 1)
                    V.tensor_tensor(y, y, rs[:, cols(b)].unsqueeze(1).to_broadcast([128, 2, BN]), ALU.mult)\
                        .then_inc(y_scaled, 1)
                    dve.wait_ge(y_scaled, total + n + 1)
                    dve.wait_ge(hold_loaded[n % 3], 16 * ((l * 2 + phase) * (NX // 3) + n // 3 + 1))
                    for k in range(2):
                        ins = V.scalar_tensor_tensor(out=y[:, k], in0=y[:, k], scalar=par[:, l, gain + m + k:gain + m + k + 1],
                                                     in1=h_old[:, n % 3, k, :], op0=ALU.mult, op1=ALU.add)
                    ins.then_inc(y_new, 1)
                    if n >= 1:
                        add_pair(total + NX, n - 1)
                add_pair(total + NX, NX - 1)

            lam, sp, nsp = (par[:, :, c:c + 8] for c in (P_LAM, P_SP, P_NSP))
            z2 = acc[:, 0:8 * L].rearrange("p (l n) -> p l n", l=L)
            series = acc[:, 64:64 + 8 * L].rearrange("p (l n) -> p l n", l=L)
            steps = [2]

            def step(ins):
                steps[0] += 1
                ins.then_inc(par_step, 1)
                dve.wait_ge(par_step, steps[0])

            dve.wait_ge(par_step, 2)
            step(V.tensor_scalar(nsp, sp, 2.0, None, ALU.add))
            step(V.reciprocal(nsp, nsp))
            step(V.tensor_tensor(sp, sp, nsp, ALU.mult))
            step(V.tensor_tensor(z2, sp, sp, ALU.mult))
            step(V.tensor_scalar(series, z2, 1.0 / 19, 1.0 / 17, ALU.mult, ALU.add))
            for n in (15, 13, 11, 9, 7, 5, 3, 1):
                step(V.tensor_tensor(series, series, z2, ALU.mult))
                step(V.tensor_scalar(series, series, 1.0 / n, None, ALU.add))
            step(V.scalar_tensor_tensor(out=sp, in0=sp, scalar=2 * LRU_C, in1=series, op0=ALU.mult, op1=ALU.mult))
            step(V.tensor_scalar(nsp, lam, -LRU_C, 0.0, ALU.mult, ALU.max))
            step(V.tensor_tensor(sp, sp, nsp, ALU.add))
            V.tensor_scalar(nsp, sp, -1.0, None, ALU.mult).then_inc(par_ready, 1)
            for n in range(NX):
                add_pair(0, n)

            with dve.Fori(0, L) as l:
                xbase = l * X_PER + NX

                def root_to_state(t):
                    for d in range(2):
                        n = (l * LT + t) * 2 + d
                        dve.wait_ge(lru_root, n + 1)
                        V.tensor_tensor(li[:, d, 0:NT], li[:, d, 0:NT], lt_[:, d, 0:NT], ALU.mult).then_inc(lru_u, 1)
                    dve.wait_ge(ylru_done, FIRST + l * LT + t)
                    for d in range(2):
                        n = (l * LT + t) * 2 + d
                        dve.wait_ge(lru_u, n + 1)
                        a, u, h = la[:, d, 0:NT], li[:, d, 0:NT], hh[d][:, 0:NT]
                        if d == 1:
                            a, u, h = a[:, ::-1], u[:, ::-1], h[:, ::-1]
                        V.tensor_tensor_scan(h, a, u, 0.0, ALU.mult, ALU.add).then_inc(lru_h, 1)

                def lru_result(t):
                    dve.wait_ge(lru_h, FIRST + (l * LT + t) * 2 + 2)
                    V.tensor_tensor(hh[0][:, 0:NT], hh[0][:, 0:NT], hh[1][:, 0:NT], ALU.add).then_inc(lru_sum, 1)
                    dve.wait_ge(lru_sum, l * LT + t + 1)
                    dve.wait_ge(gelu_done, l * LT + t + 1)
                    V.tensor_tensor(y_lru[:, t, 0:NT], hh[0][:, 0:NT], gg[:, t, 0:NT], ALU.mult).then_inc(ylru_done, 1)

                def branch_in(t, first=False):
                    jp = 0 if first else 1
                    scaled_out(l, jp, 0, l * NJ + 6 * t + jp + 1, blk(xb[:, 2:2 + NP]))
                    dve.wait_ge(ps_free[jp], FIRST + l * SET_JOBS[jp] + 3 * t + 1)

                def conv(t):
                    base = (l * LT + t) * 3

                    def tap(n):
                        return par[:, l, bass.ds(P_CONVW + 4 * t + n, 1)]
                    V.tensor_scalar(xc[:, :], xb[:, 0:NP], tap(0), par[:, l, bass.ds(P_CONVB + t, 1)], ALU.mult, ALU.add)\
                        .then_inc(conv_step, 1)
                    for n in range(1, 4):
                        dve.wait_ge(conv_step, base + n)
                        V.scalar_tensor_tensor(out=xc[:, :], in0=xb[:, n:n + NP], scalar=tap(n), in1=xc[:, :],
                                               op0=ALU.mult, op1=ALU.add).then_inc(conv_step if n < 3 else xc_ready, 1)

                def gate_in(t, first=False):
                    jp = 1 if first else 2
                    scaled_out(l, jp, 0, l * NJ + 6 * t + jp + 1, blk(gg[:, t, :]))

                def input_and_decay(t):
                    dve.wait_ge(xc_ready, l * LT + t + 1)
                    for d in range(2):
                        dve.wait_ge(ps_free[0], FIRST + l * SET_JOBS[0] + 3 * t + 3 + d)
                        V.tensor_tensor(li[:, d, 0:NT], li[:, d, 0:NT], xc[:, 0:NT], ALU.mult).then_inc(lru_ix, 1)
                    for d in range(2):
                        n = (l * LT + t) * 2 + d
                        dve.wait_ge(lru_a2, n + 1)
                        dve.wait_ge(lru_tanh, n + 1)
                        V.scalar_tensor_tensor(out=lt_[:, d, 0:NT], in0=lr[:, d, 0:NT], scalar=1.0, in1=lt_[:, d, 0:NT],
                                               op0=ALU.add, op1=ALU.mult).then_inc(lru_v, 1)

                dve.wait_ge(h_stored, 16 * (2 * NX * l + H_FIRST))
                dve.wait_ge(rs_ready, l * SUMS + (PRE_MIX + 1) * NB)
                dve.wait_ge(mm_done, FIRST + done(l, j_x(0)))
                V.memset(xb[:, 0:2], 0.0).then_inc(pad_zeroed, 1)
                V.memset(xb[:, 2 + NP:4 + NP], 0.0).then_inc(pad_zeroed, 1)
                dve.wait_ge(pad_zeroed, 2 * l + 2)
                branch_in(0, True)
                conv(0)
                gate_in(0, True)
                scaled_out(l, J_ZG, 0, done(l, J_ZG), blk(acc[0:2 * RANK, :]), rows=2 * RANK)
                input_and_decay(0)
                with dve.Fori(1, LT) as t:
                    branch_in(t)
                    dve.wait_ge(mm_done, FIRST + l * NJ + 6 * t + 1)
                    dve.wait_ge(lru_ix, (l * LT + t) * 2)
                    conv(t)
                    root_to_state(t - 1)
                    gate_in(t)
                    lru_result(t - 1)
                    input_and_decay(t)
                scaled_out(l, J_Q0, 0, done(l, J_Q0), blk(T[1][:, :]), factor=DK ** -0.5)
                root_to_state(LT - 1)
                dve.wait_ge(lru_v, (l + 1) * LT * 2)
                scaled_out(l, J_Q1, 0, done(l, J_Q1), blk(q1[:, :]), factor=DK ** -0.5)
                lru_result(LT - 1)

                for n in range(4):
                    log_term, d_n = T[2 + n % 2][:, 0:NT], dd[:, n, 0:NT]
                    dve.wait_ge(softplus_step, l * 12 + 3 * n + 1)
                    V.tensor_scalar(blk(dd[:, n, :]), ps(J_W + n), par[:, l, P_BG + n:P_BG + n + 1], 0.0, ALU.add, ALU.min)\
                        .then_inc(ps_free[(J_W + n) % 2], 1)
                    dve.wait_ge(softplus_step, l * 12 + 3 * n + 3)
                    dve.wait_ge(ps_free[(J_W + n) % 2], FIRST + freed(l, J_W + n))
                    V.tensor_tensor(d_n, d_n, log_term, ALU.subtract).then_inc(decay_step, 1)
                    dve.wait_ge(decay_step, l * 8 + 2 * n + 1)
                    if n < 2:
                        V.tensor_tensor_scan(log_term, reset[:, 0:NT], d_n, 0.0, ALU.mult, ALU.add).then_inc(decay_step, 1)
                    else:
                        V.tensor_tensor_scan(log_term[:, ::-1], reset[:, 1:NT + 1][:, ::-1], d_n[:, ::-1], 0.0, ALU.mult, ALU.add)\
                            .then_inc(decay_step, 1)
                    dve.wait_ge(decay_step, l * 8 + 2 * n + 2)
                    by_chunk = log_term.rearrange("p (c t) -> p c t", t=C)
                    end = C - 1 if n < 2 else 0
                    V.tensor_copy(b_mid[:, n, :], by_chunk[:, :, MID]).then_inc(fac_step, 1)
                    V.tensor_copy(b_tot[:, n, :], by_chunk[:, :, end]).then_inc(fac_step, 1)
                    dve.wait_ge(fac_step, l * 9 + 2 * n + 2)
                    V.tensor_tensor(d_n.rearrange("p (c t) -> p c t", t=C), by_chunk,
                                    b_mid[:, n, :].unsqueeze(2).to_broadcast([128, NC, C]), ALU.subtract).then_inc(d_ready, 1)
                V.tensor_tensor(fac[:, :, :], b_tot[:, :, :], b_mid[:, :, :], ALU.subtract).then_inc(fac_step, 1)
                dve.wait_ge(fac_step, l * 9 + 9)
                V.tensor_tensor(fac[:, 0:2, 0:NC - 1], fac[:, 0:2, 0:NC - 1], b_mid[:, 0:2, 1:NC], ALU.add).then_inc(fac_in, 1)
                V.tensor_tensor(fac[:, 2:4, 1:NC], fac[:, 2:4, 1:NC], b_mid[:, 2:4, 0:NC - 1], ALU.add).then_inc(fac_in, 1)
                for e, j in enumerate((J_Q0, J_Q1, J_K, J_K + 1)):
                    plain = (T[1], q1)[e % 2]
                    if e >= 2:
                        dve.wait_ge(qk_made, l * 8 + 2 * e - 2)
                        scaled_out(l, j, 0, done(l, j), blk(plain[:, :]))
                    dve.wait_ge(ps_free[j % 2], FIRST + freed(l, j))
                    for d in range(2):
                        dve.wait_ge(e_ready, l * 8 + 2 * e + d + 1)
                        out = (qi if e < 2 else ki)[:, 2 * d + e % 2, 0:NT]
                        V.tensor_tensor(out, plain[:, 0:NT], ee[:, d, 0:NT], ALU.mult).then_inc(qk_made, 1)
                dve.wait_ge(qk_made, l * 8 + 8)
                for h in range(HEADS):
                    scaled_out(l, J_SG + h, 0, done(l, J_SG + h), blk(sg[:, h, :]))
                for h in range(HEADS):
                    scaled_out(l, J_V + h, 0, done(l, J_V + h), blk(vT[:, h, :]))
                for t in range(LT):
                    dve.wait_ge(x_hi, xbase + t + 1)
                    V.tensor_tensor(X[:, t, 1, 0:NT], y_lru[:, t, 0:NT], X[:, t, 0, 0:NT].bitcast(f32), ALU.subtract)\
                        .then_inc(x_lo, 1)
                dve.wait_ge(fac_ready, l + 1)
                for n in range(NC - 1):
                    c = NC - 1 - n
                    dve.wait_ge(g_ktb, l * (NC - 1) + n + 1)
                    if n >= 2:
                        dve.wait_ge(g_kvb, l * (NC - 1) + n - 1)
                    V.tensor_copy(kt_b[0:C, n % 2].rearrange("p j n -> p (j n)"), banks[0:C, 2 + n % 2, 0:256])\
                        .then_inc(ktb_ready, 1)
                    dve.wait_ge(g_kvb, l * (NC - 1) + n + 1)
                    kv = banks[:, 4 + n % 2, 0:2 * DV].rearrange("p (j v) -> p j v", j=2)
                    if n == 0:
                        V.tensor_copy(kv_b[:, :, :], kv).then_inc(stb_sum, 1)
                    else:
                        dve.wait_ge(stb_ready, l * (NC - 1) + n)
                        V.tensor_tensor(kv_b[:, :, :], kv, st_b[:, c, :, :], ALU.add).then_inc(stb_sum, 1)
                    dve.wait_ge(stb_sum, l * (NC - 1) + n + 1)
                    V.tensor_tensor(st_b[:, c - 1, :, :], kv_b[:, :, :],
                                    fac[:, 2:4, c:c + 1].to_broadcast([128, 2, DV]), ALU.mult).then_inc(stb_ready, 1)
                dve.wait_ge(silu_done, (l + 1) * HEADS)

                def select(c):
                    dve.wait_ge(g_s, l * NC + c + 1)
                    dve.wait_ge(p_fwd, l * NC + c + 1)
                    dve.sem_inc(waited_dve, 1)
                    V.copy_predicated(p_t[0:C, c % 2], later[:, :, :].rearrange("p (r j) c -> p r (j c)", r=2),
                                      banks[0:C, 2:4, 2 * C:4 * C]).then_inc(p_ready, 1)

                def finish(c):
                    dve.wait_ge(ors_ready, l * NC + c + 1)
                    dve.wait_ge(o_gated, l * NC + c + 1)
                    V.tensor_tensor(o_y[:, c % 2, :], o_y[:, c % 2, :], o_rs[:, c % 2, :], ALU.mult).then_inc(oy_ready, 1)
                    dve.wait_ge(x_hi, xbase + LT + c + 1)
                    dve.wait_ge(oy_ready, l * NC + c + 1)
                    cols = slice(c * C, (c + 1) * C)
                    V.tensor_tensor(by_parity(X[:, 4:8, 1, cols]), heads(o_y[:, c % 2, :]),
                                    by_parity(X[:, 4:8, 0, cols].bitcast(f32)), ALU.subtract)\
                        .then_inc(x_lo, 1)

                select(0)
                for c in range(NC):
                    if c + 1 < NC:
                        select(c + 1)
                    if c < NC - 1:
                        dve.wait_ge(g_kvf, l * (NC - 1) + c + 1)
                        kv = banks[:, 1, 0:2 * DV].rearrange("p (j v) -> p j v", j=2)
                        if c == 0:
                            V.tensor_copy(kv_f[:, :, :], kv).then_inc(stf_sum, 1)
                        else:
                            dve.wait_ge(stf_ready, l * (NC - 1) + c)
                            V.tensor_tensor(kv_f[:, :, :], kv, st_f[:, c % 2], ALU.add).then_inc(stf_sum, 1)
                            dve.wait_ge(g_o, l * NC + c)
                        dve.wait_ge(stf_sum, l * (NC - 1) + c + 1)
                        V.tensor_tensor(st_f[:, (c + 1) % 2], kv_f[:, :, :],
                                        fac[:, 0:2, c:c + 1].to_broadcast([128, 2, DV]), ALU.mult).then_inc(stf_ready, 1)
                    dve.wait_ge(osq_ready, l * NC + c + 1)
                    if c >= 2:
                        dve.wait_ge(x_lo, xbase + LT + c - 1)
                    V.tensor_tensor(heads(o_y[:, c % 2, :]),
                                    banks[:, 4:6, 0:2 * C].rearrange("p r (j c) -> p r j c", j=2),
                                    by_parity(sg[:, :, c * C:(c + 1) * C]), ALU.mult).then_inc(o_gated, 1)
                    if c >= 1:
                        finish(c - 1)
                finish(NC - 1)

                projected(l, 0, J_O, False)
                update(l, 0, P_GMIXPOST)

                def group(g, jd):
                    def relu(i):
                        jp = J_MLP + i
                        dve.wait_ge(mm_done, FIRST + jd + i + 1)
                        if i >= 2:
                            dve.wait_ge(act_sq, l * F_TILES + g * GT + i - 1)
                        V.scalar_tensor_tensor(out=blk(T[i % 2][:, :]), in0=ps(jp), scalar=0.0, in1=blk(rs[:, :]),
                                               op0=ALU.max, op1=ALU.mult).then_inc(ps_free[jp % 2], 1)

                    def hidden_lo(i):
                        dve.wait_ge(a_hi, l * F_TILES + g * GT + i + 1)
                        V.tensor_tensor(act_lo[:, i, :], T[2 + i % 2][:, :], act_hi[:, i, :].bitcast(f32), ALU.subtract)\
                            .then_inc(a_lo, 1)

                    for i in range(GT):
                        relu(i)
                        if i >= 1:
                            hidden_lo(i - 1)
                    hidden_lo(GT - 1)

                def down_sum(m, jd, first):
                    jp = J_MLP + GT + m
                    dve.wait_ge(mm_done, FIRST + jd + GT + m + 1)
                    if first:
                        ins = V.tensor_copy(blk(Y[:, m, :]), ps(jp))
                    else:
                        ins = V.tensor_tensor(blk(Y[:, m, :]), ps(jp), blk(Y[:, m, :]), ALU.add)
                    ins.then_inc(ps_free[jp % 2], 1)

                dve.wait_ge(rs_ready, l * SUMS + (PRE_MLP + 1) * NB)
                group(0, l * NJ + J_MLP)
                dve.wait_ge(h_stored, 16 * (2 * NX * l + H_FIRST + NX))
                for m in range(KT):
                    down_sum(m, l * NJ + J_MLP, True)
                with dve.Fori(1, GROUPS - 1) as g:
                    group(g, l * NJ + J_MLP + 12 * g)
                    for m in range(KT):
                        down_sum(m, l * NJ + J_MLP + 12 * g, False)
                group(GROUPS - 1, l * NJ + j_up(GROUPS - 1, 0))
                projected(l, 1, j_down(GROUPS - 1, 0), True)
                update(l, 1, P_GMLPPOST)


def kernel(**inputs):
    import numpy as np
    import concourse.bacc as bacc
    from concourse.bass_utils import run_bass_kernel_spmd

    a = {k: np.asarray(v) for k, v in inputs.items()}

    tokens = np.concatenate([a["meta_tokens"], a["x"][0]], axis=0)
    x_in = np.zeros((KT, 128, NP), np.float32)
    x_in[:, :, :NT] = tokens.T.reshape(KT, 128, NT)

    def out_tile(w, c):
        return w[:, c:c + 128].reshape(KT, 128, 128).transpose(1, 0, 2)

    q0, k0, v0, g0, z0 = 2 * LW, 2 * LW + 256, 2 * LW + 512, 2 * LW + 1024, 2 * LW + 1536
    w_units = np.empty((L, UNITS, 128, 8, 128), np.float32)
    w_gates = np.zeros((L, LT, 128, 4, 128), np.float32)
    w_decay = np.zeros((L, 2 * RANK, 512), np.float32)
    w_zg = np.empty((L, 128, KT, 2 * RANK), np.float32)
    params = np.empty((128, L, N_LOADED), np.float32)
    for l in range(L):
        win, wout, up, down = a["w_in"][l], a["w_out"][l], a["w_mlp_up"][l], a["w_mlp_down"][l]
        columns = [c for t in range(LT) for c in (128 * t, LW + 128 * t)]
        columns += [q0, q0 + 128, k0, k0 + 128] + [g0 + 128 * h for h in range(4)] + [v0 + 128 * h for h in range(4)]
        for u, c in enumerate(columns):
            w_units[l, u] = out_tile(win, c)
        for m in range(KT):
            w_units[l, U_OUT + m] = out_tile(wout, 128 * m)
        for g in range(GROUPS):
            for i in range(GT):
                w_units[l, U_MLP + 8 * g + i] = out_tile(up, 128 * (GT * g + i))
                w_units[l, U_MLP + 8 * g + GT + i] = down[512 * g:512 * (g + 1), 256 * i:256 * (i + 1)]\
                    .reshape(4, 128, 2, 128).transpose(1, 2, 0, 3).reshape(128, 8, 128)
        w_zg[l] = win[:, z0:z0 + 2 * RANK].reshape(KT, 128, 2 * RANK).transpose(1, 0, 2)
        for n, name in enumerate(("lru_wa_f", "lru_wx_f", "lru_wa_b", "lru_wx_b")):
            for head in range(8):
                r = 64 * (head % 2)
                w_gates[l, head // 2, r:r + 64, n, r:r + 64] = a[name][l, head]
        w_decay[l, :RANK, 0:256] = a["gla_wg_f"][l]
        w_decay[l, RANK:, 256:512] = a["gla_wg_b"][l]

        def put(at, v):
            v = v.reshape(-1, 128).T
            params[:, l, at:at + v.shape[1]] = v
        for t in range(LT):
            params[:, l, P_CONVW + 4 * t:P_CONVW + 4 * t + 4] = a["conv_w"][l][:, 128 * t:128 * t + 128].T
        for at, name in ((P_CONVB, "conv_b"), (P_BAF, "lru_ba_f"), (P_BXF, "lru_bx_f"), (P_BAB, "lru_ba_b"),
                         (P_BXB, "lru_bx_b"), (P_LAM, "lru_lambda_f"), (P_LAM + 4, "lru_lambda_b"),
                         (P_BG, "gla_bg_f"), (P_BG + 2, "gla_bg_b"), (P_GMIX, "norm_mix_pre"),
                         (P_GMIXPOST, "norm_mix_post"), (P_GMLP, "norm_mlp_pre"), (P_GMLPPOST, "norm_mlp_post"),
                         (P_GOUT + 4, "gla_head_norm")):
            put(at, a[name][l])
        params[:, l, P_GOUT:P_GOUT + 4] = 1.0
        params[:, l, P_ONE:P_ONE + 8] = 1.0

    nc = bacc.Bacc("TRN2", target_bir_lowering=False, num_devices=1)
    arrays = {"x_in": x_in, "w_units": w_units, "w_zg": w_zg, "w_gates": w_gates, "w_decay": w_decay, "params": params}
    args = [nc.dram_tensor(n, v.shape, mybir.dt.float32, kind="ExternalInput").ap() for n, v in arrays.items()]
    h_out = nc.dram_tensor("h_out", (L + 1, KT, 128, NP), mybir.dt.float32, kind="ExternalOutput").ap()
    trunk_kernel(nc, *args, h_out)
    r = run_bass_kernel_spmd(nc, [arrays], core_ids=[0])
    h = np.asarray(r.results[0]["h_out"])[L]
    return np.ascontiguousarray(h.reshape(D, NP)[:, N_META:NT].T)[None]
```

```python
import concourse.bass as bass
from concourse import mybir
from contextlib import ExitStack

L = 2
D = 1024
N_META, SEQ = 16, 1024
NT = N_META + SEQ
NB, BN = 3, 348
NP = NB * BN
KT = D // 128
LW, LT = 512, 4
DK, DV, HEADS, RANK = 64, 128, 4, 16
C, NC = 104, NT // 104
MID = C // 2 - 1
F_TILES, GROUPS, GT = 32, 8, 4
EPS = 1e-6
GATE_NORM = 16.0
LRU_C = 8.0

U_OUT, U_MLP = 20, 28
UNITS = U_MLP + 8 * GROUPS
PAIRS = UNITS // 2

(P_CONVW, P_CONVB, P_BAF, P_BXF, P_BAB, P_BXB, P_LAM, P_BG, P_GMIX, P_GMIXPOST, P_GMLP, P_GMLPPOST,
 P_GOUT, P_ONE, P_SP, P_NSP, NPAR) = (0, 16, 20, 24, 28, 32, 36, 44, 48, 56, 64, 72, 80, 88, 96, 104, 112)
N_LOADED = P_SP



def j_x(t): return 6 * t + (t > 0)
def j_gate(t): return 6 * t + 1 + (t > 0)
def j_lru(t, n): return 6 * t + 3 + n


J_ZG, J_Q0, J_Q1, J_W, J_K, J_V, J_SG, J_O, J_MLP = 2, 25, 26, 27, 31, 33, 37, 41, 49
NJ = J_MLP + 12 * GROUPS
SET_JOBS = ((NJ + 1) // 2, NJ // 2)


def j_up(g, i): return J_MLP + 12 * g + i
def j_down(g, m): return J_MLP + 12 * g + GT + m


PRE_MIX, POST_MIX, PRE_MLP, POST_MLP, NEXT_PRE_MIX = range(5)
SUMS = 4 * NB
NX, QT = NB * KT // 2, KT // 2
SQ_RING = 3
H_FIRST = 2 * NB

FIRST = 3

X_PER = 4 + NC + 2 * NX


def squares_read(n):
    n -= SQ_RING
    n += n % QT == QT - 1
    return n + 1 - n // QT


def width(b):
    return min(BN, NT - b * BN)


def used(b):
    return slice(b * BN, b * BN + width(b))


def piece(n):
    return n % QT * 2, n // QT


def trunk_kernel(nc, x_in, w_units, w_zg, w_gates, w_decay, params, h_out):
    f32, f32r, bf16, u8 = mybir.dt.float32, mybir.dt.float32r, mybir.dt.bfloat16, mybir.dt.uint8
    ALU, ACT = mybir.AluOpType, mybir.ActivationFunctionType
    h_mid = nc.dram_tensor("h_mid", (L, KT, 128, NP), f32, kind="Internal").ap()

    ctx = ExitStack()
    with ctx:
        def sb(name, shape, dt=f32):
            return ctx.enter_context(nc.sbuf_tensor(name, shape, dt))

        def sem(name):
            return ctx.enter_context(nc.semaphore(name))

        X = sb("X", [128, KT, 2, NP], f32r)
        w_raw = sb("w_raw", [128, 2, 8, 128])
        w_hl = sb("w_hl", [128, 2, 2, 8, 128], f32r)
        par = sb("par", [128, L, NPAR])
        ones = sb("ones", [128, 128])
        ident = sb("ident", [128, 128])
        gates_raw = sb("gates_raw", [128, 4, 128])
        decay_w = sb("decay_w", [4 * RANK, 512])
        zg_raw = sb("zg_raw", [128, 8, 2 * RANK])
        zg_hl = sb("zg_hl", [128, 8, 2, 2 * RANK], f32r)
        reset = sb("reset", [128, NT + 1], bf16)
        later = sb("later", [C, HEADS, C], u8)
        eps = sb("eps", [128, 1])
        b_mid = sb("b_mid", [128, 4, NC])
        b_tot = sb("b_tot", [128, 4, NC])
        fac = sb("fac", [128, 4, NC])
        TB = NP * 4
        base = (nc.sbuf_base + 31) // 32 * 32

        def at(name, shape, tile, dt=f32, extra=0):
            return nc.alloc_sbuf_tensor_at(name, shape, dt, offset=base + tile * TB + extra, align_bytes=16)

        A_RS, A_ACC, A_T, A_YL, A_T3, A_SG, A_D, A_QK = 0, 1, 2, 5, 9, 10, 14, 18
        rs = at("rs", [128, NP], A_RS)
        acc = at("acc", [128, NP], A_ACC)
        T = [at("T0", [128, NP], A_T), at("T1", [128, NP], A_T + 1), at("T2", [128, NP], A_T + 2), at("T3", [128, NP], A_T3)]
        y_lru = at("y_lru", [128, LT, NP], A_YL)
        lr = at("lr", [128, 2, NP], A_SG)
        li = at("li", [128, 2, NP], A_SG + 2)
        la = at("la", [128, 2, NP], A_D)
        lt_ = at("lt", [128, 2, NP], A_D + 2)
        xc = at("xc", [128, NP], A_QK)
        xc_hl = at("xc_hl", [128, 2, NP], A_T + 1, f32r)
        gates_hl = at("gates_hl", [128, 2, 4, 128], A_T3, f32r)
        gg = at("gg", [128, LT, NP], A_QK + 1)
        xb = at("xb", [128, NP + 4], A_QK + 5)
        soft = [T[2], T[3], xc, xb]
        hh = [T[0], at("hh1", [128, NP], A_QK + 7)]
        dd = at("dd", [128, 4, NP], A_D)
        vT = at("vT", [128, HEADS, NP], A_D)
        qi = at("qi", [128, 4, NP], A_QK)
        ki = at("ki", [128, 4, NP], A_QK + 4)
        sg = at("sg", [128, HEADS, NP], A_D)
        q1, k1 = at("q1", [128, NP], A_SG), at("k1", [128, NP], A_SG + 1)
        ee = at("ee", [128, 2, NP], A_SG + 2)
        v_tok = at("v_tok", [128, NC, HEADS * DV], A_T3)
        st_b = at("st_b", [128, NC, 2, DV], A_T)
        keys_t = at("keys_t", [128, 2, 2, 128], A_ACC)
        key_vals = at("key_vals", [128, 2, DV], A_ACC, extra=2048)
        p_t = at("p_t", [128, 2, 2, 2 * C], A_RS)
        st_f = at("st_f", [128, 2, 2, DV], A_T, extra=4 * NC * 2 * DV)
        o_sq = at("o_sq", [128, 2, HEADS * C], A_YL)
        o_y = at("o_y", [128, 2, HEADS * C], A_YL + 1)
        o_rs = at("o_rs", [128, 2, HEADS * C], A_YL + 2)
        h_old = at("h_old", [128, 3, 2, BN], A_D)
        w_third = at("w_third", [128, 2, 8, 128], A_D + 2, f32r)
        sq = at("sq", [128, SQ_RING, 2, BN], A_T + 1)
        Y = at("Y", [128, KT, NP], A_QK)
        act_hi = at("act_hi", [128, GT, NP], A_YL, f32r)
        act_lo = at("act_lo", [128, GT, NP], A_SG, f32r)
        assert 4 * 2 * HEADS * C <= TB and 4 * NC * HEADS * DV <= 5 * TB and 4 * (NC + 2) * 2 * DV <= 3 * TB

        wslots = (w_hl[:, 0], w_hl[:, 1], w_third)

        banks = ctx.enter_context(nc.psum_tensor("banks", [128, 8, 512], f32))

        def ps(j, rows=128):
            s = (j % 2) * NB
            return banks[0:rows, s:s + NB, 0:BN]

        def blk(ap):
            return ap.rearrange("p (b n) -> p b n", b=NB)

        def cols(b):
            return slice(b * BN, (b + 1) * BN)

        def sum_bank(norm, b):
            return banks[:, 6 + (norm * NB + b) % 2, 0:BN]

        w_loaded = [sem(f"w_loaded{i}") for i in range(2)]
        w_scaled = sem("w_scaled")
        w_ready = sem("w_ready")
        zgw_loaded, zgw_step, zgw_ready = sem("zgw_loaded"), sem("zgw_step"), sem("zgw_ready")
        gatew_loaded, gates_hi, gates_ready = sem("gatew_loaded"), sem("gates_hi"), sem("gates_ready")
        decayw_loaded = sem("decayw_loaded")
        par_loaded, par_step, par_ready = sem("par_loaded"), sem("par_step"), sem("par_ready")
        const_step, const_ready = sem("const_step"), sem("const_ready")
        x_loaded = [sem(f"x_loaded{n}") for n in range(2 * NB)]
        mm_done = sem("mm_done")
        ps_free = [sem("ps_free_a"), sem("ps_free_b")]
        x_hi, x_lo = sem("x_hi"), sem("x_lo")
        sq_pair = sem("sq_pair")
        sq_h, sq_read = sem("sq_h"), sem("sq_read")
        sum_done, sum_read = sem("sum_done"), sem("sum_read")
        rs_ready = sem("rs_ready")
        banks_zeroed, branch_end = sem("banks_zeroed"), sem("branch_end")
        pad_zeroed, conv_step, xc_ready = sem("pad_zeroed"), sem("conv_step"), sem("xc_ready")
        xc_hi, xc_split = sem("xc_hi"), sem("xc_split")
        lru_tanh, lru_a, lru_a2 = sem("lru_tanh"), sem("lru_a"), sem("lru_a2")
        lru_ix, lru_v, lru_root, lru_u, lru_h = (sem(n) for n in ("lru_ix", "lru_v", "lru_root", "lru_u", "lru_h"))
        gelu_done, lru_sum, ylru_done = sem("gelu_done"), sem("lru_sum"), sem("ylru_done")
        softplus_step = sem("softplus_step")
        decay_step, d_ready = sem("decay_step"), sem("d_ready")
        fac_step, fac_in, fac_ready = sem("fac_step"), sem("fac_in"), sem("fac_ready")
        e_ready, qk_made = sem("e_ready"), sem("qk_made")
        silu_done = sem("silu_done")
        g_vt, g_ktb, g_kvb = sem("g_vt"), sem("g_ktb"), sem("g_kvb")
        vtok_ready, ktb_ready, stb_sum, stb_ready = sem("vtok_ready"), sem("ktb_ready"), sem("stb_sum"), sem("stb_ready")
        g_ktf, g_kvf, g_s, g_o, g_ss = (sem(n) for n in ("g_ktf", "g_kvf", "g_s", "g_o", "g_ss"))
        ktf_ready, p_fwd, p_ready = sem("ktf_ready"), sem("p_fwd"), sem("p_ready")
        stf_sum, stf_ready = sem("stf_sum"), sem("stf_ready")
        osq_ready, o_gated, ss_log, ors_ready, oy_ready = (sem(n) for n in ("osq_ready", "o_gated", "ss_log", "ors_ready", "oy_ready"))
        sq_y, acc_done = sem("sq_y"), sem("acc_done")
        hold_loaded = [sem(f"hold_loaded{i}") for i in range(3)]
        last_block, y_last = sem("last_block"), sem("y_last")
        y_scaled, y_new = sem("y_scaled"), sem("y_new")
        h_stored = sem("h_stored")
        act_sq, a_hi, a_lo = sem("act_sq"), sem("a_hi"), sem("a_lo")

        waited_pool, waited_dve = sem("waited_pool"), sem("waited_dve")

        def heads(ap):
            return ap.rearrange("p (r j c) -> p r j c", r=2, j=2)

        def by_parity(ap):
            return ap.rearrange("p (j r) c -> p r j c", r=2)

        def done(l, j):
            return l * NJ + j + 1

        def freed(l, j):
            return l * SET_JOBS[j % 2] + j // 2 + 1

        block = ctx.enter_context(nc.Block())

        @block.sync
        def _(sp):
            sp.sem_inc(w_ready, 2)
            for s in (mm_done, *ps_free, ylru_done, lru_h, a_lo):
                sp.sem_inc(s, FIRST)
            sp.dma_start(par[:, :, 0:N_LOADED], params).then_inc(par_loaded, 16)
            sp.sem_inc(sum_read, 2)

            def pair(l, i):
                for s in range(2):
                    sp.wait_ge(w_ready, (l * PAIRS + i) * 2 + s + 1)
                    sp.dma_start(w_raw[:, s], w_units[l, i * 2 + s]).then_inc(w_loaded[s], 16)

            with sp.Fori(0, L) as l:
                pair(l, 0)
                sp.wait_ge(mm_done, FIRST + l * NJ - 2)
                sp.dma_start(zg_raw[:, :, :], w_zg[l]).then_inc(zgw_loaded, 16)
                sp.dma_start(gates_raw[:, :, :], w_gates[l, 0]).then_inc(gatew_loaded, 16)
                sp.dma_start(decay_w[:, :], w_decay[l].rearrange("h r n -> (h r) n")).then_inc(decayw_loaded, 16)
                with sp.Fori(1, LT) as t:
                    pair(l, t)
                    sp.wait_ge(gates_ready, l * LT + t)
                    sp.dma_start(gates_raw[:, :, :], w_gates[l, t]).then_inc(gatew_loaded, 16)
                with sp.Fori(LT, PAIRS) as i:
                    pair(l, i)

        @block.gpsimd
        def _(pool):
            nc.gpsimd.memset(ones[:, :], 1.0).then_inc(const_step, 1)
            nc.gpsimd.memset(ident[:, :], 0.0).then_inc(const_step, 1)
            nc.gpsimd.memset(reset[:, :], 1.0).then_inc(const_step, 1)
            nc.gpsimd.memset(eps[:, :], EPS).then_inc(const_step, 1)
            pool.wait_ge(const_step, 4)
            nc.gpsimd.memset(reset[:, 0:NT + 1:C], 0.0).then_inc(const_step, 1)
            nc.gpsimd.affine_select(out=ident[:, :], in_=ident[:, :], compare_op=ALU.not_equal, fill=1.0,
                                    base=0, pattern=[[-1, 128]], channel_multiplier=1).then_inc(const_step, 1)
            nc.gpsimd.memset(T[0][0:C, 0:C], 1.0).then_inc(const_step, 1)
            pool.wait_ge(const_step, 7)
            nc.gpsimd.affine_select(out=T[0][0:C, 0:C], in_=T[0][0:C, 0:C], compare_op=ALU.is_gt, fill=0.0,
                                    base=0, pattern=[[-1, C]], channel_multiplier=1).then_inc(const_step, 1)
            pool.wait_ge(const_step, 8)
            nc.gpsimd.tensor_copy(later[:, :, :], T[0][0:C, 0:C].unsqueeze(1).to_broadcast([C, HEADS, C]))\
                .then_inc(const_ready, 1)

            pool.wait_ge(par_loaded, 16)

            def gains(l, column, n=128):
                return par[:, l, column:column + 8].unsqueeze(2).to_broadcast([128, 8, n])

            def split(l, i, s, gain, before, slot):
                unit = (l * PAIRS + i) * 2 + s
                pool.wait_ge(w_loaded[s], 16 * (l * PAIRS + i + 1))
                pool.sem_inc(waited_pool, 1)
                if gain is None:
                    pool.sem_inc(w_scaled, 1)
                else:
                    nc.gpsimd.tensor_tensor(w_raw[:, s], w_raw[:, s], gains(l, gain), ALU.mult).then_inc(w_scaled, 1)
                pool.wait_ge(w_scaled, 2 * unit + 1)
                pool.wait_ge(mm_done, FIRST + before)
                pool.sem_inc(waited_pool, 1)
                nc.gpsimd.tensor_tensor(slot[:, 0], w_raw[:, s], gains(l, P_ONE), ALU.mult).then_inc(w_scaled, 1)
                pool.wait_ge(w_scaled, 2 * unit + 2)
                nc.gpsimd.tensor_tensor(slot[:, 1], w_raw[:, s], slot[:, 0].bitcast(f32), ALU.subtract).then_inc(w_ready, 1)

            def split_pair(l, i, gain, before0, before1, slots=(0, 1)):
                for s, before in ((0, before0), (1, before1)):
                    split(l, i, s, gain, before, wslots[slots[s]])

            def split_lo(xbase):
                for n in range(NX):
                    m, b = piece(n)
                    pool.wait_ge(x_hi, xbase + n + 1)
                    nc.gpsimd.tensor_tensor(X[:, m:m + 2, 1, cols(b)], Y[:, m:m + 2, cols(b)],
                                            X[:, m:m + 2, 0, cols(b)].bitcast(f32), ALU.subtract).then_inc(x_lo, 1)

            def downs(l, g, before0, before1):
                i0 = U_MLP // 2 + 4 * g
                split_pair(l, i0 + 2, None, before0, before1)
                split_pair(l, i0 + 3, None, done(l, j_down(g, 1)), done(l, j_down(g, 3)))

            def split_gates(l, t):
                one = par[:, l, P_ONE:P_ONE + 4].unsqueeze(2).to_broadcast([128, 4, 128])
                pool.wait_ge(gatew_loaded, 16 * (l * LT + t + 1))
                if t > 0:
                    pool.wait_ge(mm_done, FIRST + done(l, j_lru(t - 1, 3)))
                pool.sem_inc(waited_pool, 1)
                nc.gpsimd.tensor_tensor(gates_hl[:, 0], gates_raw[:, :, :], one, ALU.mult).then_inc(gates_hi, 1)
                pool.wait_ge(gates_hi, l * LT + t + 1)
                nc.gpsimd.tensor_tensor(gates_hl[:, 1], gates_raw[:, :, :], gates_hl[:, 0].bitcast(f32), ALU.subtract)\
                    .then_inc(gates_ready, 1)

            with pool.Fori(0, L) as l:
                split_pair(l, 0, P_GMIX, l * NJ - 2, l * NJ - 2, (0, 2))
                split_lo(l * X_PER)
                pool.wait_ge(zgw_loaded, 16 * (l + 1))
                pool.sem_inc(waited_pool, 1)
                nc.gpsimd.tensor_tensor(zg_hl[:, :, 0], zg_raw[:, :, :], gains(l, P_GMIX, 2 * RANK), ALU.mult).then_inc(zgw_step, 1)
                pool.wait_ge(zgw_step, 2 * l + 1)
                pool.sem_inc(waited_pool, 1)
                nc.gpsimd.tensor_tensor(zg_raw[:, :, :], zg_raw[:, :, :], gains(l, P_GMIX, 2 * RANK), ALU.mult).then_inc(zgw_step, 1)
                pool.wait_ge(zgw_step, 2 * l + 2)
                nc.gpsimd.tensor_tensor(zg_hl[:, :, 1], zg_raw[:, :, :], zg_hl[:, :, 0].bitcast(f32), ALU.subtract)\
                    .then_inc(zgw_ready, 1)
                split(l, 1, 0, P_GMIX, l * NJ, wslots[1])
                split_gates(l, 0)
                split(l, 1, 1, P_GMIX, done(l, j_x(0)), wslots[0])
                for t in range(1, LT):
                    split_gates(l, t)
                    split_pair(l, t + 1, P_GMIX, done(l, j_x(t)), done(l, j_gate(t)), (1, 0))
                split_pair(l, 5, P_GMIX, done(l, J_Q0), done(l, J_Q1), (1, 0))
                with pool.Fori(0, 4) as i:
                    split_pair(l, 6 + i, P_GMIX, done(l, J_K + 2 * i), done(l, J_K + 2 * i + 1), (1, 0))
                with pool.Fori(0, 4) as i:
                    split_pair(l, U_OUT // 2 + i, P_GOUT, done(l, J_O - 2 + 2 * i), done(l, J_O - 1 + 2 * i), (1, 0))
                split_pair(l, U_MLP // 2, P_GMLP, done(l, J_O + 6), done(l, J_O + 5), (1, 2))
                split(l, U_MLP // 2 + 1, 0, P_GMLP, done(l, J_O + 7), wslots[0])
                split_lo(l * X_PER + NX + LT + NC)
                split(l, U_MLP // 2 + 1, 1, P_GMLP, done(l, j_up(0, 0)), wslots[1])
                downs(l, 0, done(l, j_up(0, 2)), done(l, j_up(0, 3)))
                with pool.Fori(1, GROUPS) as g:
                    i0 = U_MLP // 2 + 4 * g
                    split_pair(l, i0, P_GMLP, done(l, j_down(g - 1, 5)), done(l, j_down(g - 1, 7)))
                    split_pair(l, i0 + 1, P_GMLP, done(l, j_up(g, 0)), done(l, j_up(g, 1)))
                    downs(l, g, done(l, j_up(g, 2)), done(l, j_up(g, 3)))

        @block.tensor
        def _(pe):
            def product(out, w, xs, first, last):
                for n, (wp, xp) in enumerate(((w[0], xs[0]), (w[0], xs[1]), (w[1], xs[0]))):
                    for b in range(NB):
                        ins = nc.tensor.matmul(out[:, b, 0:width(b)], wp, xp[:, used(b)],
                                               start=first and n == 0, stop=last and n == 2)
                return ins

            def wslot(s, k):
                return wslots[s][:, 0, k, :], wslots[s][:, 1, k, :]

            def xtile(k):
                return X[:, k, 0, :], X[:, k, 1, :]

            def take_set(l, j):
                pe.wait_ge(ps_free[j % 2], FIRST + l * SET_JOBS[j % 2] + j // 2)

            def unit_job(l, unit, s, jp, jx):
                pe.wait_ge(w_ready, l * UNITS + unit + 3)
                pe.wait_ge(ps_free[jp % 2], FIRST + l * SET_JOBS[jp % 2] + jx)
                for k in range(KT):
                    ins = product(ps(jp), wslot(s, k), xtile(k), k == 0, k == KT - 1)
                ins.then_inc(mm_done, 1)

            def product_block(j, b, w, xs, first, last):
                for n, (wp, xp) in enumerate(((w[0], xs[0]), (w[0], xs[1]), (w[1], xs[0]))):
                    ins = nc.tensor.matmul(ps(j)[:, b, 0:width(b)], wp, xp[:, used(b)], start=first and n == 0, stop=last and n == 2)
                return ins

            def take_sum_bank(l, norm, b):
                pe.wait_ge(sum_read, l * SUMS + norm * NB + b + 1)

            def add_piece(l, norm, n, sbase):
                b, first, last = n // QT, n % QT == 0, n % QT == QT - 1
                if first:
                    take_sum_bank(l, norm, b)
                pe.wait_ge(sq_pair, sbase + n + 1)
                nc.tensor.matmul(sum_bank(norm, b), ones[:, :], sq[:, n % SQ_RING, 0, :], start=first, stop=last)\
                    .then_inc(sum_done if last else sq_read, 1)

            def first_pair(l, norm, unit, j, s, xbase, sbase):
                def hi_passes(u, b, k):
                    w = wslot((s, 2)[u], k)
                    for n, wp in enumerate(w):
                        nc.tensor.matmul(ps(j + u)[:, b, 0:width(b)], wp, xtile(k)[0][:, used(b)], start=k == 0 and n == 0, stop=False)

                def lo_pass(u, b, k):
                    return nc.tensor.matmul(ps(j + u)[:, b, 0:width(b)], wslot((s, 2)[u], k)[0], xtile(k)[1][:, used(b)],
                                            start=False, stop=k == KT - 1)

                for n in range(NX):
                    m, b = piece(n)
                    late = b == NB - 1
                    lag = [k - QT for k in (m, m + 1) if k >= QT] if late else [m, m + 1]
                    if n == 0:
                        pe.wait_ge(w_ready, l * UNITS + unit + 3)
                        take_set(l, j)
                    pe.wait_ge(x_hi, xbase + n + 1)
                    for k in (m, m + 1):
                        hi_passes(0, b, k)
                    if n == 0:
                        pe.wait_ge(w_ready, l * UNITS + unit + 1 + 3)
                        take_set(l, j + 1)
                    for k in lag:
                        hi_passes(1, b, k)
                    add_piece(l, norm, n, sbase)
                    pe.wait_ge(x_lo, xbase + n + 1)
                    for k in (m, m + 1):
                        first = lo_pass(0, b, k)
                    if n == NX - 1:
                        first.then_inc(mm_done, 1)
                    for k in lag:
                        lo_pass(1, b, k)
                for k in range(QT, KT):
                    hi_passes(1, NB - 1, k)
                for k in range(QT, KT):
                    ins = lo_pass(1, NB - 1, k)
                ins.then_inc(mm_done, 1)

            def by_blocks(l, j, s, blocks, xs, norm, n):
                for b in range(NB):
                    if b == NB - 1:
                        row_sum(l, norm, 0, n)
                    for i, (k, x) in enumerate(zip(blocks, xs)):
                        ins = product_block(j, b, wslot(s, k), x, i == 0, i == len(blocks) - 1)
                    ins.then_inc(last_block if b < NB - 1 else mm_done, 1)
                for b in range(1, NB):
                    row_sum(l, norm, b, n)

            def row_sum(l, norm, b, n):
                take_sum_bank(l, norm, b)
                pe.wait_ge(acc_done, n + b + 1)
                nc.tensor.matmul(sum_bank(norm, b), ones[:, :], acc[:, cols(b)], start=True, stop=True)\
                    .then_inc(sum_done, 1)

            def lru_gates(l, t):
                pe.wait_ge(gates_ready, l * LT + t + 1)
                pe.wait_ge(xc_split, l * LT + t + 1)
                for n in range(4):
                    jp = 3 + n
                    pe.wait_ge(ps_free[jp % 2], FIRST + l * SET_JOBS[jp % 2] + 3 * t + jp // 2)
                    product(ps(jp), (gates_hl[:, 0, n, :], gates_hl[:, 1, n, :]), (xc_hl[:, 0, :], xc_hl[:, 1, :]), True, True)\
                        .then_inc(mm_done, 1)

            def down_unit(l, g, i):
                s = i % 2
                pe.wait_ge(w_ready, l * UNITS + U_MLP + 8 * g + 4 + i + 3)
                order = ((0, (0, 1, 2)), (1, (0, 1)), (0, (3,)), (1, (2, 3))) if i == 0 else ((0, range(GT)), (1, range(GT)))
                for m, ks in order:
                    jp = j_down(0, 2 * i + m)
                    if ks[0] == 0:
                        pe.wait_ge(ps_free[jp % 2], FIRST + l * SET_JOBS[jp % 2] + 6 * g + jp // 2)
                    for k in ks:
                        if i == 0 and m == 0:
                            pe.wait_ge(a_hi, l * F_TILES + GT * g + k + 1)
                            pe.wait_ge(a_lo, FIRST + l * F_TILES + GT * g + k + 1)
                        ins = product(ps(jp), wslot(s, m * 4 + k), (act_hi[:, k, :], act_lo[:, k, :]),
                                      k == 0, k == GT - 1)
                    if ks[-1] == 3:
                        ins.then_inc(mm_done, 1)

            def last_down_unit(l, g):
                pe.wait_ge(w_ready, (l + 1) * UNITS + 2)
                j = j_down(g, KT - 2)
                for m in range(2):
                    take_set(l, j + m)
                    if m == 0:
                        for k in range(GT):
                            ins = product(ps(j), wslot(1, k), (act_hi[:, k, :], act_lo[:, k, :]), k == 0, k == GT - 1)
                        ins.then_inc(mm_done, 1)
                    else:
                        by_blocks(l, j + 1, 1, range(GT, 2 * GT), [(act_hi[:, k, :], act_lo[:, k, :]) for k in range(GT)],
                                  POST_MLP, l * 18 + 15)

            def gla(l, xbase):
                def chunk(c):
                    return slice(c * C, (c + 1) * C)

                def key_transposes(c, d, bank, signal):
                    for j in range(2):
                        ins = nc.tensor.transpose(banks[0:C, bank, j * 128:(j + 1) * 128],
                                                  ki[:, 2 * d + j, chunk(c)], ident[:, :])
                    ins.then_inc(signal, 1)

                def key_values(c, kt, bank, signal):
                    for h in range(HEADS):
                        j, r = h // 2, 64 * (h % 2)
                        ins = nc.tensor.matmul(banks[r:r + DK, bank, j * DV:(j + 1) * DV], kt[0:C, j, r:r + DK],
                                               v_tok[0:C, c, h * DV:(h + 1) * DV], start=True, stop=True)
                    ins.then_inc(signal, 1)

                def to_rows(n):
                    if n == 0:
                        for j in (J_V + 2, J_V + 3):
                            pe.wait_ge(ps_free[j % 2], FIRST + freed(l, j))
                    if n >= 2:
                        pe.wait_ge(vtok_ready, l * NC + n - 1)
                    for h in range(HEADS):
                        ins = nc.tensor.transpose(banks[0:C, 6 + n % 2, h * DV:(h + 1) * DV],
                                                  vT[:, h, chunk(NC - 1 - n)], ident[:, :])
                    ins.then_inc(g_vt, 1)

                def keys_backward(n):
                    if n == 0:
                        pe.wait_ge(vtok_ready, l * NC + NC - 1)
                    else:
                        pe.wait_ge(ktb_ready, l * (NC - 1) + n)
                    key_transposes(NC - 1 - n, 1, 6, g_ktb)

                def state_backward(n):
                    if n == 0:
                        pe.wait_ge(vtok_ready, (l + 1) * NC)
                    else:
                        pe.wait_ge(stb_sum, l * (NC - 1) + n)
                    pe.wait_ge(ktb_ready, l * (NC - 1) + n + 1)
                    key_values(NC - 1 - n, keys_t[:, n % 2], 7, g_kvb)

                after = {1 + n: [(to_rows, n)] for n in range(NC)}
                for n in range(NC - 1):
                    after.setdefault(NC + 1 + 2 * n, []).append((keys_backward, n))
                    after.setdefault(NC + 4 + 2 * n, []).append((state_backward, n))
                for h in range(HEADS):
                    j = J_SG + h
                    pe.wait_ge(w_ready, l * UNITS + 16 + h + 3)
                    take_set(l, j)
                    for k in range(KT):
                        ins = product(ps(j), wslot(1 - h % 2, k), xtile(k), k == 0, k == KT - 1)
                        if k == KT - 1:
                            ins.then_inc(mm_done, 1)
                        for work, n in after.get(h * KT + k + 1, ()):
                            work(n)
                for j in (J_SG + 2, J_SG + 3):
                    pe.wait_ge(ps_free[j % 2], FIRST + freed(l, j))
                pe.wait_ge(stb_ready, (l + 1) * (NC - 1))

                def keys_in_rows(c):
                    if c >= 1:
                        pe.wait_ge(ktf_ready, l * (NC - 1) + c)
                    key_transposes(c, 0, 0, g_ktf)

                def scores(c):
                    if c >= 1:
                        pe.wait_ge(p_ready, l * NC + c)
                    for d in range(2):
                        for j in range(2):
                            for r in range(2):
                                rows = slice(64 * r, 64 * r + DK)
                                ins = nc.tensor.matmul(banks[0:C, 2 + r, (2 * d + j) * C:(2 * d + j + 1) * C],
                                                       ki[rows, 2 * d + j, chunk(c)], qi[rows, 2 * d + j, chunk(c)],
                                                       start=True, stop=True)
                    ins.then_inc(g_s, 1)

                def squares(c):
                    pe.wait_ge(osq_ready, l * NC + c + 1)
                    if c >= 1:
                        pe.wait_ge(ss_log, l * NC + c)
                    nc.tensor.matmul(banks[:, 6, 0:HEADS * C], ones[:, :], o_sq[:, c % 2, :], start=True, stop=True)\
                        .then_inc(g_ss, 1)

                keys_in_rows(0)
                scores(0)
                for c in range(NC):
                    if c + 1 < NC - 1:
                        keys_in_rows(c + 1)
                    if c < NC - 1:
                        pe.wait_ge(ktf_ready, l * (NC - 1) + c + 1)
                        if c >= 1:
                            pe.wait_ge(stf_sum, l * (NC - 1) + c)
                        key_values(c, keys_t[:, c % 2], 1, g_kvf)
                    if c + 1 < NC:
                        scores(c + 1)
                    pe.wait_ge(p_ready, l * NC + c + 1)
                    if c >= 1:
                        pe.wait_ge(stf_ready, l * (NC - 1) + c)
                        pe.wait_ge(o_gated, l * NC + c)
                    for j in range(2):
                        for r in range(2):
                            h, rows = 2 * j + r, slice(64 * r, 64 * r + DK)
                            terms = [(v_tok[0:C, c, h * DV:(h + 1) * DV], p_t[0:C, c % 2, r, j * C:(j + 1) * C])]
                            if c > 0:
                                terms.append((st_f[rows, c % 2, j, :], qi[rows, j, chunk(c)]))
                            if c < NC - 1:
                                terms.append((st_b[rows, c, j, :], qi[rows, 2 + j, chunk(c)]))
                            for n, (a, b) in enumerate(terms):
                                ins = nc.tensor.matmul(banks[:, 4 + r, j * C:(j + 1) * C], a, b,
                                                       start=n == 0, stop=n == len(terms) - 1)
                    ins.then_inc(g_o, 1)
                    if c >= 1:
                        squares(c - 1)

                def half(s, ks):
                    for k in ks:
                        ins = product(ps(J_O + s), wslot(1 - s, k), xtile(k), k == 0, k == KT - 1)
                    return ins

                pe.wait_ge(w_ready, l * UNITS + U_OUT + 1 + 3)
                for s in (1, 0):
                    take_set(l, J_O + s)
                    if s == 1:
                        pe.wait_ge(x_lo, xbase + NX + LT)
                    else:
                        squares(NC - 1)
                        pe.wait_ge(o_gated, (l + 1) * NC)
                    half(s, range(LT))
                pe.wait_ge(x_hi, xbase + NX + LT + NC)
                pe.wait_ge(x_lo, xbase + NX + LT + NC)
                for s in range(2):
                    half(s, range(LT, KT)).then_inc(mm_done, 1)

            pe.wait_ge(const_ready, 1)
            with pe.Fori(0, L) as l:
                xbase = l * X_PER
                first_pair(l, PRE_MIX, 0, j_x(0), 0, xbase, l * 2 * NX)
                pe.wait_ge(zgw_ready, l + 1)
                take_set(l, J_ZG)
                for k in range(KT):
                    for n, xp in enumerate(xtile(k)):
                        for b in range(NB):
                            ins = nc.tensor.matmul(ps(J_ZG, 4 * RANK)[:, b, 0:width(b)], zg_hl[:, k].rearrange("p h n -> p (h n)"),
                                                   xp[:, used(b)], start=k == 0 and n == 0, stop=k == KT - 1 and n == 1)
                ins.then_inc(mm_done, 1)
                lru_gates(l, 0)
                unit_job(l, 2, 1, j_x(1), 3)
                unit_job(l, 3, 0, j_gate(1), 4)
                lru_gates(l, 1)
                with pe.Fori(2, LT) as t:
                    unit_job(l, 2 * t, 1, 1, 3 * t)
                    unit_job(l, 2 * t + 1, 0, 2, 3 * t + 1)
                    lru_gates(l, t)
                unit_job(l, 8, 1, J_Q0, J_Q0 // 2)
                unit_job(l, 9, 0, J_Q1, J_Q1 // 2)
                pe.wait_ge(decayw_loaded, 16 * (l + 1))
                pe.wait_ge(ps_free[J_ZG % 2], FIRST + freed(l, J_ZG))
                for n in range(4):
                    take_set(l, J_W + n)
                    for b in range(NB):
                        ins = nc.tensor.matmul(ps(J_W + n)[:, b, 0:width(b)], decay_w[:, n * 128:(n + 1) * 128],
                                               acc[0:4 * RANK, used(b)], start=True, stop=True)
                    ins.then_inc(mm_done, 1)
                with pe.Fori(0, 3) as i:
                    unit_job(l, 10 + 2 * i, 1, J_K, J_K // 2 + i)
                    unit_job(l, 11 + 2 * i, 0, J_K + 1, (J_K + 1) // 2 + i)
                gla(l, xbase)
                with pe.Fori(1, 3) as i:
                    unit_job(l, U_OUT + 2 * i, 1, J_O, J_O // 2 + i)
                    unit_job(l, U_OUT + 2 * i + 1, 0, J_O + 1, (J_O + 1) // 2 + i)
                unit_job(l, U_OUT + 6, 1, J_O + 6, (J_O + 6) // 2)
                pe.wait_ge(w_ready, l * UNITS + U_OUT + 7 + 3)
                take_set(l, J_O + 7)
                by_blocks(l, J_O + 7, 0, range(KT), [xtile(k) for k in range(KT)], POST_MIX, l * 18 + 6)
                first_pair(l, PRE_MLP, U_MLP, J_MLP, 1, xbase + NX + LT + NC, l * 2 * NX + NX)
                unit_job(l, U_MLP + 2, 0, J_MLP + 2, (J_MLP + 2) // 2)
                unit_job(l, U_MLP + 3, 1, J_MLP + 3, (J_MLP + 3) // 2)
                for i in range(4):
                    down_unit(l, 0, i)
                with pe.Fori(1, GROUPS - 1) as g:
                    for i in range(GT):
                        unit_job(l, U_MLP + 8 * g + i, i % 2, J_MLP + i, (J_MLP + i) // 2 + 6 * g)
                    for i in range(4):
                        down_unit(l, g, i)
                g = GROUPS - 1
                for i in range(GT):
                    unit_job(l, U_MLP + 8 * g + i, i % 2, j_up(g, i), j_up(g, i) // 2)
                for i in range(3):
                    down_unit(l, g, i)
                last_down_unit(l, g)
            for n in range(NX):
                add_piece(L, PRE_MIX, n, L * 2 * NX)

        @block.scalar
        def _(act):
            def log_mean(l, norm, b):
                act.wait_ge(sum_done, l * SUMS + norm * NB + b + 1)
                nc.scalar.activation(rs[:, cols(b)], sum_bank(norm, b), ACT.Ln, scale=1.0 / D, bias=eps[:, 0:1])\
                    .then_inc(sum_read, 1)

            def inv_root(l, norm, b):
                act.wait_ge(sum_read, l * SUMS + norm * NB + b + 3)
                nc.scalar.activation(rs[:, cols(b)], rs[:, cols(b)], ACT.Exp, scale=-0.5).then_inc(rs_ready, 1)

            def split_hi_and_square(n, read):
                m, b = piece(n)
                nc.scalar.activation(X[:, m:m + 2, 0, cols(b)], Y[:, m:m + 2, cols(b)], ACT.Copy).then_inc(x_hi, 1)
                if n >= SQ_RING:
                    act.wait_ge(sq_read, read + squares_read(n))
                nc.scalar.activation(sq[:, n % SQ_RING], Y[:, m:m + 2, cols(b)], ACT.Square).then_inc(sq_h, 1)

            def sums_between(l, norm, n):
                if n == QT:
                    log_mean(l, norm, 0)
                if n == 2 * QT:
                    log_mean(l, norm, 1)
                    inv_root(l, norm, 0)
                    inv_root(l, norm, 1)

            def last_sum(l, norm):
                log_mean(l, norm, NB - 1)
                inv_root(l, norm, NB - 1)

            def stream(dram, n):
                m, b = piece(n)
                return dram[m:m + 2, :, cols(b)].rearrange("k p n -> p k n")

            def load_old(n, source):
                act.dma_start(h_old[:, n % 3], stream(source, n)).then_inc(hold_loaded[n % 3], 16)

            def square_out(l, m, j, phase):
                if m < KT - 1:
                    act.wait_ge(ps_free[j % 2], FIRST + l * SET_JOBS[j % 2] + j // 2 + 1)
                    if m >= 3:
                        act.wait_ge(acc_done, l * 18 + phase * 9 + m - 2)
                    out = acc if m == 0 else T[2 + m % 2]
                    nc.scalar.activation(out[:, :], Y[:, m, :], ACT.Square).then_inc(sq_y, 1)
                else:
                    for b in range(NB):
                        if b < NB - 1:
                            act.wait_ge(y_last, l * 4 + phase * 2 + b + 1)
                        else:
                            log_mean(l, POST_MIX + 2 * phase, 0)
                            inv_root(l, POST_MIX + 2 * phase, 0)
                            act.wait_ge(ps_free[j % 2], FIRST + l * SET_JOBS[j % 2] + j // 2 + 1)
                        nc.scalar.activation(T[0][:, cols(b)], Y[:, m, cols(b)], ACT.Square).then_inc(sq_y, 1)

            def update(l, phase, source, target):
                norm = POST_MIX + 2 * phase
                log_mean(l, norm, 1)
                log_mean(l, norm, 2)
                for n in range(NX):
                    m, b = piece(n)
                    act.wait_ge(y_new, (l * 2 + phase) * NX + n + 1)
                    split_hi_and_square(n, (l * 2 + phase + 1) * NB * (QT - 1))
                    if n == 0:
                        inv_root(l, norm, 1)
                        inv_root(l, norm, 2)
                    if n + 3 < NX:
                        load_old(n + 3, source)
                    act.dma_start(stream(target, n), Y[:, m:m + 2, cols(b)]).then_inc(h_stored, 16)
                    sums_between(l, norm + 1, n)

            def load_x(n):
                tiles, c = slice(n % 2 * 4, n % 2 * 4 + 4), cols(n // 2)
                act.dma_start(Y[:, tiles, c], x_in[tiles, :, c].rearrange("k p n -> p k n")).then_inc(x_loaded[n], 16)

            load_x(0)
            act.wait_ge(const_ready, 1)
            act.wait_ge(par_loaded, 16)
            for n in range(1, 2 * NB):
                load_x(n)
            nc.scalar.activation(par[:, :, P_SP:P_SP + 8], par[:, :, P_LAM:P_LAM + 8], ACT.Abs).then_inc(par_step, 1)
            act.wait_ge(par_step, 1)
            nc.scalar.activation(par[:, :, P_SP:P_SP + 8], par[:, :, P_SP:P_SP + 8], ACT.Exp, scale=-1.0).then_inc(par_step, 1)
            for n in range(NX):
                if n % 2 == 0:
                    act.wait_ge(x_loaded[n // 2], 16)
                    tiles, c = slice(n % QT * 2, n % QT * 2 + 4), cols(n // QT)
                    act.dma_start(h_out[0, tiles, :, c].rearrange("k p n -> p k n"), Y[:, tiles, c]).then_inc(h_stored, 16)
                split_hi_and_square(n, 0)
                sums_between(0, PRE_MIX, n)
            act.wait_ge(par_ready, 1)
            with act.Fori(0, L) as l:
                xbase = l * X_PER + NX
                last_sum(l, PRE_MIX)
                with act.Fori(0, LT) as t:
                    for n, (out, bias) in enumerate(((lr[:, 0], P_BAF), (li[:, 0], P_BXF), (lr[:, 1], P_BAB), (li[:, 1], P_BXB))):
                        jp = 3 + n
                        act.wait_ge(mm_done, FIRST + l * NJ + 6 * t + jp + 1)
                        if n == 1:
                            act.wait_ge(lru_h, FIRST + (l * LT + t) * 2)
                        nc.scalar.activation(blk(out), ps(jp), ACT.Sigmoid, bias=par[:, l, bass.ds(bias + t, 1)])\
                            .then_inc(ps_free[jp % 2], 1)
                    for d in range(2):
                        act.wait_ge(ps_free[1], FIRST + l * SET_JOBS[1] + 3 * t + d + 2)
                        nc.scalar.activation(lt_[:, d, 0:NT], lr[:, d, 0:NT], ACT.Tanh,
                                             scale=par[:, l, bass.ds(P_SP + 4 * d + t, 1)]).then_inc(lru_tanh, 1)
                    for d in range(2):
                        nc.scalar.activation(la[:, d, 0:NT], lr[:, d, 0:NT], ACT.Exp,
                                             scale=par[:, l, bass.ds(P_NSP + 4 * d + t, 1)]).then_inc(lru_a, 1)
                    for d in range(2):
                        act.wait_ge(lru_a, (l * LT + t) * 2 + d + 1)
                        nc.scalar.activation(lr[:, d, 0:NT], la[:, d, 0:NT], ACT.Square).then_inc(lru_a2, 1)
                    act.wait_ge(ps_free[0], FIRST + l * SET_JOBS[0] + 3 * t + 2)
                    nc.scalar.activation(gg[:, t, 0:NT], gg[:, t, 0:NT], ACT.Gelu_apprx_tanh).then_inc(gelu_done, 1)
                    for d in range(2):
                        act.wait_ge(lru_v, (l * LT + t) * 2 + d + 1)
                        nc.scalar.activation(lt_[:, d, 0:NT], lt_[:, d, 0:NT], ACT.Sqrt).then_inc(lru_root, 1)
                def soft_n(n):
                    return soft[n][:, 0:NT]

                for n in range(4):
                    act.wait_ge(mm_done, FIRST + done(l, J_W + n))
                    nc.scalar.activation(blk(soft[n][:, 0:NP]), ps(J_W + n), ACT.Abs, bias=par[:, l, P_BG + n:P_BG + n + 1])\
                        .then_inc(softplus_step, 1)
                for n in range(4):
                    act.wait_ge(softplus_step, l * 12 + n + 1)
                    nc.scalar.activation(soft_n(n), soft_n(n), ACT.Exp, scale=-1.0).then_inc(softplus_step, 1)
                for n in range(4):
                    act.wait_ge(softplus_step, l * 12 + 4 + n + 1)
                    nc.scalar.activation(soft_n(n), soft_n(n), ACT.Ln, bias=1.0).then_inc(softplus_step, 1)
                for e in range(4):
                    j = e % 2
                    for d in range(2):
                        if e == 0:
                            act.wait_ge(d_ready, l * 4 + 2 * d + 2)
                        else:
                            act.wait_ge(qk_made, l * 8 + 2 * (e - 1) + d + 1)
                        nc.scalar.activation(ee[:, d, 0:NT], dd[:, 2 * d + j, 0:NT], ACT.Exp,
                                             scale=(1.0 if e < 2 else -1.0) / GATE_NORM).then_inc(e_ready, 1)
                act.wait_ge(fac_in, 2 * l + 2)
                nc.scalar.activation(fac[:, :, :], fac[:, :, :], ACT.Exp, scale=1.0 / GATE_NORM).then_inc(fac_ready, 1)
                for n in range(NC):
                    act.wait_ge(g_vt, l * NC + n + 1)
                    nc.scalar.activation(v_tok[0:C, NC - 1 - n, :], banks[0:C, 6 + n % 2, :], ACT.Copy).then_inc(vtok_ready, 1)
                for h in range(HEADS):
                    act.wait_ge(ps_free[(J_SG + h) % 2], FIRST + freed(l, J_SG + h))
                    nc.scalar.activation(sg[:, h, 0:NT], sg[:, h, 0:NT], ACT.Silu).then_inc(silu_done, 1)
                act.wait_ge(stb_ready, (l + 1) * (NC - 1))

                def lru_hi(t):
                    if t == 0:
                        act.wait_ge(mm_done, FIRST + done(l, J_SG + 3))
                    nc.scalar.activation(X[:, t, 0, 0:NT], y_lru[:, t, 0:NT], ACT.Copy).then_inc(x_hi, 1)

                def before_scores(c):
                    if c < NC - 1:
                        act.wait_ge(g_ktf, l * (NC - 1) + c + 1)
                        if c >= 2:
                            act.wait_ge(g_kvf, l * (NC - 1) + c - 1)
                        nc.scalar.activation(keys_t[0:C, c % 2].rearrange("p j n -> p (j n)"), banks[0:C, 0, 0:256], ACT.Copy)\
                            .then_inc(ktf_ready, 1)
                    act.wait_ge(g_s, l * NC + c + 1)
                    if c >= 2:
                        act.wait_ge(g_o, l * NC + c - 1)
                    nc.scalar.activation(p_t[0:C, c % 2], banks[0:C, 2:4, 0:2 * C], ACT.Copy)\
                        .then_inc(p_fwd, 1)

                def head_norm(c):
                    act.wait_ge(g_ss, l * NC + c + 1)
                    flat = o_rs[:, c % 2, :]
                    if c == 0:
                        act.wait_ge(x_lo, xbase + LT)
                    if c >= 2:
                        act.wait_ge(oy_ready, l * NC + c - 1)
                    nc.scalar.activation(flat, banks[:, 6, 0:HEADS * C], ACT.Ln, scale=1.0 / DV, bias=eps[:, 0:1])\
                        .then_inc(ss_log, 1)
                    act.wait_ge(ss_log, l * NC + c + 1)
                    nc.scalar.activation(flat, flat, ACT.Exp, scale=-0.5).then_inc(ors_ready, 1)
                    act.wait_ge(oy_ready, l * NC + c + 1)
                    nc.scalar.activation(by_parity(X[:, 4:8, 0, c * C:(c + 1) * C]), heads(o_y[:, c % 2, :]), ACT.Copy).then_inc(x_hi, 1)

                before_scores(0)
                lru_hi(0)
                lru_hi(1)
                for c in range(NC):
                    if c + 1 < NC:
                        before_scores(c + 1)
                    if c == 0:
                        act.wait_ge(x_lo, xbase + 1)
                    act.wait_ge(g_o, l * NC + c + 1)
                    if c >= 2:
                        act.wait_ge(g_ss, l * NC + c - 1)
                    nc.scalar.activation(o_sq[:, c % 2, :].rearrange("p (r n) -> p r n", r=2), banks[:, 4:6, 0:2 * C], ACT.Square)\
                        .then_inc(osq_ready, 1)
                    if c == 0:
                        lru_hi(2)
                        lru_hi(3)
                    if c >= 1:
                        head_norm(c - 1)
                head_norm(NC - 1)
                act.wait_ge(x_lo, xbase + LT + NC)
                act.wait_ge(h_stored, 16 * (2 * NX * l + H_FIRST))
                for n in range(3):
                    load_old(n, h_out[l])
                for m in range(KT):
                    square_out(l, m, J_O + m, 0)
                update(l, 0, h_out[l], h_mid[l])
                last_sum(l, PRE_MLP)

                def hidden(g, i):
                    jp = J_MLP + i
                    act.wait_ge(ps_free[jp % 2], FIRST + l * SET_JOBS[jp % 2] + 6 * g + jp // 2 + 1)
                    if i >= 2:
                        act.wait_ge(a_lo, FIRST + l * F_TILES + g * GT + i - 1)
                    else:
                        act.wait_ge(a_lo, FIRST + l * F_TILES + g * GT)
                    nc.scalar.activation(T[2 + i % 2][:, :], T[i % 2][:, :], ACT.Square).then_inc(act_sq, 1)
                    act.wait_ge(act_sq, l * F_TILES + g * GT + i + 1)
                    nc.scalar.activation(act_hi[:, i, :], T[2 + i % 2][:, :], ACT.Copy).then_inc(a_hi, 1)

                with act.Fori(0, GROUPS - 1) as g:
                    for i in range(GT):
                        hidden(g, i)
                act.wait_ge(h_stored, 16 * (2 * NX * l + H_FIRST + NX))
                for n in range(3):
                    load_old(n, h_mid[l])
                for i in range(GT):
                    hidden(GROUPS - 1, i)
                for m in range(KT):
                    if m < 2:
                        act.wait_ge(a_lo, FIRST + (l + 1) * F_TILES)
                    square_out(l, m, j_down(GROUPS - 1, m), 1)
                update(l, 1, h_mid[l], h_out[l + 1])
            act.wait_ge(h_stored, 16 * (2 * NX * L + H_FIRST))

        @block.vector
        def _(dve):
            V = nc.vector

            def add_pair(total, n):
                dve.wait_ge(sq_h, total + n + 1)
                V.tensor_tensor(sq[:, n % SQ_RING, 0, :], sq[:, n % SQ_RING, 0, :], sq[:, n % SQ_RING, 1, :], ALU.add)\
                    .then_inc(sq_pair, 1)

            def scaled_out(l, jp, jx, jd, out, rows=128, factor=None):
                dve.wait_ge(mm_done, FIRST + jd)
                if factor is None:
                    ins = V.tensor_tensor(out, ps(jp, rows), blk(rs[0:rows, :]), ALU.mult)
                else:
                    ins = V.scalar_tensor_tensor(out=out, in0=ps(jp, rows), scalar=factor, in1=blk(rs[0:rows, :]),
                                                 op0=ALU.mult, op1=ALU.mult)
                ins.then_inc(ps_free[jp % 2], 1)

            def add_square(l, phase, m, b=None):
                last = m == KT - 1
                c = cols(b) if last else slice(0, NP)
                dve.wait_ge(sq_y, l * 20 + phase * 10 + m + 1 + (b if last else 0))
                if m >= 2:
                    dve.wait_ge(acc_done, l * 18 + phase * 9 + m - 1)
                V.tensor_tensor(acc[:, c], acc[:, c], T[0][:, c] if last else T[2 + m % 2][:, :], ALU.add).then_inc(acc_done, 1)

            def projected(l, phase, j0, add):
                for m in range(KT):
                    j = j0 + m
                    for b in range(NB) if m == KT - 1 else (None,):
                        if b is None or b == NB - 1:
                            dve.wait_ge(mm_done, FIRST + done(l, j))
                        else:
                            dve.wait_ge(last_block, l * 4 + phase * 2 + b + 1)
                        if b is None:
                            y, out = blk(Y[:, m, :]), ps(j)
                        else:
                            y, out = Y[:, m, cols(b)], ps(j)[:, b, :]
                        ins = V.tensor_tensor(y, out, y, ALU.add) if add else V.tensor_copy(y, out)
                        ins.then_inc(y_last if b is not None and b < NB - 1 else ps_free[j % 2], 1)
                        if b is None and m >= 2:
                            add_square(l, phase, m - 1)
                        elif b == 0:
                            add_square(l, phase, KT - 2)
                        elif b is not None:
                            add_square(l, phase, KT - 1, b - 1)
                add_square(l, phase, KT - 1, NB - 1)

            def update(l, phase, gain):
                total = (l * 2 + phase) * NX
                for n in range(NX):
                    m, b = piece(n)
                    y = Y[:, m:m + 2, cols(b)]
                    if m == 0:
                        dve.wait_ge(rs_ready, l * SUMS + (POST_MIX + 2 * phase) * NB + b + 1)
                    V.tensor_tensor(y, y, rs[:, cols(b)].unsqueeze(1).to_broadcast([128, 2, BN]), ALU.mult)\
                        .then_inc(y_scaled, 1)
                    dve.wait_ge(y_scaled, total + n + 1)
                    dve.wait_ge(hold_loaded[n % 3], 16 * ((l * 2 + phase) * (NX // 3) + n // 3 + 1))
                    for k in range(2):
                        ins = V.scalar_tensor_tensor(out=y[:, k], in0=y[:, k], scalar=par[:, l, gain + m + k:gain + m + k + 1],
                                                     in1=h_old[:, n % 3, k, :], op0=ALU.mult, op1=ALU.add)
                    ins.then_inc(y_new, 1)
                    if n >= 1:
                        add_pair(total + NX, n - 1)
                add_pair(total + NX, NX - 1)

            for b in (NB - 1, 2 * NB - 1):
                V.memset(banks[:, b, width(NB - 1):BN], 0.0).then_inc(banks_zeroed, 1)
            dve.wait_ge(banks_zeroed, 2)

            lam, sp, nsp = (par[:, :, c:c + 8] for c in (P_LAM, P_SP, P_NSP))
            z2 = acc[:, 0:8 * L].rearrange("p (l n) -> p l n", l=L)
            series = acc[:, 64:64 + 8 * L].rearrange("p (l n) -> p l n", l=L)
            steps = [2]

            def step(ins):
                steps[0] += 1
                ins.then_inc(par_step, 1)
                dve.wait_ge(par_step, steps[0])

            dve.wait_ge(par_step, 2)
            step(V.tensor_scalar(nsp, sp, 2.0, None, ALU.add))
            step(V.reciprocal(nsp, nsp))
            step(V.tensor_tensor(sp, sp, nsp, ALU.mult))
            step(V.tensor_tensor(z2, sp, sp, ALU.mult))
            step(V.tensor_scalar(series, z2, 1.0 / 19, 1.0 / 17, ALU.mult, ALU.add))
            for n in (15, 13, 11, 9, 7, 5, 3, 1):
                step(V.tensor_tensor(series, series, z2, ALU.mult))
                step(V.tensor_scalar(series, series, 1.0 / n, None, ALU.add))
            step(V.scalar_tensor_tensor(out=sp, in0=sp, scalar=2 * LRU_C, in1=series, op0=ALU.mult, op1=ALU.mult))
            step(V.tensor_scalar(nsp, lam, -LRU_C, 0.0, ALU.mult, ALU.max))
            step(V.tensor_tensor(sp, sp, nsp, ALU.add))
            V.tensor_scalar(nsp, sp, -1.0, None, ALU.mult).then_inc(par_ready, 1)
            for n in range(NX):
                add_pair(0, n)

            with dve.Fori(0, L) as l:
                xbase = l * X_PER + NX

                def root_in(t):
                    for d in range(2):
                        n = (l * LT + t) * 2 + d
                        dve.wait_ge(lru_root, n + 1)
                        V.tensor_tensor(li[:, d, 0:NT], li[:, d, 0:NT], lt_[:, d, 0:NT], ALU.mult).then_inc(lru_u, 1)

                def scans(t):
                    dve.wait_ge(ylru_done, FIRST + l * LT + t)
                    for d in range(2):
                        n = (l * LT + t) * 2 + d
                        dve.wait_ge(lru_u, n + 1)
                        a, u, h = la[:, d, 0:NT], li[:, d, 0:NT], hh[d][:, 0:NT]
                        if d == 1:
                            a, u, h = a[:, ::-1], u[:, ::-1], h[:, ::-1]
                        V.tensor_tensor_scan(h, a, u, 0.0, ALU.mult, ALU.add).then_inc(lru_h, 1)

                def lru_result(t):
                    dve.wait_ge(lru_h, FIRST + (l * LT + t) * 2 + 2)
                    V.tensor_tensor(hh[0][:, 0:NT], hh[0][:, 0:NT], hh[1][:, 0:NT], ALU.add).then_inc(lru_sum, 1)
                    dve.wait_ge(lru_sum, l * LT + t + 1)
                    dve.wait_ge(gelu_done, l * LT + t + 1)
                    V.tensor_tensor(y_lru[:, t, 0:NT], hh[0][:, 0:NT], gg[:, t, 0:NT], ALU.mult).then_inc(ylru_done, 1)

                def branch_in(t, first=False):
                    jp = 0 if first else 1
                    scaled_out(l, jp, 0, l * NJ + 6 * t + jp + 1, blk(xb[:, 2:2 + NP]))
                    dve.wait_ge(ps_free[jp], FIRST + l * SET_JOBS[jp] + 3 * t + 1)
                    V.memset(xb[:, 2 + NT:2 + NP], 0.0).then_inc(branch_end, 1)
                    dve.wait_ge(branch_end, l * LT + t + 1)

                def conv(t):
                    base = (l * LT + t) * 3

                    def tap(n):
                        return par[:, l, bass.ds(P_CONVW + 4 * t + n, 1)]
                    V.tensor_scalar(xc[:, :], xb[:, 0:NP], tap(0), par[:, l, bass.ds(P_CONVB + t, 1)], ALU.mult, ALU.add)\
                        .then_inc(conv_step, 1)
                    for n in range(1, 4):
                        dve.wait_ge(conv_step, base + n)
                        V.scalar_tensor_tensor(out=xc[:, :], in0=xb[:, n:n + NP], scalar=tap(n), in1=xc[:, :],
                                               op0=ALU.mult, op1=ALU.add).then_inc(conv_step if n < 3 else xc_ready, 1)
                    dve.wait_ge(xc_ready, l * LT + t + 1)
                    V.tensor_copy(xc_hl[:, 0, :], xc[:, :]).then_inc(xc_hi, 1)
                    dve.wait_ge(xc_hi, l * LT + t + 1)
                    V.tensor_tensor(xc_hl[:, 1, :], xc[:, :], xc_hl[:, 0, :].bitcast(f32), ALU.subtract).then_inc(xc_split, 1)

                def gate_in(t, first=False):
                    jp = 1 if first else 2
                    scaled_out(l, jp, 0, l * NJ + 6 * t + jp + 1, blk(gg[:, t, :]))

                def input_and_decay(t):
                    dve.wait_ge(xc_ready, l * LT + t + 1)
                    for d in range(2):
                        dve.wait_ge(ps_free[0], FIRST + l * SET_JOBS[0] + 3 * t + 3 + d)
                        V.tensor_tensor(li[:, d, 0:NT], li[:, d, 0:NT], xc[:, 0:NT], ALU.mult).then_inc(lru_ix, 1)
                    for d in range(2):
                        n = (l * LT + t) * 2 + d
                        dve.wait_ge(lru_a2, n + 1)
                        dve.wait_ge(lru_tanh, n + 1)
                        V.scalar_tensor_tensor(out=lt_[:, d, 0:NT], in0=lr[:, d, 0:NT], scalar=1.0, in1=lt_[:, d, 0:NT],
                                               op0=ALU.add, op1=ALU.mult).then_inc(lru_v, 1)

                dve.wait_ge(h_stored, 16 * (2 * NX * l + H_FIRST))
                dve.wait_ge(rs_ready, l * SUMS + (PRE_MIX + 1) * NB)
                dve.wait_ge(mm_done, FIRST + done(l, j_x(0)))
                V.memset(xb[:, 0:2], 0.0).then_inc(pad_zeroed, 1)
                V.memset(xb[:, 2 + NP:4 + NP], 0.0).then_inc(pad_zeroed, 1)
                dve.wait_ge(pad_zeroed, 2 * l + 2)
                branch_in(0, True)
                conv(0)
                gate_in(0, True)
                scaled_out(l, J_ZG, 0, done(l, J_ZG), blk(acc[0:4 * RANK, :]), rows=4 * RANK)
                input_and_decay(0)
                with dve.Fori(1, LT) as t:
                    branch_in(t)
                    dve.wait_ge(mm_done, FIRST + l * NJ + 6 * t + 1)
                    dve.wait_ge(lru_ix, (l * LT + t) * 2)
                    dve.wait_ge(xc_split, l * LT + t)
                    conv(t)
                    root_in(t - 1)
                    gate_in(t)
                    scans(t - 1)
                    lru_result(t - 1)
                    input_and_decay(t)
                scaled_out(l, J_Q0, 0, done(l, J_Q0), blk(T[1][:, :]), factor=DK ** -0.5)
                root_in(LT - 1)
                scans(LT - 1)
                dve.wait_ge(lru_v, (l + 1) * LT * 2)
                scaled_out(l, J_Q1, 0, done(l, J_Q1), blk(q1[:, :]), factor=DK ** -0.5)
                lru_result(LT - 1)

                for n in range(4):
                    dve.wait_ge(softplus_step, l * 12 + n + 1)
                    V.tensor_scalar(blk(dd[:, n, :]), ps(J_W + n), par[:, l, P_BG + n:P_BG + n + 1], 0.0, ALU.add, ALU.min)\
                        .then_inc(ps_free[(J_W + n) % 2], 1)
                for n in range(4):
                    if n == 2:
                        dve.wait_ge(ylru_done, FIRST + (l + 1) * LT)
                        scaled_out(l, J_K, 0, done(l, J_K), blk(T[0][:, :]))
                    log_term, d_n = soft[n][:, 0:NT], dd[:, n, 0:NT]
                    dve.wait_ge(softplus_step, l * 12 + 8 + n + 1)
                    dve.wait_ge(ps_free[(J_W + n) % 2], FIRST + freed(l, J_W + n))
                    V.tensor_tensor(d_n, d_n, log_term, ALU.subtract).then_inc(decay_step, 1)
                    dve.wait_ge(decay_step, l * 8 + 2 * n + 1)
                    if n < 2:
                        V.tensor_tensor_scan(log_term, reset[:, 0:NT], d_n, 0.0, ALU.mult, ALU.add).then_inc(decay_step, 1)
                    else:
                        V.tensor_tensor_scan(log_term[:, ::-1], reset[:, 1:NT + 1][:, ::-1], d_n[:, ::-1], 0.0, ALU.mult, ALU.add)\
                            .then_inc(decay_step, 1)
                    dve.wait_ge(decay_step, l * 8 + 2 * n + 2)
                    by_chunk = log_term.rearrange("p (c t) -> p c t", t=C)
                    end = C - 1 if n < 2 else 0
                    V.tensor_copy(b_mid[:, n, :], by_chunk[:, :, MID]).then_inc(fac_step, 1)
                    V.tensor_copy(b_tot[:, n, :], by_chunk[:, :, end]).then_inc(fac_step, 1)
                    dve.wait_ge(fac_step, l * 9 + 2 * n + 2)
                    V.tensor_tensor(d_n.rearrange("p (c t) -> p c t", t=C), by_chunk,
                                    b_mid[:, n, :].unsqueeze(2).to_broadcast([128, NC, C]), ALU.subtract).then_inc(d_ready, 1)
                scaled_out(l, J_K + 1, 0, done(l, J_K + 1), blk(k1[:, :]))
                V.tensor_tensor(fac[:, :, :], b_tot[:, :, :], b_mid[:, :, :], ALU.subtract).then_inc(fac_step, 1)
                dve.wait_ge(fac_step, l * 9 + 9)
                V.tensor_tensor(fac[:, 0:2, 0:NC - 1], fac[:, 0:2, 0:NC - 1], b_mid[:, 0:2, 1:NC], ALU.add).then_inc(fac_in, 1)
                V.tensor_tensor(fac[:, 2:4, 1:NC], fac[:, 2:4, 1:NC], b_mid[:, 2:4, 0:NC - 1], ALU.add).then_inc(fac_in, 1)
                for e, j in enumerate((J_Q0, J_Q1, J_K, J_K + 1)):
                    plain = (T[1], q1, T[0], k1)[e]
                    dve.wait_ge(ps_free[j % 2], FIRST + freed(l, j))
                    for d in range(2):
                        dve.wait_ge(e_ready, l * 8 + 2 * e + d + 1)
                        out = (qi if e < 2 else ki)[:, 2 * d + e % 2, 0:NT]
                        V.tensor_tensor(out, plain[:, 0:NT], ee[:, d, 0:NT], ALU.mult).then_inc(qk_made, 1)
                for h in range(HEADS):
                    scaled_out(l, J_V + h, 0, done(l, J_V + h), blk(vT[:, h, :]))

                def keys_backward(n):
                    dve.wait_ge(g_ktb, l * (NC - 1) + n + 1)
                    if n >= 2:
                        dve.wait_ge(g_kvb, l * (NC - 1) + n - 1)
                    V.tensor_copy(keys_t[0:C, n % 2].rearrange("p j n -> p (j n)"), banks[0:C, 6, 0:256])\
                        .then_inc(ktb_ready, 1)

                def state_backward(n):
                    c = NC - 1 - n
                    dve.wait_ge(g_kvb, l * (NC - 1) + n + 1)
                    kv = banks[:, 7, 0:2 * DV].rearrange("p (j v) -> p j v", j=2)
                    if n == 0:
                        V.tensor_copy(key_vals[:, :, :], kv).then_inc(stb_sum, 1)
                    else:
                        dve.wait_ge(stb_ready, l * (NC - 1) + n)
                        V.tensor_tensor(key_vals[:, :, :], kv, st_b[:, c, :, :], ALU.add).then_inc(stb_sum, 1)
                    dve.wait_ge(stb_sum, l * (NC - 1) + n + 1)
                    V.tensor_tensor(st_b[:, c - 1, :, :], key_vals[:, :, :],
                                    fac[:, 2:4, c:c + 1].to_broadcast([128, 2, DV]), ALU.mult).then_inc(stb_ready, 1)

                dve.wait_ge(qk_made, l * 8 + 8)
                dve.wait_ge(fac_ready, l + 1)
                dve.wait_ge(g_vt, (l + 1) * NC)
                for step in range(1, HEADS * KT + 1):
                    n = (step - NC - 1) // 2
                    if 0 <= n < NC - 1 and step == NC + 1 + 2 * n:
                        keys_backward(n)
                    n = (step - NC - 4) // 2
                    if 0 <= n < NC - 1 and step == NC + 4 + 2 * n:
                        state_backward(n)
                    if step > NC and step % KT == 3:
                        h = step // KT - 1
                        scaled_out(l, J_SG + h, 0, done(l, J_SG + h), blk(sg[:, h, :]))
                scaled_out(l, J_SG + 3, 0, done(l, J_SG + 3), blk(sg[:, 3, :]))

                def lru_lo(t):
                    dve.wait_ge(x_hi, xbase + t + 1)
                    V.tensor_tensor(X[:, t, 1, 0:NT], y_lru[:, t, 0:NT], X[:, t, 0, 0:NT].bitcast(f32), ALU.subtract)\
                        .then_inc(x_lo, 1)
                dve.wait_ge(silu_done, (l + 1) * HEADS)

                def select(c):
                    dve.wait_ge(g_s, l * NC + c + 1)
                    dve.wait_ge(p_fwd, l * NC + c + 1)
                    dve.sem_inc(waited_dve, 1)
                    V.copy_predicated(p_t[0:C, c % 2], later[:, :, :].rearrange("p (r j) c -> p r (j c)", r=2),
                                      banks[0:C, 2:4, 2 * C:4 * C]).then_inc(p_ready, 1)

                def finish(c):
                    dve.wait_ge(ors_ready, l * NC + c + 1)
                    dve.wait_ge(o_gated, l * NC + c + 1)
                    V.tensor_tensor(o_y[:, c % 2, :], o_y[:, c % 2, :], o_rs[:, c % 2, :], ALU.mult).then_inc(oy_ready, 1)
                    dve.wait_ge(x_hi, xbase + LT + c + 1)
                    dve.wait_ge(oy_ready, l * NC + c + 1)
                    cols = slice(c * C, (c + 1) * C)
                    V.tensor_tensor(by_parity(X[:, 4:8, 1, cols]), heads(o_y[:, c % 2, :]),
                                    by_parity(X[:, 4:8, 0, cols].bitcast(f32)), ALU.subtract)\
                        .then_inc(x_lo, 1)

                select(0)
                lru_lo(0)
                lru_lo(1)
                for c in range(NC):
                    if c + 1 < NC:
                        select(c + 1)
                    if c < NC - 1:
                        dve.wait_ge(g_kvf, l * (NC - 1) + c + 1)
                        kv = banks[:, 1, 0:2 * DV].rearrange("p (j v) -> p j v", j=2)
                        if c == 0:
                            V.tensor_copy(key_vals[:, :, :], kv).then_inc(stf_sum, 1)
                        else:
                            dve.wait_ge(stf_ready, l * (NC - 1) + c)
                            V.tensor_tensor(key_vals[:, :, :], kv, st_f[:, c % 2], ALU.add).then_inc(stf_sum, 1)
                            dve.wait_ge(g_o, l * NC + c)
                        dve.wait_ge(stf_sum, l * (NC - 1) + c + 1)
                        V.tensor_tensor(st_f[:, (c + 1) % 2], key_vals[:, :, :],
                                        fac[:, 0:2, c:c + 1].to_broadcast([128, 2, DV]), ALU.mult).then_inc(stf_ready, 1)
                    dve.wait_ge(osq_ready, l * NC + c + 1)
                    if c == 0:
                        dve.wait_ge(x_lo, xbase + 2)
                    if c >= 2:
                        dve.wait_ge(x_lo, xbase + LT + c - 1)
                    V.tensor_tensor(heads(o_y[:, c % 2, :]),
                                    banks[:, 4:6, 0:2 * C].rearrange("p r (j c) -> p r j c", j=2),
                                    by_parity(sg[:, :, c * C:(c + 1) * C]), ALU.mult).then_inc(o_gated, 1)
                    if c == 0:
                        lru_lo(2)
                        lru_lo(3)
                    if c >= 1:
                        finish(c - 1)
                finish(NC - 1)

                projected(l, 0, J_O, False)
                update(l, 0, P_GMIXPOST)

                def group(g, jd):
                    def relu(i):
                        jp = J_MLP + i
                        dve.wait_ge(mm_done, FIRST + jd + i + 1)
                        if i >= 2:
                            dve.wait_ge(act_sq, l * F_TILES + g * GT + i - 1)
                        V.scalar_tensor_tensor(out=blk(T[i % 2][:, :]), in0=ps(jp), scalar=0.0, in1=blk(rs[:, :]),
                                               op0=ALU.max, op1=ALU.mult).then_inc(ps_free[jp % 2], 1)

                    def hidden_lo(i):
                        dve.wait_ge(a_hi, l * F_TILES + g * GT + i + 1)
                        V.tensor_tensor(act_lo[:, i, :], T[2 + i % 2][:, :], act_hi[:, i, :].bitcast(f32), ALU.subtract)\
                            .then_inc(a_lo, 1)

                    for i in range(GT):
                        relu(i)
                        if i >= 1:
                            hidden_lo(i - 1)
                    hidden_lo(GT - 1)

                def down_sum(m, jd, first):
                    jp = J_MLP + GT + m
                    dve.wait_ge(mm_done, FIRST + jd + GT + m + 1)
                    if first:
                        ins = V.tensor_copy(blk(Y[:, m, :]), ps(jp))
                    else:
                        ins = V.tensor_tensor(blk(Y[:, m, :]), ps(jp), blk(Y[:, m, :]), ALU.add)
                    ins.then_inc(ps_free[jp % 2], 1)

                dve.wait_ge(rs_ready, l * SUMS + (PRE_MLP + 1) * NB)
                group(0, l * NJ + J_MLP)
                dve.wait_ge(h_stored, 16 * (2 * NX * l + H_FIRST + NX))
                for m in range(KT):
                    down_sum(m, l * NJ + J_MLP, True)
                with dve.Fori(1, GROUPS - 1) as g:
                    group(g, l * NJ + J_MLP + 12 * g)
                    for m in range(KT):
                        down_sum(m, l * NJ + J_MLP + 12 * g, False)
                group(GROUPS - 1, l * NJ + j_up(GROUPS - 1, 0))
                projected(l, 1, j_down(GROUPS - 1, 0), True)
                update(l, 1, P_GMLPPOST)


def kernel(**inputs):
    import numpy as np
    import concourse.bacc as bacc
    from concourse.bass_utils import run_bass_kernel_spmd

    a = {k: np.asarray(v) for k, v in inputs.items()}

    tokens = np.concatenate([a["meta_tokens"], a["x"][0]], axis=0)
    x_in = np.zeros((KT, 128, NP), np.float32)
    x_in[:, :, :NT] = tokens.T.reshape(KT, 128, NT)

    def out_tile(w, c):
        return w[:, c:c + 128].reshape(KT, 128, 128).transpose(1, 0, 2)

    q0, k0, v0, g0, z0 = 2 * LW, 2 * LW + 256, 2 * LW + 512, 2 * LW + 1024, 2 * LW + 1536
    w_units = np.empty((L, UNITS, 128, 8, 128), np.float32)
    w_gates = np.zeros((L, LT, 128, 4, 128), np.float32)
    w_decay = np.zeros((L, 2, 2 * RANK, 512), np.float32)
    w_zg = np.empty((L, 128, KT, 2 * RANK), np.float32)
    params = np.empty((128, L, N_LOADED), np.float32)
    for l in range(L):
        win, wout, up, down = a["w_in"][l], a["w_out"][l], a["w_mlp_up"][l], a["w_mlp_down"][l]
        columns = [c for t in range(LT) for c in (128 * t, LW + 128 * t)]
        columns += [q0, q0 + 128, k0, k0 + 128] + [v0 + 128 * h for h in range(4)] + [g0 + 128 * h for h in range(4)]
        for u, c in enumerate(columns):
            w_units[l, u] = out_tile(win, c)
        for m in range(KT):
            w_units[l, U_OUT + m] = out_tile(wout, 128 * m)
        for g in range(GROUPS):
            for i in range(GT):
                w_units[l, U_MLP + 8 * g + i] = out_tile(up, 128 * (GT * g + i))
                w_units[l, U_MLP + 8 * g + GT + i] = down[512 * g:512 * (g + 1), 256 * i:256 * (i + 1)]\
                    .reshape(4, 128, 2, 128).transpose(1, 2, 0, 3).reshape(128, 8, 128)
        w_zg[l] = win[:, z0:z0 + 2 * RANK].reshape(KT, 128, 2 * RANK).transpose(1, 0, 2)
        for n, name in enumerate(("lru_wa_f", "lru_wx_f", "lru_wa_b", "lru_wx_b")):
            for head in range(8):
                r = 64 * (head % 2)
                w_gates[l, head // 2, r:r + 64, n, r:r + 64] = a[name][l, head]
        w_decay[l, :, :RANK, 0:256] = a["gla_wg_f"][l]
        w_decay[l, :, RANK:, 256:512] = a["gla_wg_b"][l]

        def put(at, v):
            v = v.reshape(-1, 128).T
            params[:, l, at:at + v.shape[1]] = v
        for t in range(LT):
            params[:, l, P_CONVW + 4 * t:P_CONVW + 4 * t + 4] = a["conv_w"][l][:, 128 * t:128 * t + 128].T
        for at, name in ((P_CONVB, "conv_b"), (P_BAF, "lru_ba_f"), (P_BXF, "lru_bx_f"), (P_BAB, "lru_ba_b"),
                         (P_BXB, "lru_bx_b"), (P_LAM, "lru_lambda_f"), (P_LAM + 4, "lru_lambda_b"),
                         (P_BG, "gla_bg_f"), (P_BG + 2, "gla_bg_b"), (P_GMIX, "norm_mix_pre"),
                         (P_GMIXPOST, "norm_mix_post"), (P_GMLP, "norm_mlp_pre"), (P_GMLPPOST, "norm_mlp_post"),
                         (P_GOUT + 4, "gla_head_norm")):
            put(at, a[name][l])
        params[:, l, P_GOUT:P_GOUT + 4] = 1.0
        params[:, l, P_ONE:P_ONE + 8] = 1.0

    nc = bacc.Bacc("TRN2", target_bir_lowering=False, num_devices=1)
    arrays = {"x_in": x_in, "w_units": w_units, "w_zg": w_zg, "w_gates": w_gates, "w_decay": w_decay, "params": params}
    args = [nc.dram_tensor(n, v.shape, mybir.dt.float32, kind="ExternalInput").ap() for n, v in arrays.items()]
    h_out = nc.dram_tensor("h_out", (L + 1, KT, 128, NP), mybir.dt.float32, kind="ExternalOutput").ap()
    trunk_kernel(nc, *args, h_out)
    r = run_bass_kernel_spmd(nc, [arrays], core_ids=[0])
    h = np.asarray(r.results[0]["h_out"])[L]
    return np.ascontiguousarray(h.reshape(D, NP)[:, N_META:NT].T)[None]
```
